# Optimizing a Trainium2 kernel written in Bass

```python
import math
import jax, jax.numpy as jnp
from jax import lax
import numpy as np

D_MODEL = 2048
BATCH = 1
SEQ = 256
DEPTH = 1

MEM_LEN = 256
XA_HEADS = 4
XA_HEAD_DIM = D_MODEL // XA_HEADS
MIX_WIDTH = D_MODEL
POOL_WIDTH = MIX_WIDTH // 2
POOL_WINDOWS = (2, 4, 8, 16)
POOL_GROUP = POOL_WIDTH // len(POOL_WINDOWS)
DN_HEAD_DIM = 128
DN_WIDTH = MIX_WIDTH - POOL_WIDTH
DN_HEADS = DN_WIDTH // DN_HEAD_DIM
DN_CONV = 4
DN_CHUNK = 64
IN_WIDTH = POOL_WIDTH + 4 * DN_WIDTH + 2 * DN_HEADS
D_FF = 256 * ((8 * D_MODEL // 3 + 255) // 256)
FFN_CONV = 3
EPS = 1e-6


def rms_norm(x, g):
    xf = x.astype(jnp.float32)
    y = xf * lax.rsqrt(jnp.mean(xf * xf, axis=-1, keepdims=True) + EPS)
    return (y * g.astype(jnp.float32)).astype(x.dtype)

def l2_normalize(t):
    return t * lax.rsqrt(jnp.sum(t * t, axis=-1, keepdims=True) + EPS)

def causal_dwconv(x, w, b=None):
    K = w.shape[0]
    S = x.shape[1]
    xp = jnp.pad(x, ((0, 0), (K - 1, 0), (0, 0)))
    y = sum(xp[:, k:k + S] * w[k] for k in range(K))
    if b is not None:
        y = y + b
    return y

def pool_mixer(u, w_pool, pool_scale):
    B, S, _ = u.shape
    uf = u.astype(jnp.float32)
    cs = jnp.pad(jnp.cumsum(uf, axis=1), ((0, 0), (1, 0), (0, 0)))
    pos = jnp.arange(1, S + 1, dtype=jnp.float32)
    groups = []
    for i, w in enumerate(POOL_WINDOWS):
        sl = slice(i * POOL_GROUP, (i + 1) * POOL_GROUP)
        c = cs[:, :, sl]
        lagged = jnp.pad(c, ((0, 0), (w - 1, 0), (0, 0)))[:, :S]
        count = jnp.minimum(pos, float(w))
        mean = (c[:, 1:] - lagged) / count[None, :, None]
        groups.append(mean - uf[:, :, sl])
    mixed = jnp.stack(groups, axis=2).astype(u.dtype)
    y = jnp.einsum('bsng,ngh->bsnh', mixed, w_pool).reshape(B, S, POOL_WIDTH)
    return y * pool_scale

def gated_delta_net(q, k, v, z, b_logit, a_logit, conv_w, a_log, dt_bias, norm_g):
    B, S, _ = q.shape
    H, Dh, C = DN_HEADS, DN_HEAD_DIM, DN_CHUNK
    N = S // C
    f32 = jnp.float32
    qkv = jax.nn.silu(causal_dwconv(jnp.concatenate([q, k, v], axis=-1), conv_w)).astype(f32)
    q, k, v = [t.reshape(B, S, H, Dh) for t in jnp.split(qkv, 3, axis=-1)]
    q = l2_normalize(q) * (Dh ** -0.5)
    k = l2_normalize(k)
    beta = jax.nn.sigmoid(b_logit.astype(f32))
    g = -jnp.exp(a_log.astype(f32)) * jax.nn.softplus(a_logit.astype(f32) + dt_bias.astype(f32))

    def to_chunks(t):
        return t.reshape(B, N, C, H, -1).transpose(0, 3, 1, 2, 4)

    q, k, v = to_chunks(q), to_chunks(k), to_chunks(v)
    beta = to_chunks(beta[..., None])[..., 0]
    gc = jnp.cumsum(to_chunks(g[..., None])[..., 0], axis=-1)
    idx = jnp.arange(C)
    causal = idx[:, None] >= idx[None, :]
    strict = idx[:, None] > idx[None, :]
    decay = jnp.exp(jnp.where(causal, gc[..., :, None] - gc[..., None, :], -jnp.inf))
    kk = jnp.einsum('bhncd,bhnjd->bhncj', k, k)
    l_mat = jnp.where(strict, beta[..., :, None] * kk * decay, 0.0)
    rhs = jnp.concatenate([v * beta[..., None], k * (beta * jnp.exp(gc))[..., None]], axis=-1)
    sol = lax.linalg.triangular_solve(l_mat, rhs, left_side=True, lower=True, unit_diagonal=True)
    u_c, w_c = sol[..., :Dh], sol[..., Dh:]
    attn = jnp.einsum('bhncd,bhnjd->bhncj', q, k) * decay
    q_dec = q * jnp.exp(gc)[..., None]
    k_dec = k * jnp.exp(gc[..., -1:] - gc)[..., None]
    chunk_decay = jnp.exp(gc[..., -1])
    xs = tuple(jnp.moveaxis(t, 2, 0) for t in (u_c, w_c, q_dec, k_dec, attn, chunk_decay))

    def step(state, inp):
        u_i, w_i, qd_i, kd_i, a_i, dec_i = inp
        v_new = u_i - jnp.einsum('bhcd,bhde->bhce', w_i, state)
        o_i = jnp.einsum('bhcd,bhde->bhce', qd_i, state) + jnp.einsum('bhcj,bhje->bhce', a_i, v_new)
        state = state * dec_i[..., None, None] + jnp.einsum('bhcd,bhce->bhde', kd_i, v_new)
        return state, o_i

    _, o = lax.scan(step, jnp.zeros((B, H, Dh, Dh), f32), xs)
    o = o.transpose(1, 0, 3, 2, 4).reshape(B, S, H, Dh)
    o = rms_norm(o, norm_g) * jax.nn.silu(z.astype(f32).reshape(B, S, H, Dh))
    return o.reshape(B, S, DN_WIDTH).astype(z.dtype)

def hybrid_mixer(h, w_in, w_pool, pool_scale, dn_conv_w, dn_a_log, dn_dt_bias, dn_norm_g, w_mix_out):
    p = h @ w_in
    o0 = POOL_WIDTH
    u = p[..., :o0]
    q = p[..., o0:o0 + DN_WIDTH]
    k = p[..., o0 + DN_WIDTH:o0 + 2 * DN_WIDTH]
    v = p[..., o0 + 2 * DN_WIDTH:o0 + 3 * DN_WIDTH]
    z = p[..., o0 + 3 * DN_WIDTH:o0 + 4 * DN_WIDTH]
    o1 = o0 + 4 * DN_WIDTH
    b_logit = p[..., o1:o1 + DN_HEADS]
    a_logit = p[..., o1 + DN_HEADS:o1 + 2 * DN_HEADS]
    y_pool = pool_mixer(u, w_pool, pool_scale)
    y_dn = gated_delta_net(q, k, v, z, b_logit, a_logit, dn_conv_w, dn_a_log, dn_dt_bias, dn_norm_g)
    return jnp.concatenate([y_pool, y_dn], axis=-1) @ w_mix_out

def memory_cross_attention(h, mem_h, w_xq, w_xkv, w_xo):
    B, S, _ = h.shape
    M = mem_h.shape[1]
    q = (h @ w_xq).reshape(B, S, XA_HEADS, XA_HEAD_DIM)
    kv = mem_h @ w_xkv
    k = kv[..., :D_MODEL].reshape(B, M, XA_HEADS, XA_HEAD_DIM)
    v = kv[..., D_MODEL:].reshape(B, M, XA_HEADS, XA_HEAD_DIM)
    s = jnp.einsum('bshd,bmhd->bhsm', q, k).astype(jnp.float32) * (XA_HEAD_DIM ** -0.5)
    pr = jax.nn.softmax(s, axis=-1).astype(v.dtype)
    o = jnp.einsum('bhsm,bmhd->bshd', pr, v).reshape(B, S, D_MODEL)
    return o @ w_xo

def conv_glu_ffn(h, w_gate, w_up, conv_w, conv_b, w_down):
    gate = causal_dwconv(h @ w_gate, conv_w, conv_b)
    return (jax.nn.silu(gate) * (h @ w_up)) @ w_down

def first_inputs(seed: int = 0) -> dict:
    key = jax.random.key(seed)
    ks = jax.random.split(key, 32)
    f32 = jnp.float32

    def nrm(i, shape, scale):
        return jax.random.normal(ks[i], shape, f32) * scale

    def gain(i, shape):
        return 1.0 + 0.02 * jax.random.normal(ks[i], shape, f32)

    dt = jnp.exp(jax.random.uniform(ks[7], (DEPTH, DN_HEADS), f32) * (math.log(0.1) - math.log(0.001)) + math.log(0.001))
    return {
        "x": nrm(0, (BATCH, SEQ, D_MODEL), 1.0),
        "mem": nrm(1, (BATCH, MEM_LEN, D_MODEL), 1.0),
        "mix_norm_g": gain(2, (DEPTH, D_MODEL)),
        "w_in": nrm(3, (DEPTH, D_MODEL, IN_WIDTH), D_MODEL ** -0.5),
        "w_pool": nrm(4, (DEPTH, len(POOL_WINDOWS), POOL_GROUP, POOL_GROUP), POOL_GROUP ** -0.5),
        "pool_scale": gain(5, (DEPTH, POOL_WIDTH)),
        "dn_conv_w": nrm(6, (DEPTH, DN_CONV, 3 * DN_WIDTH), DN_CONV ** -0.5),
        "dn_a_log": jnp.log(jax.random.uniform(ks[8], (DEPTH, DN_HEADS), f32, 1.0, 16.0)),
        "dn_dt_bias": dt + jnp.log(-jnp.expm1(-dt)),
        "dn_norm_g": gain(9, (DEPTH, DN_HEAD_DIM)),
        "w_mix_out": nrm(10, (DEPTH, MIX_WIDTH, D_MODEL), MIX_WIDTH ** -0.5),
        "xa_norm_g": gain(11, (DEPTH, D_MODEL)),
        "mem_norm_g": gain(12, (D_MODEL,)),
        "w_xq": nrm(13, (DEPTH, D_MODEL, D_MODEL), D_MODEL ** -0.5),
        "w_xkv": nrm(14, (DEPTH, D_MODEL, 2 * D_MODEL), D_MODEL ** -0.5),
        "w_xo": nrm(15, (DEPTH, D_MODEL, D_MODEL), D_MODEL ** -0.5),
        "ffn_norm_g": gain(16, (DEPTH, D_MODEL)),
        "w_gate": nrm(17, (DEPTH, D_MODEL, D_FF), D_MODEL ** -0.5),
        "w_up": nrm(18, (DEPTH, D_MODEL, D_FF), D_MODEL ** -0.5),
        "ffn_conv_w": nrm(19, (DEPTH, FFN_CONV, D_FF), FFN_CONV ** -0.5),
        "ffn_conv_b": nrm(20, (DEPTH, D_FF), 0.01),
        "w_down": nrm(21, (DEPTH, D_FF, D_MODEL), D_FF ** -0.5),
        "final_norm_g": gain(22, (D_MODEL,)),
    }

def first_block(x, mem, mix_norm_g, w_in, w_pool, pool_scale, dn_conv_w, dn_a_log, dn_dt_bias, dn_norm_g,
              w_mix_out, xa_norm_g, mem_norm_g, w_xq, w_xkv, w_xo, ffn_norm_g, w_gate, w_up,
              ffn_conv_w, ffn_conv_b, w_down, final_norm_g):
    mem_h = rms_norm(mem, mem_norm_g)
    for l in range(DEPTH):
        x = x + hybrid_mixer(rms_norm(x, mix_norm_g[l]), w_in[l], w_pool[l], pool_scale[l], dn_conv_w[l],
                             dn_a_log[l], dn_dt_bias[l], dn_norm_g[l], w_mix_out[l])
        x = x + memory_cross_attention(rms_norm(x, xa_norm_g[l]), mem_h, w_xq[l], w_xkv[l], w_xo[l])
        x = x + conv_glu_ffn(rms_norm(x, ffn_norm_g[l]), w_gate[l], w_up[l], ffn_conv_w[l], ffn_conv_b[l], w_down[l])
    return rms_norm(x, final_norm_g)


HEAD_DIM = 128
MIX_WIDTH_2 = D_MODEL
NSA_HEADS = MIX_WIDTH_2 // 2 // HEAD_DIM
NSA_KV_GROUPS = 2
NSA_HPG = NSA_HEADS // NSA_KV_GROUPS
MOBA_HEADS = MIX_WIDTH_2 // 2 // HEAD_DIM
CMP_LEN = 32
CMP_STRIDE = 16
CMP_HIDDEN = HEAD_DIM
SEL_LEN = 64
SEL_TOPK = 16
WINDOW = 512
MOBA_BLOCK = 256
MOBA_TOPK = 3
D_FF_2 = 4 * D_MODEL
ROPE_THETA = 10000.0
NSA_Q_CHUNK = 64
MOBA_Q_CHUNK = 16

NSA_Q_W = NSA_HEADS * HEAD_DIM
NSA_KV_W = NSA_KV_GROUPS * HEAD_DIM
NSA_GATE_W = 3 * NSA_HEADS
MOBA_W = MOBA_HEADS * HEAD_DIM
IN_WIDTHS = (NSA_Q_W,) + (NSA_KV_W,) * 6 + (NSA_GATE_W, MOBA_W, MOBA_W, MOBA_W)
IN_COLS = sum(IN_WIDTHS)


def rms_norm_2(x, g):
    x32 = x.astype(jnp.float32)
    y = x32 * lax.rsqrt(jnp.mean(x32 * x32, axis=-1, keepdims=True) + EPS)
    return (y * g.astype(jnp.float32)).astype(x.dtype)

def modulate(h, shift, scale):
    return h * (1.0 + scale[:, None, :]) + shift[:, None, :]

def rope_tables(T):
    pos = jnp.arange(T, dtype=jnp.float32)
    inv = ROPE_THETA ** (-jnp.arange(0, HEAD_DIM, 2, dtype=jnp.float32) / HEAD_DIM)
    ang = pos[:, None] * inv[None, :]
    return jnp.cos(ang), jnp.sin(ang)

def apply_rope(x, cos, sin):
    shp = (x.shape[1],) + (1,) * (x.ndim - 3) + (HEAD_DIM // 2,)
    c_ = cos.reshape(shp)
    s_ = sin.reshape(shp)
    x32 = x.astype(jnp.float32)
    x1, x2 = jnp.split(x32, 2, axis=-1)
    return jnp.concatenate([x1 * c_ - x2 * s_, x2 * c_ + x1 * s_], axis=-1).astype(x.dtype)

def masked_softmax(s, mask):
    s = jnp.where(mask, s.astype(jnp.float32), -jnp.inf)
    m = jnp.max(s, axis=-1, keepdims=True)
    m = jnp.where(jnp.isfinite(m), m, 0.0)
    e = jnp.exp(s - m)
    return e / jnp.maximum(jnp.sum(e, axis=-1, keepdims=True), jnp.float32(1e-30))

def compress(x, pos, w1, w2):
    B, T, G, dh = x.shape
    n_cmp = (T - CMP_LEN) // CMP_STRIDE + 1
    idx = np.arange(n_cmp)[:, None] * CMP_STRIDE + np.arange(CMP_LEN)[None, :]
    blocks = x[:, idx] + pos[:, None, :].astype(x.dtype)
    blocks = blocks.transpose(0, 1, 3, 2, 4).reshape(B, n_cmp, G, CMP_LEN * dh)
    return jax.nn.silu(blocks @ w1) @ w2

def nsa_mixer(q, k_cmp, v_cmp, k_sel, v_sel, k_win, v_win, gate_logits,
              cmp_k_pos, cmp_k_w1, cmp_k_w2, cmp_v_pos, cmp_v_w1, cmp_v_w2, cos, sin):
    B, T, _ = q.shape
    G, Hg, dh = NSA_KV_GROUPS, NSA_HPG, HEAD_DIM
    Qc = NSA_Q_CHUNK
    q = apply_rope(q.reshape(B, T, G, Hg, dh), cos, sin) * (dh ** -0.5)
    kv = lambda a: a.reshape(B, T, G, dh)
    k_cmp = apply_rope(kv(k_cmp), cos, sin)
    k_sel = apply_rope(kv(k_sel), cos, sin)
    k_win = apply_rope(kv(k_win), cos, sin)
    v_cmp, v_sel, v_win = kv(v_cmp), kv(v_sel), kv(v_win)
    gates = jax.nn.sigmoid(gate_logits.astype(jnp.float32)).reshape(B, T, G, Hg, 3)

    kc = compress(k_cmp, cmp_k_pos, cmp_k_w1, cmp_k_w2)
    vc = compress(v_cmp, cmp_v_pos, cmp_v_w1, cmp_v_w2)
    n_cmp = kc.shape[1]
    cmp_start = np.arange(n_cmp) * CMP_STRIDE
    cmp_end_np = cmp_start + CMP_LEN
    cmp_end = jnp.asarray(cmp_end_np - 1)

    n_sel = T // SEL_LEN
    k_top = min(SEL_TOPK, n_sel)
    sel_start = np.arange(n_sel) * SEL_LEN
    overlap = np.clip(np.minimum(cmp_end_np[:, None], sel_start[None, :] + SEL_LEN)
                      - np.maximum(cmp_start[:, None], sel_start[None, :]), 0, None)
    sel_map = jnp.asarray((overlap / CMP_LEN).astype(np.float32))
    ks_blk = k_sel.reshape(B, n_sel, SEL_LEN, G, dh).transpose(0, 3, 1, 2, 4)
    vs_blk = v_sel.reshape(B, n_sel, SEL_LEN, G, dh).transpose(0, 3, 1, 2, 4)
    bi = jnp.arange(B)[:, None, None, None]
    gi = jnp.arange(G)[None, :, None, None]

    pad = ((0, 0), (WINDOW, 0), (0, 0), (0, 0))
    kw_pad = jnp.pad(k_win, pad)
    vw_pad = jnp.pad(v_win, pad)

    def chunk(i):
        s0 = i * Qc
        qc = lax.dynamic_slice_in_dim(q, s0, Qc, axis=1)
        gc = lax.dynamic_slice_in_dim(gates, s0, Qc, axis=1)
        tq = s0 + jnp.arange(Qc)
        sc = jnp.einsum('bqghd,bcgd->bghqc', qc, kc)
        p_c = masked_softmax(sc, cmp_end[None, :] <= tq[:, None])
        o_c = jnp.einsum('bghqc,bcgd->bqghd', p_c.astype(vc.dtype), vc)
        imp = jnp.einsum('bghqc,cs->bgqs', p_c, sel_map)
        cb = tq // SEL_LEN
        blk = jnp.arange(n_sel)[None, :]
        causal = blk <= cb[:, None]
        forced = (blk == 0) | (blk == cb[:, None]) | (blk == cb[:, None] - 1)
        score = jnp.where(causal, jnp.where(forced, jnp.inf, imp), -jnp.inf)
        _, idx = lax.top_k(score, k_top)
        ksg = ks_blk[bi, gi, idx]
        vsg = vs_blk[bi, gi, idx]
        kpos = idx[..., None] * SEL_LEN + jnp.arange(SEL_LEN)
        mask_s = (kpos <= tq[:, None, None]).reshape(B, G, 1, Qc, k_top * SEL_LEN)
        ss = jnp.einsum('bqghd,bgqkld->bghqkl', qc, ksg).reshape(B, G, Hg, Qc, k_top * SEL_LEN)
        p_s = masked_softmax(ss, mask_s)
        o_s = jnp.einsum('bghqn,bgqnd->bqghd', p_s.astype(vsg.dtype),
                         vsg.reshape(B, G, Qc, k_top * SEL_LEN, dh))
        kw = lax.dynamic_slice_in_dim(kw_pad, s0, Qc + WINDOW, axis=1)
        vw = lax.dynamic_slice_in_dim(vw_pad, s0, Qc + WINDOW, axis=1)
        kp = s0 - WINDOW + jnp.arange(Qc + WINDOW)
        dist = tq[:, None] - kp[None, :]
        mask_w = (dist >= 0) & (dist < WINDOW) & (kp[None, :] >= 0)
        sw = jnp.einsum('bqghd,bkgd->bghqk', qc, kw)
        p_w = masked_softmax(sw, mask_w)
        o_w = jnp.einsum('bghqk,bkgd->bqghd', p_w.astype(vw.dtype), vw)
        g = gc.astype(o_c.dtype)
        o = g[..., 0:1] * o_c + g[..., 1:2] * o_s + g[..., 2:3] * o_w
        return o.reshape(B, Qc, NSA_HEADS * dh)

    out = lax.map(chunk, jnp.arange(T // Qc))
    return jnp.moveaxis(out, 0, 1).reshape(B, T, NSA_HEADS * dh)

def moba_mixer(q, k, v, cos, sin):
    B, T, _ = q.shape
    H, dh, BLK, Qc = MOBA_HEADS, HEAD_DIM, MOBA_BLOCK, MOBA_Q_CHUNK
    q = apply_rope(q.reshape(B, T, H, dh), cos, sin) * (dh ** -0.5)
    k = apply_rope(k.reshape(B, T, H, dh), cos, sin)
    v = v.reshape(B, T, H, dh)
    nb = -(-T // BLK)
    pad = ((0, 0), (0, nb * BLK - T), (0, 0), (0, 0))
    k_pad = jnp.pad(k, pad)
    v_pad = jnp.pad(v, pad)
    k_blk = k_pad.reshape(B, nb, BLK, H, dh).transpose(0, 3, 1, 2, 4)
    v_blk = v_pad.reshape(B, nb, BLK, H, dh).transpose(0, 3, 1, 2, 4)
    k_mean = jnp.mean(k_blk.astype(jnp.float32), axis=3).astype(k.dtype)
    k_past = min(MOBA_TOPK, nb - 1)
    bi = jnp.arange(B)[:, None, None, None]
    hi = jnp.arange(H)[None, :, None, None]

    def chunk(i):
        s0 = i * Qc
        qc = lax.dynamic_slice_in_dim(q, s0, Qc, axis=1)
        tq = s0 + jnp.arange(Qc)
        cur = s0 // BLK
        ko = lax.dynamic_slice_in_dim(k_pad, cur * BLK, BLK, axis=1)
        vo = lax.dynamic_slice_in_dim(v_pad, cur * BLK, BLK, axis=1)
        opos = cur * BLK + jnp.arange(BLK)
        s_own = jnp.einsum('bqhd,blhd->bhql', qc, ko)
        m_own = jnp.broadcast_to(opos[None, :] <= tq[:, None], (B, H, Qc, BLK))
        if k_past > 0:
            gsc = jnp.einsum('bqhd,bhnd->bhqn', qc, k_mean).astype(jnp.float32)
            gsc = jnp.where(jnp.arange(nb) < cur, gsc, -jnp.inf)
            _, idx = lax.top_k(gsc, k_past)
            kg = k_blk[bi, hi, idx]
            vg = v_blk[bi, hi, idx]
            s_past = jnp.einsum('bqhd,bhqkld->bhqkl', qc, kg).reshape(B, H, Qc, k_past * BLK)
            m_past = jnp.broadcast_to((idx < cur)[..., None],
                                      (B, H, Qc, k_past, BLK)).reshape(B, H, Qc, k_past * BLK)
            p = masked_softmax(jnp.concatenate([s_past, s_own], axis=-1),
                               jnp.concatenate([m_past, m_own], axis=-1))
            p = p.astype(v.dtype)
            o = (jnp.einsum('bhqn,bhqnd->bqhd', p[..., :k_past * BLK],
                            vg.reshape(B, H, Qc, k_past * BLK, dh))
                 + jnp.einsum('bhql,blhd->bqhd', p[..., k_past * BLK:], vo))
        else:
            p = masked_softmax(s_own, m_own).astype(v.dtype)
            o = jnp.einsum('bhql,blhd->bqhd', p, vo)
        return o.reshape(B, Qc, H * dh)

    out = lax.map(chunk, jnp.arange(T // Qc))
    return jnp.moveaxis(out, 0, 1).reshape(B, T, H * dh)

def second_inputs(seed: int = 0) -> dict:
    key = jax.random.key(seed)
    ks = jax.random.split(key, 18)
    nrm = lambda k, shape, s: jax.random.normal(k, shape, jnp.float32) * s
    L = DEPTH
    return {
        'x': nrm(ks[0], (BATCH, SEQ, D_MODEL), 1.0),
        'c': nrm(ks[1], (BATCH, D_MODEL), 1.0),
        'w_ada': nrm(ks[2], (L, D_MODEL, 6 * D_MODEL), 0.5 * D_MODEL ** -0.5),
        'b_ada': nrm(ks[3], (L, 6 * D_MODEL), 0.01),
        'pre_norm_mix': 1.0 + nrm(ks[4], (L, D_MODEL), 0.05),
        'post_norm_mix': 1.0 + nrm(ks[5], (L, D_MODEL), 0.05),
        'w_in': nrm(ks[6], (L, D_MODEL, IN_COLS), D_MODEL ** -0.5),
        'cmp_k_pos': nrm(ks[7], (L, CMP_LEN, HEAD_DIM), 0.1),
        'cmp_k_w1': nrm(ks[8], (L, CMP_LEN * HEAD_DIM, CMP_HIDDEN), (CMP_LEN * HEAD_DIM) ** -0.5),
        'cmp_k_w2': nrm(ks[9], (L, CMP_HIDDEN, HEAD_DIM), CMP_HIDDEN ** -0.5),
        'cmp_v_pos': nrm(ks[10], (L, CMP_LEN, HEAD_DIM), 0.1),
        'cmp_v_w1': nrm(ks[11], (L, CMP_LEN * HEAD_DIM, CMP_HIDDEN), (CMP_LEN * HEAD_DIM) ** -0.5),
        'cmp_v_w2': nrm(ks[12], (L, CMP_HIDDEN, HEAD_DIM), CMP_HIDDEN ** -0.5),
        'w_o': nrm(ks[13], (L, MIX_WIDTH_2, D_MODEL), MIX_WIDTH_2 ** -0.5),
        'pre_norm_ffn': 1.0 + nrm(ks[14], (L, D_MODEL), 0.05),
        'post_norm_ffn': 1.0 + nrm(ks[15], (L, D_MODEL), 0.05),
        'w_up': nrm(ks[16], (L, D_MODEL, D_FF_2), D_MODEL ** -0.5),
        'w_down': nrm(ks[17], (L, D_FF_2, D_MODEL), D_FF_2 ** -0.5),
    }

def second_block(x, c, w_ada, b_ada, pre_norm_mix, post_norm_mix, w_in,
              cmp_k_pos, cmp_k_w1, cmp_k_w2, cmp_v_pos, cmp_v_w1, cmp_v_w2,
              w_o, pre_norm_ffn, post_norm_ffn, w_up, w_down):
    T = x.shape[1]
    cos, sin = rope_tables(T)
    split_at = np.cumsum(IN_WIDTHS)[:-1].tolist()
    for l in range(DEPTH):
        mod = jax.nn.silu(c) @ w_ada[l] + b_ada[l]
        shift_m, scale_m, gate_m, shift_f, scale_f, gate_f = jnp.split(mod, 6, axis=-1)
        h = modulate(rms_norm_2(x, pre_norm_mix[l]), shift_m, scale_m)
        (q_n, k_c, v_c, k_s, v_s, k_w, v_w, g_n,
         q_m, k_m, v_m) = jnp.split(h @ w_in[l], split_at, axis=-1)
        o_n = nsa_mixer(q_n, k_c, v_c, k_s, v_s, k_w, v_w, g_n,
                        cmp_k_pos[l], cmp_k_w1[l], cmp_k_w2[l],
                        cmp_v_pos[l], cmp_v_w1[l], cmp_v_w2[l], cos, sin)
        o_m = moba_mixer(q_m, k_m, v_m, cos, sin)
        o = jnp.concatenate([o_n, o_m], axis=-1) @ w_o[l]
        x = x + gate_m[:, None, :] * rms_norm_2(o, post_norm_mix[l])
        h = modulate(rms_norm_2(x, pre_norm_ffn[l]), shift_f, scale_f)
        f = jnp.square(jax.nn.relu(h @ w_up[l])) @ w_down[l]
        x = x + gate_f[:, None, :] * rms_norm_2(f, post_norm_ffn[l])
    return x


def setup_inputs(seed=0):
    out = dict(first_inputs(seed))
    for name, value in second_inputs(seed + 1).items():
        if name != "x":
            out[name + "_2"] = value
    return out


def reference(
    x, mem, mix_norm_g, w_in, w_pool, pool_scale, dn_conv_w, dn_a_log, dn_dt_bias, dn_norm_g,
    w_mix_out, xa_norm_g, mem_norm_g, w_xq, w_xkv, w_xo, ffn_norm_g, w_gate, w_up, ffn_conv_w,
    ffn_conv_b, w_down, final_norm_g, c_2, w_ada_2, b_ada_2, pre_norm_mix_2, post_norm_mix_2,
    w_in_2, cmp_k_pos_2, cmp_k_w1_2, cmp_k_w2_2, cmp_v_pos_2, cmp_v_w1_2, cmp_v_w2_2, w_o_2,
    pre_norm_ffn_2, post_norm_ffn_2, w_up_2, w_down_2,
):
    x = first_block(
        x, mem, mix_norm_g, w_in, w_pool, pool_scale, dn_conv_w, dn_a_log, dn_dt_bias,
        dn_norm_g, w_mix_out, xa_norm_g, mem_norm_g, w_xq, w_xkv, w_xo, ffn_norm_g, w_gate,
        w_up, ffn_conv_w, ffn_conv_b, w_down, final_norm_g,
    )
    return second_block(
        x, c_2, w_ada_2, b_ada_2, pre_norm_mix_2, post_norm_mix_2, w_in_2, cmp_k_pos_2,
        cmp_k_w1_2, cmp_k_w2_2, cmp_v_pos_2, cmp_v_w1_2, cmp_v_w2_2, w_o_2, pre_norm_ffn_2,
        post_norm_ffn_2, w_up_2, w_down_2,
    )


_drawn_inputs = setup_inputs


def setup_inputs(seed=0):
    import zlib

    import numpy as np

    out = dict(_drawn_inputs(seed))
    spreads = {}
    factors = {'mix_norm_g': 3.356,
     'pool_scale': 4.976,
     'dn_norm_g': 6.804,
     'xa_norm_g': 8.0,
     'mem_norm_g': 8.0,
     'ffn_norm_g': 4.615,
     'ffn_conv_b': 8.0,
     'final_norm_g': 2.804,
     'b_ada_2': 3.421,
     'pre_norm_mix_2': 3.849,
     'post_norm_mix_2': 11.135,
     'cmp_k_pos_2': 8.0,
     'cmp_v_pos_2': 19.36,
     'pre_norm_ffn_2': 3.583,
     'post_norm_ffn_2': 12.682}
    for name, (base, spread) in spreads.items():
        noise = np.random.default_rng([zlib.crc32(name.encode()), seed]).standard_normal(out[name].shape)
        drawn = base * np.exp(spread * noise) if base else spread * noise
        out[name] = __import__('jax').numpy.asarray(drawn.astype(out[name].dtype))
    for name, factor in factors.items():
        out[name] = (out[name] * factor).astype(out[name].dtype)
    return out
```

```python
import numpy as np
from contextlib import ExitStack, contextmanager

import concourse.bass as bass
from concourse import mybir

F32 = mybir.dt.float32
F32R = mybir.dt.float32r
ALU = mybir.AluOpType
ACT = mybir.ActivationFunctionType
AX = mybir.AxisListType

P = 128
T = 256
NH = T // P
D = 2048
KT = D // P
EPS = 1e-6
NEG = -1e30
POOL_W = 1024
DN_W = 1024
DN_H = 8
IN_W = 5136
XA_H = 4
XA_D = 512
FF1 = 5632
FF2 = 8192
IN2_W = 5656
UK = 4
NSLOT = 4
NRING = 4
LEAD = 2
CREDIT = 8
CMP_N = (T - 32) // 16 + 1


def constant_table():
    parts, at, n = [], {}, 0

    def put(name, a):
        nonlocal n
        a = np.asarray(a, np.float32).reshape(P, -1)
        at[name] = (n, a.shape[1])
        parts.append(a)
        n += a.shape[1]

    i = np.arange(P)
    same = (i[:, None] // 64) == (i[None, :] // 64)
    put("ident", np.eye(P))
    put("ones", np.ones((P, P)))
    put("negones", -np.ones((P, P)))
    put("upto", same & (i[:, None] <= i[None, :]))
    put("after", same & (i[:, None] > i[None, :]))
    put("chunk0", np.repeat((i < 64)[:, None], P, 1))
    put("chunk1", np.repeat((i >= 64)[:, None], P, 1))
    put("chunk_mask", np.where(same & (i[:, None] <= i[None, :]), 0.0, NEG))
    put("strict", same & (i[:, None] < i[None, :]))
    levels = []
    for s in range(6):
        b = 1 << s
        levels.append((i[:, None] // (2 * b) == i[None, :] // (2 * b))
                      & (i[:, None] % (2 * b) < b) & (i[None, :] % (2 * b) >= b))
    put("levels", np.stack(levels, 1))
    put("causal", np.where(i[None, :] <= i[:, None], 0.0, NEG))
    ang = (np.arange(T, dtype=np.float32)[:, None]
           * (np.float32(10000.0) ** (-np.arange(0, P, 2, dtype=np.float32) / P))[None, :])
    put("cos", np.cos(ang).reshape(NH, P, 64).transpose(1, 0, 2))
    put("sin", np.sin(ang).reshape(NH, P, 64).transpose(1, 0, 2))
    t = np.arange(T)
    ok = (np.arange(CMP_N) * 16 + 31)[None, :] <= t[:, None]
    put("cmp_mask", np.where(ok, 0.0, NEG).reshape(NH, P, CMP_N).transpose(1, 0, 2))
    put("cmp_valid", ok.any(1).reshape(NH, P).T)
    return np.concatenate(parts, 1), at


def pooling_table():
    t = np.arange(T)
    m = []
    for w in (2, 4, 8, 16):
        b = ((t[:, None] <= t[None, :]) & (t[:, None] > t[None, :] - w)).astype(np.float32)
        b = b / np.minimum(t + 1, w)[None, :].astype(np.float32) - np.eye(T, dtype=np.float32)
        m.append(b.reshape(NH, P, T).transpose(1, 0, 2))
    return np.ascontiguousarray(np.stack(m, 1).reshape(P, -1))


CONST, CAT = constant_table()


class Phase:

    def __init__(self, name, n, nb, units, width, ada=False):
        self.name, self.n, self.nb, self.units, self.width, self.ada = name, n, nb, units, width, ada
        self.seq = []
        g = [("g", b, u) for b in range(nb) for u in range(units)]
        for i, x in enumerate(g):
            self.seq.append(x)
            if ada and i % 2 == 1:
                self.seq.append(("a", 0, i // 2))
        assert len(self.seq) % NSLOT == 0 and (2 * len(g)) % NRING == 0


def plan():
    ph = [Phase("w_in", 6, 2, 4, 428, True), Phase("mix_out", 2, 2, 4, 512, True),
          Phase("xkv", 4, 2, 4, 512, True), Phase("xq", 2, 2, 4, 512, True),
          Phase("xo", 2, 2, 4, 512, True),
          Phase("ffn1a", 6, 2, 4, 512), Phase("down1a", 2, 2, 6, 512),
          Phase("ffn1b", 5, 2, 4, 512), Phase("down1b", 1, 4, 5, 512),
          Phase("w_in2", 6, 2, 4, 472, True), Phase("w_o", 2, 2, 4, 512, True)]
    for s in range(4):
        ph += [Phase(f"up2{s}", 2, 2, 4, 512), Phase(f"down2{s}", 2, 2, 4, 512)]
    units = subs = evs = adas = 0
    for q in ph:
        q.unit0, q.sub0, q.ev0, q.ada0 = units, subs, evs, adas
        q.subs = 2 * q.nb * q.units
        units += q.n * len(q.seq)
        subs += q.n * q.subs
        evs += q.n * q.nb // 2
        adas += q.n * q.ada
        q.sub1, q.ev1, q.ada1 = subs, evs, adas
    assert adas == 24
    return {q.name: q for q in ph}


def program(nc, A, out):
    PH = plan()
    order = list(PH.values())
    with ExitStack() as ctx:
        sems = {}

        def S(name):
            if name not in sems:
                sems[name] = ctx.enter_context(nc.semaphore(name))
            return sems[name]

        def fixed(name, shape, dt=F32):
            return ctx.enter_context(nc.sbuf_tensor(name, shape, dt))

        raw = [fixed(f"raw{i}", [P, UK, 512]) for i in range(NSLOT)]
        whi = [fixed(f"whi{i}", [P, 2, 512], F32R) for i in range(NRING)]
        wlo = [fixed(f"wlo{i}", [P, 2, 512], F32R) for i in range(NRING)]
        x = fixed("x", [P, NH, D])
        hhi = fixed("hhi", [P, KT, T], F32R)
        hlo = fixed("hlo", [P, KT, T], F32R)
        cst = fixed("cst", [P, CONST.shape[1]])
        gains = fixed("gains", [P, 6, KT])
        shifts = fixed("shifts", [P, 2, KT])
        conv_w = fixed("conv_w", [P, 24, 4])
        ffn_w = fixed("ffn_w", [P, FF1 // P * 4])
        pool_s = fixed("pool_s", [P, 8])
        mod = fixed("mod", [P, 96])
        b_ada = fixed("b_ada", [P, 96])
        cvec = fixed("cvec", [P, KT])
        csig = fixed("csig", [P, KT])
        ada_acc = fixed("ada_acc", [P, 512])
        small = fixed("small", [P, 320])
        ngb = fixed("ngb", [P, P])
        flat = fixed("flat", [P, 1024])
        fbx = [flat[:, 512 * i:512 * i + 512] for i in range(2)]
        kTc = flat[:, 0:512].rearrange("p (a b) -> p a b", b=T)
        kcT = flat[:, 512:512 + 2 * CMP_N].rearrange("p (a b) -> p a b", b=CMP_N)
        vc = flat[0:CMP_N, 640:896].rearrange("p (a b) -> p a b", b=P)
        arena0 = ((nc.sbuf_base + 31) // 32) * 32
        arena_end = nc.sbuf_usable_end
        names = iter(range(10 ** 6))

        class Arena:
            def __init__(self):
                self.at = arena0

            def __call__(self, name, shape, dt=F32):
                t = nc.alloc_sbuf_tensor_at(f"{name}_{next(names)}", shape, dt, offset=self.at)
                self.at += (int(np.prod(shape[1:])) * 4 + 31) // 32 * 32
                assert self.at <= arena_end, (name, self.at, arena_end)
                return t

        GP = ctx.enter_context(nc.psum_tensor("GP", [P, 4, 512], F32))
        TA = ctx.enter_context(nc.psum_tensor("TA", [P, 1024], F32))
        TB = ctx.enter_context(nc.psum_tensor("TB", [P, 1024], F32))

        def C(name, lo=0, n=None):
            a, w = CAT[name]
            return cst[:, a + lo:a + (w if n is None else lo + n)]

        STAGES, grown = {}, dict.fromkeys(("ss", "ms", "rt", "xn", "t", "f", "hi", "lo"), 0)
        for n in ("mix", "mem", "xa", "ffn", "fin", "pre2", "pf2"):
            STAGES[n] = ("norm", dict(grown))
            for k, m in (("ss", 2), ("ms", 1), ("rt", 1)) + (n != "fin") * (("xn", 2), ("t", 8), ("f", 8), ("hi", 8), ("lo", 8)):
                grown[k] += m
        STAGES |= {n: ("att", {k: (i if k == "go" else g if k in ("o", "hi", "lo") else u)
                               for k in ("go", "qk", "m", "e", "n", "t", "c", "o", "hi", "lo")})
                   for i, (n, u, g) in enumerate((("xatt", 0, 0), ("natt", 2, 8), ("matt", 14, 12)))}
        STAGES |= {n: ("turn", {"t": i, "c": i}) for n, i in (("kx", 0), ("qx", 4), ("n2", 8), ("m2", 11))}

        def N(stage, what, count=0):
            kind, before = STAGES[stage]
            return S(f"{kind}_{what}"), before[what] + count

        ident = C("ident")

        def rows(ap, n):
            return ap.unsqueeze(1).broadcast_to([ap.shape[0], n, ap.shape[1]])

        def cols(ap, n):
            return ap.unsqueeze(2).broadcast_to([ap.shape[0], ap.shape[1], n])

        def v(ps, b):
            return ps[:, :].rearrange("p (a b) -> p a b", b=b)

        _s = [0]

        def sm(n):
            a = _s[0]
            _s[0] += n
            assert _s[0] <= 320
            return small[:, a:a + n]

        ss = sm(2); ms = sm(2); rt = sm(2); rstd = sm(2)
        beta = sm(16); gdec = sm(16); za = sm(16); zb = sm(16); zc = sm(16); zd = sm(16); ze = sm(16)
        dtb = sm(8); ea = sm(8); ex = sm(32); s16 = sm(16); m16 = sm(16); r16 = sm(16); i16 = sm(16)
        gates = sm(48)
        mx = [sm(4), sm(4)]; nm = [sm(4), sm(4)]; sme = [sm(4), sm(4)]; rc = [sm(4), sm(4)]

        ar = Arena()
        p1 = ar("p1", [P, NH, IN_W])
        norm_at = ar.at
        tmp = [ar(f"t{i}", [P, 8, P]) for i in range(9)]
        tmp += [flat[:, :].rearrange("p (a b) -> p a b", b=P)]
        tmp += [p1[:, h, 0:1024].rearrange("p (a b) -> p a b", b=P) for h in range(2)]
        (KB, KBT, KTt, QT, DT, LT, MT, TT, AA, YY) = tmp[:10]
        ST, SQ = tmp[10], tmp[11]
        ar = Arena(); ar.at = norm_at
        pmat = ar("pmat", [P, 4, NH, T]); wpool = ar("wpool", [P, 4, 2, T])
        mixT = ar("mixT", [P, 2, T]); fpool = ar("fpool", [P, 2, T])
        ar = Arena(); ar.at = norm_at
        cbuf = [ar(f"cbuf{i}", [P, 4, T]) for i in range(2)]; csg = ar("csg", [P, 4, T])
        ar = Arena()
        xn = ar("xn", [P, NH, D])
        memt = ar("memt", [P, NH, D])
        ar = Arena()
        kv = ar("kv", [P, NH, 2 * D]); kTx = ar("kTx", [P, KT, T]); qTx = ar("qTx", [P, KT, T])
        xq = kv[:, :, 0:D]
        xpr = [kv[:, 0, 1024 * i:1024 * i + 1024].rearrange("p (a b) -> p a b", b=T) for i in range(2)]
        xpT = [kv[:, 1, 1024 * i:1024 * i + 1024].rearrange("p (a b c) -> p a b c", b=4, c=P) for i in range(2)]
        ar = Arena()
        fhi = ar("fhi", [P, 24, T], F32R); flo = ar("flo", [P, 24, T], F32R)
        tok = [ar(f"tok{i}", [P, NH, 512]) for i in range(2)]
        ft = ar("ft", [P, 4, T]); fsg = ar("fsg", [P, 4, T])
        ar = Arena()
        xn_f = ar("xn_f", [P, NH, D]); fgb = ar("fgb", [P, D])
        ar = Arena()
        p2 = ar("p2", [P, NH, IN2_W])
        qT2 = ar("qT2", [P, 8, T]); kT2 = ar("kT2", [P, 8, T])
        scr2 = ar.at
        pr2 = [p2[:, i, 0:1024].rearrange("p (a b) -> p a b", b=T) for i in range(2)]
        pT2 = [ar(f"pT2{i}", [P, 2, 4, P]) for i in range(3)]
        posT = ar("posT", [P, 2, 32]); w2c = ar("w2c", [P, 2, P]); hid = ar("hid", [P, 62])
        ar = Arena(); ar.at = scr2
        rc1 = ar("rc1", [P, 32, 31])
        ar = Arena(); ar.at = scr2 - 16384
        w1c = ar("w1c", [P, 32, P])
        ar = Arena(); ar.at = scr2 - 16384
        rp = [ar(f"rp{i}", [P, 8, 64]) for i in range(4)]
        ar = Arena()
        o2 = ar("o2", [P, NH, D]); gpb = ar("gpb", [P, D]); pnb = ar("pnb", [P, D])
        dg = ar("dg", [P, 4, P]); junk = ar("junk", [P, D])
        ar = Arena()
        o3 = ar("o3", [P, NH, D])
        f2hi = ar("f2hi", [P, 16, T], F32R); f2lo = ar("f2lo", [P, 16, T], F32R)
        tok2 = [ar(f"tok2{i}", [P, NH, 512]) for i in range(2)]; fq2 = [ar(f"fq2{i}", [P, 4, T]) for i in range(2)]

        block = ctx.enter_context(nc.Block())

        @contextmanager
        def loop(eng, n):
            if n == 1:
                yield 0
            else:
                with eng.Fori(0, n) as i:
                    yield i

        class Chain:

            def __init__(self, eng, sem):
                self.eng, self.sem, self.n, self.reg, self.per = eng, sem, 0, 0, 0

            def __call__(self, ins):
                self.n += 1
                ins.then_inc(self.sem, 1)
                self.eng.wait_ge(self.sem, self.reg * self.per + self.n if self.per else self.n)

            @contextmanager
            def loop(self, i, n, per):
                start = self.n
                self.reg, self.per = i, per if n > 1 else 0
                yield
                assert self.n - start == per, (self.n - start, per)
                self.n, self.reg, self.per = start + n * per, 0, 0

        def block_end(q, it, b):
            return q.sub0 + it * q.subs + (b + 1) * 2 * q.units

        def cross_units():
            us = []
            for hf in range(NH):
                us.append(dict(hf=hf, L=T, mask=None, scale=XA_D ** -0.5,
                               qk=[[(qTx[:, 4 * h + d, hf * P:hf * P + P], kTx[:, 4 * h + d, :]) for d in range(4)] for h in range(4)],
                               pr=xpr[hf], pT=xpT[hf], coef=None,
                               groups=[dict(kt0=4 * h, hf=hf,
                                            pv=[[(kv[:, m, D + h * XA_D + d * P:D + h * XA_D + d * P + P], xpT[hf][:, m, h, :]) for m in range(2)]
                                                for d in range(4)]) for h in range(4)]))
            return us

        KV0 = 1024

        def nsa_units():
            us = []
            n = 0
            for hf in range(NH):
                for g in range(2):
                    hs = range(4 * g, 4 * g + 4)
                    pts = [pT2[(n + i) % 3] for i in range(3)]
                    nk = hf + 1
                    for br in range(3):
                        q = lambda h: qT2[:, h, hf * P:hf * P + P]
                        if br == 0:
                            us.append(dict(hf=hf, L=CMP_N, mask="cmp", scale=P ** -0.5, qk=[[(q(h), kcT[:, g, :])] for h in hs],
                                           pr=pr2[n % 2], pT=pts[0], coef=(g, 0), groups=[]))
                        else:
                            kk = kT2[:, 2 * (br - 1) + g, 0:nk * P]
                            us.append(dict(hf=hf, L=nk * P, mask="causal", scale=P ** -0.5, qk=[[(q(h), kk)] for h in hs],
                                           pr=pr2[n % 2], pT=pts[br], coef=(g, br), groups=[]))
                        n += 1
                    pv = []
                    for i, h in enumerate(hs):
                        one = [(vc[:, g, :], pts[0][0:CMP_N, 0, i, :])]
                        for br in (1, 2):
                            c = KV0 + 512 * br + 256 + P * g
                            one += [(p2[:, m, c:c + P], pts[br][:, m, i, :]) for m in range(nk)]
                        pv.append(one)
                    us[-1]["groups"] = [dict(kt0=4 * g, hf=hf, pv=pv)]
            return us

        QM0 = 2584

        def moba_units():
            us = []
            n = 0
            for hf in range(NH):
                for g in range(2):
                    hs = range(4 * g, 4 * g + 4)
                    nk = hf + 1
                    pt = pT2[n % 3]
                    us.append(dict(hf=hf, L=nk * P, mask="causal", scale=P ** -0.5,
                                   qk=[[(qT2[:, h, hf * P:hf * P + P], kT2[:, h, 0:nk * P])] for h in hs],
                                   pr=pr2[n % 2], pT=pt, coef=None,
                                   groups=[dict(kt0=8 + 4 * g, hf=hf,
                                                pv=[[(p2[:, m, QM0 + 2048 + h * P:QM0 + 2048 + h * P + P], pt[:, m, i, :]) for m in range(nk)]
                                                    for i, h in enumerate(hs)])]))
                    n += 1
            return us

        def group_of(us, i):
            n = 0
            for j, u in enumerate(us):
                n += len(u["groups"])
                if j >= i and u["groups"]:
                    return n
            return n

        def attention_pe(pe, turn, nm_, us):
            pe.wait_ge(*N(nm_, "go", 1))
            ngroup = 0

            def scores(i):
                u = us[i]
                if i >= 2:
                    pe.wait_ge(*N(nm_, "m", i - 1))
                o = GP[:, 2 * (i % 2):2 * (i % 2) + 2, :].rearrange("p a b -> p (a b)")
                for h in range(4):
                    n = len(u["qk"][h])
                    for d, (l, r) in enumerate(u["qk"][h]):
                        m = pe.matmul(o[:, h * T:h * T + u["L"]], l, r, start=(d == 0), stop=(d == n - 1),
                                      skip_group_check=True)
                m.then_inc(N(nm_, "qk")[0], 1)

            scores(0)
            for i, u in enumerate(us):
                if i + 1 < len(us):
                    scores(i + 1)
                pe.wait_ge(*N(nm_, "n", i + 1))
                if i:
                    pe.wait_ge(*N(nm_, "c", i))
                for kb in range((u["L"] + P - 1) // P):
                    w = min(P, u["L"])
                    for h in range(4):
                        m = turn(TA[0:w, kb * 512 + h * P:kb * 512 + h * P + P], u["pr"][:, h, kb * P:kb * P + w])
                m.then_inc(N(nm_, "t")[0], 1)
                for gr in u["groups"]:
                    pe.wait_ge(*N(nm_, "c", i + 1))
                    if ngroup >= 2:
                        pe.wait_ge(*N(nm_, "lo", ngroup - 1))
                    bank = TB[:, 512 * (ngroup % 2):512 * (ngroup % 2) + 512]
                    for j, terms in enumerate(gr["pv"]):
                        for d, (l, r) in enumerate(terms):
                            m = pe.matmul(bank[:, j * P:j * P + P], l, r, start=(d == 0), stop=(d == len(terms) - 1),
                                          skip_group_check=True)
                    m.then_inc(N(nm_, "o")[0], 1)
                    ngroup += 1

        def attention_act(act, nm_, us):
            ng = 0

            def exps(i):
                u = us[i]
                act.wait_ge(*N(nm_, "m", i + 1))
                for h in range(4):
                    a = u["pr"][:, h, 0:u["L"]]
                    m = nc.scalar.activation(a, a, ACT.Exp, bias=nm[i % 2][:, h:h + 1], scale=u["scale"],
                                             accum_out=sme[i % 2][:, h:h + 1])
                m.then_inc(N(nm_, "e")[0], 1)

            exps(0)
            for i, u in enumerate(us):
                if i + 1 < len(us):
                    exps(i + 1)
                act.wait_ge(*N(nm_, "t", i + 1))
                if i >= 3:
                    act.wait_ge(*N(nm_, "o", group_of(us, i - 3)))
                w = min(P, u["L"])
                for kb in range((u["L"] + P - 1) // P):
                    m = nc.scalar.copy(u["pT"][0:w, kb, :, :], v(TA, P)[0:w, 4 * kb:4 * kb + 4, :])
                m.then_inc(N(nm_, "c")[0], 1)
                for gr in u["groups"]:
                    act.wait_ge(*N(nm_, "o", ng + 1))
                    t = slice(gr["hf"] * P, gr["hf"] * P + P)
                    nc.scalar.copy(hhi[:, gr["kt0"]:gr["kt0"] + 4, t], v(TB, P)[:, 4 * (ng % 2):4 * (ng % 2) + 4, :])\
                        .then_inc(N(nm_, "hi")[0], 1)
                    ng += 1

        def attention_dve(dve, link, nm_, us):
            ng = 0

            def mask_max(i):
                u = us[i]
                L, hf = u["L"], u["hf"]
                dve.wait_ge(*N(nm_, "qk", i + 1))
                ps = v(GP_flat(i % 2), T)[:, :, 0:L] if L != T else v(GP_flat(i % 2), T)
                pr = u["pr"]
                if i >= 2:
                    dve.wait_ge(*N(nm_, "t", i - 1))
                if u["mask"] is None:
                    link(nc.vector.tensor_copy(pr[:, :, 0:L], ps))
                elif u["mask"] == "cmp":
                    link(nc.vector.tensor_tensor(pr[:, :, 0:L], ps, rows(C("cmp_mask", hf * CMP_N, CMP_N), 4), ALU.add))
                else:
                    if L > P:
                        nc.vector.tensor_copy(pr[:, :, 0:P], ps[:, :, 0:P])
                    link(nc.vector.tensor_tensor(pr[:, :, L - P:L], ps[:, :, L - P:L], rows(C("causal"), 4), ALU.add))
                link(nc.vector.tensor_reduce(mx[i % 2], pr[:, :, 0:L], AX.X, ALU.max))
                nc.vector.tensor_scalar(nm[i % 2], mx[i % 2], -u["scale"], None, ALU.mult).then_inc(N(nm_, "m")[0], 1)

            def normalise(i):
                u = us[i]
                L = u["L"]
                dve.wait_ge(*N(nm_, "e", i + 1))
                r = rc[i % 2]
                link(nc.vector.tensor_scalar(sme[i % 2], sme[i % 2], 1e-30, None, ALU.max))
                link(nc.vector.reciprocal(r, sme[i % 2]))
                if u["coef"] is not None:
                    g, br = u["coef"]
                    gt = gates[:, u["hf"] * 24:u["hf"] * 24 + 24].rearrange("p (h b) -> p h b", b=3)[:, 4 * g:4 * g + 4, br]
                    link(nc.vector.tensor_tensor(r, r, gt, ALU.mult))
                    if br == 0:
                        link(nc.vector.tensor_scalar(r, r, C("cmp_valid", u["hf"], 1), None, ALU.mult))
                nc.vector.tensor_tensor(u["pr"][:, :, 0:L], u["pr"][:, :, 0:L], cols(r, L), ALU.mult).then_inc(N(nm_, "n")[0], 1)

            mask_max(0)
            for i, u in enumerate(us):
                if i + 1 < len(us):
                    mask_max(i + 1)
                normalise(i)
                for gr in u["groups"]:
                    dve.wait_ge(*N(nm_, "hi", ng + 1))
                    t = slice(gr["hf"] * P, gr["hf"] * P + P)
                    a = slice(gr["kt0"], gr["kt0"] + 4)
                    nc.vector.tensor_tensor(hlo[:, a, t], v(TB, P)[:, 4 * (ng % 2):4 * (ng % 2) + 4, :],
                                            hhi[:, a, t].bitcast(F32), ALU.subtract).then_inc(N(nm_, "lo")[0], 1)
                    ng += 1

        def GP_flat(e):
            class _F:
                def __getitem__(self, k):
                    return GP[:, 2 * e:2 * e + 2, :].rearrange("p a b -> p (a b)")
            return _F()

        def turn_in(pe, turn, nm_, src, c0, _):
            for g in range(4):
                tp = (TA, TB)[g % 2]
                if g >= 2:
                    pe.wait_ge(*N(nm_, "c", g - 1))
                for f in range(4):
                    for h in range(NH):
                        c = c0 + (4 * g + f) * P
                        m = turn(tp[:, f * T + h * P:f * T + h * P + P], src[:, h, c:c + P])
                m.then_inc(N(nm_, "t")[0], 1)

        def turn_in_act(act, nm_, dst):
            for g in range(4):
                act.wait_ge(*N(nm_, "t", g + 1))
                nc.scalar.copy(dst[:, 4 * g:4 * g + 4, :], v((TA, TB)[g % 2], T)).then_inc(N(nm_, "c")[0], 1)

        def columns2(nm_):
            if nm_ == "n2":
                return [(qT2, 0, [0, 128, 256, 384]), (qT2, 4, [512, 640, 768, 896]),
                        (kT2, 0, [KV0 + 512, KV0 + 640, KV0 + 1024, KV0 + 1152])]
            return [(qT2, 0, [QM0 + P * i for i in range(4)]), (qT2, 4, [QM0 + P * i for i in range(4, 8)]),
                    (kT2, 0, [QM0 + 1024 + P * i for i in range(4)]), (kT2, 4, [QM0 + 1024 + P * i for i in range(4, 8)])]

        def turn_in2(pe, turn, nm_):
            for g, (_, _, cs) in enumerate(columns2(nm_)):
                tp = (TA, TB)[g % 2]
                if g >= 2:
                    pe.wait_ge(*N(nm_, "c", g - 1))
                elif nm_ == "m2":
                    pe.wait_ge(*N("natt", "lo", 4))
                    pe.wait_ge(*N("natt", "c", 12))
                for f, c in enumerate(cs):
                    for h in range(NH):
                        m = turn(tp[:, f * T + h * P:f * T + h * P + P], p2[:, h, c:c + P])
                m.then_inc(N(nm_, "t")[0], 1)

        def turn_in2_act(act, nm_):
            for g, (dst, a, _) in enumerate(columns2(nm_)):
                act.wait_ge(*N(nm_, "t", g + 1))
                m = nc.scalar.copy(dst[:, a:a + 4, :], v((TA, TB)[g % 2], T)).then_inc(N(nm_, "c")[0], 1)

        xn_of = {"mix": xn, "mem": xn, "xa": None, "ffn": xn, "pre2": xn_f, "pf2": None}
        ar = Arena(); ar.at = arena0 + 4 * NH * 2 * D
        ar.at += 4 * KT * T
        xn_of["xa"] = ar("xn_xa", [P, NH, D])
        ar = Arena(); ar.at = arena0 + 4 * NH * D
        xn_of["pf2"] = ar("xn_pf2", [P, NH, D])

        def wsrc(w, col, width, k0=0, u=0):
            return w.rearrange("(u k p) n -> p u k n", k=UK, p=P)[:, k0 + u, :, bass.ds(col, width)]

        def unit_source(q, it, b, u):
            n = q.name
            if n == "w_in":
                return wsrc(A["w_in"], (2 * it + b) * 428, 428, 0, u)
            if n == "w_in2":
                return wsrc(A["w_in_2"], (2 * it + b) * 472, 472, 0, u)
            if n in ("mix_out", "xkv", "xq", "xo", "w_o"):
                w = A[{"mix_out": "w_mix_out", "xkv": "w_xkv", "xq": "w_xq", "xo": "w_xo", "w_o": "w_o_2"}[n]]
                return wsrc(w, (2 * it + b) * 512, 512, 0, u)
            if n in ("ffn1a", "ffn1b"):
                return wsrc(A["w_gate" if b == 0 else "w_up"], (it + (6 if n == "ffn1b" else 0)) * 512, 512, 0, u)
            if n in ("down1a", "down1b"):
                return wsrc(A["w_down"], (q.nb * it + b) * 512, 512, 6 if n == "down1b" else 0, u)
            if n.startswith("up2"):
                return wsrc(A["w_up_2"], (2 * it + b) * 512 + 2048 * int(n[3:]), 512, 0, u)
            return wsrc(A["w_down_2"], (2 * it + b) * 512, 512, 4 * int(n[5:]), u)

        @block.sync
        def _(sp):
            def iteration(q, it, last_cols=False):
                for j, (kind, b, u) in enumerate(q.seq):
                    sp.wait_ge(S("unit_used"), (it * len(q.seq) + (q.unit0 + j - NSLOT + 1)) * 2 + CREDIT)
                    if kind == "a":
                        src = wsrc(A["w_ada_2"], (it + q.ada0) * 512, 512, 0, u)
                        dst = raw[j % NSLOT][:, :, :]
                    elif last_cols and b == 1:
                        src = wsrc(A["w_in_2"], IN2_W - 472, 472, 0, u)
                        dst = raw[j % NSLOT][:, :, 0:472]
                    else:
                        src = unit_source(q, it, b, u)
                        dst = raw[j % NSLOT][:, :, 0:q.width]
                    sp.dma_start(dst, src).then_inc(S(f"raw_in{j % NSLOT}"), 16)

            for q in order:
                n = q.n - 1 if q.name == "w_in2" else q.n
                with loop(sp, n) as it:
                    iteration(q, it)
                if q.name == "w_in2":
                    iteration(q, n, True)

        @block.gpsimd
        def _(g):
            g.dma_start(cst[:, :], A["const"]).then_inc(S("cst_in"), 16)
            g.dma_start(x[:, :, :], A["x"].rearrange("b (h p) d -> p (b h) d", p=P)).then_inc(S("x_in"), 16)
            loads = [(gains[:, 0, :], "mix_norm_g"), (gains[:, 1, :], "xa_norm_g"), (gains[:, 2, :], "mem_norm_g"),
                     (gains[:, 3, :], "ffn_norm_g"), (gains[:, 4, :], "pre_norm_mix_2"), (gains[:, 5, :], "pre_norm_ffn_2"),
                     (conv_w[:, :, :], "dn_conv_w"), (pool_s[:, :], "pool_scale"), (b_ada[:, :], "b_ada_2"),
                     (cvec[:, :], "c_2"),
                     (ffn_w[:, :].rearrange("p (c j) -> p c j", j=4)[:, :, 3:4], "ffn_conv_b")]
            with nc.allow_non_contiguous_dma(reason="per-channel constants"):
                for dst, name in loads:
                    g.dma_start(dst, A[name]).then_inc(S("tab_in"), 16)
                for j in range(3):
                    g.dma_start(ffn_w[:, :].rearrange("p (c j) -> p c j", j=4)[:, :, j:j + 1],
                                A["ffn_conv_w"][:, j, :, :]).then_inc(S("tab_in"), 16)
                g.dma_start(dtb, A["dn_dt_bias"].partition_broadcast(P)).then_inc(S("tab_in"), 16)
                g.dma_start(ea, A["dn_a_log"].partition_broadcast(P)).then_inc(S("tab_in"), 16)
                g.dma_start(ngb[:, :], A["dn_norm_g"].partition_broadcast(P)).then_inc(S("tab_in"), 16)
            g.wait_ge(*N("mix", "lo", 8))
            g.dma_start(pmat[:, :, :, :].rearrange("p a b c -> p (a b c)"), A["pool_mats"]).then_inc(S("pool_in"), 16)
            g.dma_start(wpool[:, :, :, :], A["w_pool"]).then_inc(S("pool_in"), 16)
            g.wait_ge(S("dn_lo"), 2)
            g.dma_start(memt[:, :, :], A["mem"].rearrange("b (h p) d -> p (b h) d", p=P)).then_inc(S("mem_in"), 16)
            for e in range(2):
                g.wait_ge(S(f"evac{e}"), 1 + PH["down1b"].ev1)
            g.wait_ge(S("f1_lo"), 12)
            g.dma_start(fgb[:, :], A["final_norm_g"].partition_broadcast(P)).then_inc(S("fgb_in"), 16)
            for j, w in enumerate(("cmp_k_w1_2", "cmp_v_w1_2")):
                if j == 0:
                    g.wait_ge(*N("pre2", "lo", 8))
                    g.wait_ge(S("rope_done"), 1)
                    for dst, name in ((posT[:, 0, :], "cmp_k_pos_2"), (posT[:, 1, :], "cmp_v_pos_2"),
                                      (w2c[:, 0, :], "cmp_k_w2_2"), (w2c[:, 1, :], "cmp_v_w2_2")):
                        g.dma_start(dst, A[name]).then_inc(S("cmp_in"), 16)
                else:
                    g.wait_ge(S("cmp_hid"), 1)
                g.dma_start(w1c[:, :, :], A[w]).then_inc(S("w1_in"), 16)
            g.wait_ge(S("o_lo"), 1)
            g.dma_start(pnb[:, :], A["post_norm_mix_2"].partition_broadcast(P)).then_inc(S("pn_in"), 16)
            g.wait_ge(S("f2_lo"), 18)
            for e in range(2):
                g.wait_ge(S(f"evac{e}"), 1 + PH["down23"].ev1)
            g.dma_start(pnb[:, :], A["post_norm_ffn_2"].partition_broadcast(P)).then_inc(S("pn_in"), 16)
            for h in range(NH):
                g.wait_ge(S("y_done"), h + 1)
                g.dma_start(out[0, h * P:(h + 1) * P, :], x[:, h, :]).then_inc(S("out_done"), 16)
            g.wait_ge(S("out_done"), 32)

        @block.tensor
        def _(pe):
            def turn(dst, src, n=P):
                return pe.transpose(dst, src, ident[0:n, 0:n] if n != P else ident)

            def product(q, ahi, alo, ready, mid=None, end=None):
                with loop(pe, q.n) as it:
                    for b in range(q.nb):
                        pe.wait_ge(S(f"evac{b % 2}"), it * (q.nb // 2) + (q.ev0 + b // 2 + 1))
                        for u in range(q.units):
                            if b == 0:
                                pe.wait_ge(*ready(u))
                            for s in range(2):
                                pos = [i for i, z in enumerate(q.seq) if z == ("g", b, u)][0]
                                pe.wait_ge(S("unit_used"), it * (2 * len(q.seq)) + 2 * (q.unit0 + pos) + s + 1 + CREDIT)
                                r = ((b * q.units + u) * 2 + s) % NRING
                                for k in range(2):
                                    kt = u * UK + 2 * s + k
                                    first, last = kt == 0, kt == q.units * UK - 1
                                    for h in range(NH):
                                        t = slice(h * P, h * P + P)
                                        o = GP[:, 2 * (b % 2) + h, 0:q.width]
                                        pe.matmul(o, ahi[:, kt, t], whi[r][:, k, 0:q.width], start=first, stop=False)
                                        pe.matmul(o, ahi[:, kt, t], wlo[r][:, k, 0:q.width], start=False, stop=False)
                                        m = pe.matmul(o, alo[:, kt, t], whi[r][:, k, 0:q.width], start=False, stop=last)
                                m.then_inc(S("mm_done"), 1)
                            if mid and b % 2 == 1 and u == 1:
                                mid(it)
                    if q.ada:
                        pe.wait_ge(S("unit_used"), it * (2 * len(q.seq)) + 2 * (q.unit0 + len(q.seq)) + CREDIT)
                        pe.wait_ge(S("ada_read"), it + (q.ada0 + 1))
                        for j in range(4):
                            m = pe.matmul(TB[:, 512 + j:513 + j], ada_acc[:, j * P:(j + 1) * P], C("ones", 0, 1),
                                          start=True, stop=True)
                        m.then_inc(S("ada_sum"), 1)
                    if end:
                        end(it)

            def norm(nm_):
                for q in range(4):
                    for h in range(NH):
                        g = q * NH + h
                        pe.wait_ge(*N(nm_, "xn", h + 1))
                        if g >= 3:
                            pe.wait_ge(*N(nm_, "f", g - 2))
                        bank = (TA[:, 0:512], TA[:, 512:1024], TB[:, 0:512])[g % 3]
                        for k in range(4):
                            m = turn(bank[:, k * P:(k + 1) * P], xn_of[nm_][:, h, (4 * q + k) * P:(4 * q + k + 1) * P])
                        m.then_inc(N(nm_, "t")[0], 1)

            pe.wait_ge(S("cst_in"), 16)
            norm("mix")
            product(PH["w_in"], hhi, hlo, lambda u: N("mix", "lo", 2 * u + 2))

            for e in range(2):
                pe.wait_ge(S(f"evac{e}"), 1 + PH["w_in"].ev1)
            pe.wait_ge(S("pool_in"), 32)
            pe.wait_ge(S("ada_read"), 1 + PH["w_in"].ada1)
            for i in range(4):
                if i:
                    pe.wait_ge(S("pool_mix"), i)
                for f in range(2):
                    for h in range(NH):
                        c = i * 256 + f * P
                        m = pe.matmul(TA[:, f * T:(f + 1) * T], p1[:, h, c:c + P], pmat[:, i, h, :],
                                      start=(h == 0), stop=(h == 1), skip_group_check=True)
                m.then_inc(S("pool_m"), 1)
                pe.wait_ge(S("pool_mix"), i + 1)
                if i:
                    pe.wait_ge(S("pool_f"), i)
                for f in range(2):
                    for k in range(2):
                        m = pe.matmul(TB[:, f * T:(f + 1) * T], wpool[:, i, k, f * P:(f + 1) * P], mixT[:, k, :],
                                      start=(k == 0), stop=(k == 1), skip_group_check=True)
                m.then_inc(S("pool_y"), 1)

            pe.wait_ge(S("pool_f"), 4)
            for g in range(7):
                if g < 6:
                    if g:
                        pe.wait_ge(S("cv_c"), g)
                    for f in range(4):
                        for h in range(NH):
                            c = POOL_W + 512 * g + P * f
                            m = turn(TA[:, f * T + h * P:f * T + h * P + P], p1[:, h, c:c + P])
                    m.then_inc(S("cv_t"), 1)
                if g >= 1:
                    pe.wait_ge(S("cv_m"), g)
                    if g >= 2:
                        pe.wait_ge(S("cv_e"), g - 1)
                    for h in range(NH):
                        for f in range(4):
                            m = turn(TB[:, h * 512 + f * P:h * 512 + f * P + P], cbuf[(g - 1) % 2][:, f, h * P:h * P + P])
                    m.then_inc(S("cv_b"), 1)

            A8, B8 = v(TA, P), v(TB, P)
            for hf in range(NH):
                q3 = p1[:, hf, POOL_W:POOL_W + 1024].rearrange("p (a b) -> p a b", b=P)
                k3 = p1[:, hf, POOL_W + 1024:POOL_W + 2048].rearrange("p (a b) -> p a b", b=P)
                v3 = p1[:, hf, POOL_W + 2048:POOL_W + 3072].rearrange("p (a b) -> p a b", b=P)
                gd = gdec[:, hf * 8:hf * 8 + 8]
                pe.wait_ge(S("gp_g"), 1)
                pe.wait_ge(S("cv_e"), 6)
                if hf:
                    pe.wait_ge(S("dn_lo"), 1)
                for j, m_ in enumerate(("upto", "after", "chunk0", "chunk1")):
                    m = pe.matmul(TA[:, 8 * j:8 * j + 8], C(m_), gd, start=True, stop=True)
                m.then_inc(S("dn_sum"), 1)
                pe.wait_ge(S("dn_tg"), hf + 1)
                for b in range(2):
                    pe.matmul(TB[:, 512 * b:512 * b + 512], C("ones"), KB[:, 4 * b:4 * b + 4, :].rearrange("p a b -> p (a b)"),
                              start=True, stop=False, skip_group_check=True)
                    for h in range(4 * b, 4 * b + 4):
                        m = pe.matmul(B8[:, h, :], KB[:, h, :], C("negones"), start=False, stop=(h % 4 == 3),
                                      skip_group_check=True)
                m.then_inc(S("dn_diff"), 1)
                pe.wait_ge(S("dn_ex"), hf + 1)
                pe.wait_ge(S("dn_kb"), hf + 1)
                for h in range(8):
                    m = turn(A8[:, h, :], k3[:, h, :])
                m.then_inc(S("dn_t"), 1)
                pe.wait_ge(S("dn_dm"), hf + 1)
                for h in range(8):
                    m = turn(B8[:, h, :], KB[:, h, :])
                m.then_inc(S("dn_t"), 1)
                pe.wait_ge(S("dn_tc"), 4 * hf + 1)
                for h in range(8):
                    m = turn(A8[:, h, :], q3[:, h, :])
                m.then_inc(S("dn_t"), 1)
                pe.wait_ge(S("dn_tc"), 4 * hf + 2)
                for h in range(8):
                    m = pe.matmul(B8[:, h, :], KTt[:, h, :], KBT[:, h, :], start=True, stop=True)
                m.then_inc(S("dn_lt_mm"), 1)
                pe.wait_ge(S("dn_tc"), 4 * hf + 3)
                for h in range(8):
                    m = pe.matmul(A8[:, h, :], KTt[:, h, :], QT[:, h, :], start=True, stop=True)
                m.then_inc(S("dn_at_mm"), 1)
                pe.wait_ge(S("dn_lt"), hf + 1)
                pe.wait_ge(S("dn_qd"), hf + 1)
                for h in range(8):
                    m = turn(B8[:, h, :], q3[:, h, :])
                m.then_inc(S("dn_t"), 1)
                pe.wait_ge(S("dn_at"), hf + 1)
                pe.wait_ge(S("dn_tc"), 4 * hf + 4)
                with loop(pe, 6) as lv:
                    c = lv + 6 * hf
                    pe.wait_ge(S("lv_m"), c + 1)
                    for h in range(8):
                        m = pe.matmul(A8[:, h, :], MT[:, h, :], TT[:, h, :], start=True, stop=True)
                    m.then_inc(S("lv_y"), 1)
                    pe.wait_ge(S("lv_yc"), c + 1)
                    for h in range(8):
                        pe.matmul(B8[:, h, :], AA[:, h, :], YY[:, h, :], start=True, stop=True)
                    for h in range(8):
                        m = pe.matmul(A8[:, h, :], YY[:, h, :], AA[:, h, :], start=True, stop=True)
                    m.then_inc(S("lv_z"), 1)
                pe.wait_ge(S("lv_u"), 6 * hf + 6)
                pe.wait_ge(S("dn_mul"), hf + 1)
                for h in range(8):
                    pe.matmul(A8[:, h, :], AA[:, h, :], v3[:, h, :], start=True, stop=True)
                for h in range(8):
                    m = pe.matmul(B8[:, h, :], KB[:, h, :], AA[:, h, :], start=True, stop=True)
                m.then_inc(S("dn_uw"), 1)
                pe.wait_ge(S("dn_uwc"), hf + 1)
                for c in range(2):
                    r = slice(64 * c, 64 * c + 64)
                    n = 2 * hf + c
                    pe.wait_ge(S("sc_u"), n + 1)
                    for h in range(8):
                        m = pe.matmul(A8[r, h, :], KBT[:, h, r], ST[:, h, :], start=True, stop=True)
                    m.then_inc(S("sc_w"), 1)
                    pe.wait_ge(S("sc_v"), n + 1)
                    for h in range(8):
                        pe.matmul(B8[r, h, :], QT[:, h, r], ST[:, h, :], start=True, stop=False, skip_group_check=True)
                        pe.matmul(B8[r, h, :], DT[r, h, r], YY[r, h, :], start=False, stop=True, skip_group_check=True)
                    for h in range(8):
                        m = pe.matmul(A8[:, h, :], k3[r, h, :], YY[r, h, :], start=True, stop=True)
                    m.then_inc(S("sc_s"), 1)
                pe.wait_ge(S("sc_u"), 2 * hf + 3)
                pe.wait_ge(S("dn_y"), hf + 1)
                for h in range(8):
                    m = turn(A8[:, h, :], MT[:, h, :])
                m.then_inc(S("dn_yt"), 1)

            pe.wait_ge(S("pool_lo"), 4)
            product(PH["mix_out"], hhi, hlo, lambda u: (S("dn_lo"), 2))
            norm("mem")
            product(PH["xkv"], hhi, hlo, lambda u: N("mem", "lo", 2 * u + 2))
            for e in range(2):
                pe.wait_ge(S(f"evac{e}"), 1 + PH["xkv"].ev1)
            pe.wait_ge(S("ada_read"), 1 + PH["xkv"].ada1)
            turn_in(pe, turn, "kx", kv, 0, 0)
            norm("xa")
            product(PH["xq"], hhi, hlo, lambda u: N("xa", "lo", 2 * u + 2))
            for e in range(2):
                pe.wait_ge(S(f"evac{e}"), 1 + PH["xq"].ev1)
            pe.wait_ge(S("ada_read"), 1 + PH["xq"].ada1)
            turn_in(pe, turn, "qx", kv, 0, 0)
            attention_pe(pe, turn, "xatt", cross_units())
            product(PH["xo"], hhi, hlo, lambda u: N("xatt", "lo", 8))
            norm("ffn")

            def ffn1_mid(base):
                def f(it):
                    pe.wait_ge(S("evac0"), it + base[0] + 2)
                    pe.wait_ge(S("f1_conv"), it + base[1] + 1)
                    for f_ in range(4):
                        for h in range(NH):
                            m = turn(TA[:, f_ * T + h * P:f_ * T + h * P + P], tok[0][:, h, f_ * P:f_ * P + P])
                    m.then_inc(S("f1_tg"), 1)
                return f

            def ffn1_end(base):
                def f(it):
                    pe.wait_ge(S("evac1"), it + base[0] + 2)
                    pe.wait_ge(S("f1_f"), it + base[1] + 1)
                    for f_ in range(4):
                        for h in range(NH):
                            m = turn(TB[:, f_ * T + h * P:f_ * T + h * P + P], tok[1][:, h, f_ * P:f_ * P + P])
                    m.then_inc(S("f1_tu"), 1)
                return f

            ba, bb = (PH["ffn1a"].ev0, 0), (PH["ffn1b"].ev0, 6)
            product(PH["ffn1a"], hhi, hlo, lambda u: N("ffn", "lo", 2 * u + 2), ffn1_mid(ba), ffn1_end(ba))
            product(PH["down1a"], fhi, flo, lambda u: (S("f1_lo"), u + 2))
            product(PH["ffn1b"], hhi, hlo, lambda u: N("ffn", "lo", 8), ffn1_mid(bb), ffn1_end(bb))
            product(PH["down1b"], fhi, flo, lambda u: (S("f1_lo"), 6 + u + 2))
            norm("pre2")
            product(PH["w_in2"], hhi, hlo, lambda u: N("pre2", "lo", 2 * u + 2))

            for e in range(2):
                pe.wait_ge(S(f"evac{e}"), 1 + PH["w_in2"].ev1)
            pe.wait_ge(S("ada_read"), 1 + PH["w_in2"].ada1)
            for j in range(2):
                if j == 0:
                    pe.wait_ge(S("rope_done"), 1)
                else:
                    pe.wait_ge(S("cmp_kt"), 1)
                for g in range(2):
                    for h in range(NH):
                        c = 1024 + 256 * j + P * g
                        m = turn(TA[:, g * T + h * P:g * T + h * P + P], p2[:, h, c:c + P])
                m.then_inc(S("cmp_t"), 1)
                pe.wait_ge(S("cmp_r"), j + 1)
                pe.wait_ge(S("w1_in"), 16 * (j + 1))
                pe.wait_ge(S("cmp_in"), 64)
                for l in range(32):
                    m = pe.matmul(TA[:, 512:543], w1c[:, l, :], rc1[:, l, :], start=(l == 0), stop=(l == 31))
                m.then_inc(S("cmp_hid"), 1)
                pe.wait_ge(S("cmp_s"), j + 1)
                if j:
                    pe.wait_ge(S("cmp_oc"), 1)
                if j == 0:
                    m = pe.matmul(TB[:, 0:30], w2c[:, 0, :], hid[:, 0:30], start=True, stop=True)
                else:
                    for g in range(2):
                        m = pe.matmul(TB[0:CMP_N, g * P:g * P + P], hid[:, 15 * g:15 * g + 15], w2c[:, 1, :],
                                      start=True, stop=True)
                m.then_inc(S("cmp_o"), 1)
            pe.wait_ge(S("cmp_oc"), 2)
            turn_in2(pe, turn, "n2")
            attention_pe(pe, turn, "natt", nsa_units())
            turn_in2(pe, turn, "m2")
            attention_pe(pe, turn, "matt", moba_units())
            pe.wait_ge(*N("natt", "lo", 4))
            product(PH["w_o"], hhi, hlo, lambda u: N("matt", "lo", 4))

            def gate_row(n):
                for i in range(4):
                    pe.wait_ge(S("dg_done"), 4 * n + i + 1)
                    bank = (TA[:, 0:512], TA[:, 512:1024])[i % 2]
                    pe.matmul(bank, C("ones"), dg[:, :, :].rearrange("p a b -> p (a b)"), start=True, stop=True)\
                        .then_inc(S("gate_mm"), 1)
            gate_row(0)
            norm("pf2")

            def up2_turn(s, e):
                q = PH[f"up2{s}"]

                def f(it):
                    pe.wait_ge(S(f"evac{e}"), it + q.ev0 + 2)
                    pe.wait_ge(S(f"f2_q{e}"), it + 2 * s + 1)
                    tp = (TA, TB)[e]
                    for f_ in range(4):
                        for h in range(NH):
                            m = turn(tp[:, f_ * T + h * P:f_ * T + h * P + P], tok2[e][:, h, f_ * P:f_ * P + P])
                    m.then_inc(S(f"f2_t{e}"), 1)
                return f
            for s in range(4):
                product(PH[f"up2{s}"], hhi, hlo, lambda u: N("pf2", "lo", 2 * u + 2), up2_turn(s, 0), up2_turn(s, 1))
                product(PH[f"down2{s}"], f2hi, f2lo, lambda u: (S("f2_lo"), 4 * s + u + 3))
            gate_row(1)

        @block.scalar
        def _(act):
            def split_hi(q, it, j):
                kind, b, u = q.seq[j]
                if kind == "a":
                    return
                act.wait_ge(S(f"raw_in{j % NSLOT}"), 16 * (it * (len(q.seq) // NSLOT) + q.unit0 // NSLOT + j // NSLOT + 1))
                g = b * q.units + u
                for s in range(2):
                    act.wait_ge(S("mm_done"), it * q.subs + (q.sub0 + 2 * g + s - NRING + 1) + NRING)
                    nc.scalar.copy(whi[(2 * g + s) % NRING][:, :, 0:q.width], raw[j % NSLOT][:, 2 * s:2 * s + 2, 0:q.width])\
                        .then_inc(S("hi_done"), 1)

            def body(q, it, nxt, hooks):
                g = 0
                for j, (kind, b, u) in enumerate(q.seq):
                    if j < LEAD:
                        g += 1
                        continue
                    split_hi(q, it, j)
                    if kind == "g":
                        g += 1
                        for f in hooks.get(g, ()):
                            f(it)
                for j in range(LEAD):
                    if nxt is not None:
                        split_hi(*nxt, j)
                    for f in hooks.get(g + j + 1, ()):
                        f(it)

            def phase(q, hooks, peel=False):
                i0 = order.index(q)
                nq = order[i0 + 1] if i0 + 1 < len(order) else None
                same = nq is not None and nq.width == q.width and not peel and len(nq.seq) // NSLOT >= 1
                m = q.n if same else q.n - 1
                if m:
                    with loop(act, m) as it:
                        body(q, it, (q, it + 1), hooks)
                if not same:
                    body(q, q.n - 1, (nq, 0) if nq is not None else None, hooks)

            def store(q, dst, scale=None, func=ACT.Copy, lastcol=None):
                def hook(b):
                    def f(it):
                        e = b % 2
                        act.wait_ge(S("mm_done"), block_end(q, it, b) + NRING)
                        col = (q.nb * it + b) * q.width
                        if lastcol is not None and isinstance(it, int) and it == q.n - 1 and b == q.nb - 1:
                            col = lastcol
                        nc.scalar.copy(dst[:, :, bass.ds(col, q.width)], GP[:, 2 * e:2 * e + 2, 0:q.width])\
                            .then_inc(S(f"evac{e}"), 1)
                    return f
                return {(b + 1) * q.units + LEAD: [hook(b)] for b in range(q.nb)}

            def norm(nm_, X, ready):
                for w in ready:
                    act.wait_ge(*w)
                for h in range(NH):
                    m = nc.scalar.activation(xn_of[nm_][:, h, :], X[:, h, :], ACT.Square, accum_out=ss[:, h:h + 1])
                    m.then_inc(N(nm_, "ss")[0], 1)
                act.wait_ge(*N(nm_, "ms", 1))
                nc.scalar.activation(rt, ms, ACT.Sqrt).then_inc(N(nm_, "rt")[0], 1)
                for g in range(8):
                    q, h = divmod(g, NH)
                    act.wait_ge(*N(nm_, "f", g + 1))
                    nc.scalar.copy(hhi[:, 4 * q:4 * q + 4, h * P:h * P + P], fbx[g % 2].rearrange("p (a b) -> p a b", b=P))\
                        .then_inc(N(nm_, "hi")[0], 1)

            act.wait_ge(S("x_in"), 16)
            for j in range(LEAD):
                split_hi(order[0], 0, j)
            norm("mix", x, [(S("x_in"), 16)])
            act.wait_ge(S("tab_in"), 16 * 17)
            nc.scalar.activation(csig[:, :], cvec[:, :], ACT.Sigmoid).then_inc(S("csig"), 1)
            phase(PH["w_in"], store(PH["w_in"], p1))

            for i in range(4):
                act.wait_ge(S("pool_m"), i + 1)
                if i:
                    act.wait_ge(S("pool_y"), i)
                nc.scalar.copy(mixT[:, :, :], v(TA, T)[:, 0:2, :]).then_inc(S("pool_mix"), 1)
                act.wait_ge(S("pool_f"), i + 1)
                nc.scalar.copy(hhi[:, 2 * i:2 * i + 2, :], fpool[:, :, :]).then_inc(S("pool_hi"), 1)

            def tap(g):
                act.wait_ge(S("cv_t"), g + 1)
                if g >= 2:
                    act.wait_ge(S("cv_b"), g - 1)
                for f in range(4):
                    m = nc.scalar.activation(cbuf[g % 2][:, f, :], v(TA, T)[:, f, :], ACT.Copy, scale=conv_w[:, 4 * g + f, 3:4])
                m.then_inc(S("cv_a"), 1)
            act.wait_ge(S("pool_lo"), 4)
            tap(0)
            for g in range(6):
                act.wait_ge(S("cv_c"), g + 1)
                nc.scalar.activation(csg[:, :, :], cbuf[g % 2][:, :, :], ACT.Sigmoid).then_inc(S("cv_s"), 1)
                if g < 5:
                    tap(g + 1)
                act.wait_ge(S("cv_b"), g + 1)
                c = POOL_W + 512 * g
                nc.scalar.copy(p1[:, :, c:c + 512], v(TB, 512)).then_inc(S("cv_e"), 1)

            for e in range(2):
                act.wait_ge(S(f"evac{e}"), 1 + PH["w_in"].ev1)
            bl = p1[:, :, IN_W - 16:IN_W - 8]
            nc.scalar.activation(beta.rearrange("p (a b) -> p a b", b=8), bl, ACT.Sigmoid).then_inc(S("gp_b"), 1)
            act.wait_ge(S("gp_ax"), 1)
            nc.scalar.activation(zc, zb, ACT.Exp, scale=-1.0)
            nc.scalar.activation(ea, ea, ACT.Exp).then_inc(S("gp_e"), 1)

            A8, B8 = v(TA, P), v(TB, P)
            for hf in range(NH):
                act.wait_ge(S("dn_ms"), hf + 1)
                nc.scalar.activation(r16, m16, ACT.Sqrt).then_inc(S("dn_rt"), 1)
                act.wait_ge(S("dn_sum"), hf + 1)
                nc.scalar.activation(ex, TA[:, 0:32], ACT.Exp).then_inc(S("dn_ex"), 1)
                act.wait_ge(S("dn_dm"), hf + 1)
                nc.scalar.activation(DT[:, :, :], DT[:, :, :], ACT.Exp).then_inc(S("dn_dt"), 1)
                for j, (dst, src) in enumerate(((KTt, A8), (KBT, B8), (QT, A8), (QT, B8))):
                    act.wait_ge(S("dn_t"), 4 * hf + j + 1)
                    if j == 3:
                        act.wait_ge(S("dn_at_mm"), hf + 1)
                    nc.scalar.copy(dst[:, :, :], src).then_inc(S("dn_tc"), 1)
                with loop(act, 6) as lv:
                    act.wait_ge(S("lv_y"), lv + 6 * hf + 1)
                    nc.scalar.copy(YY, A8).then_inc(S("lv_yc"), 1)
                act.wait_ge(S("dn_uw"), hf + 1)
                nc.scalar.copy(TT[:, :, :], A8)
                nc.scalar.copy(KBT[:, :, :], B8).then_inc(S("dn_uwc"), 1)
                z3 = p1[:, hf, POOL_W + 3072:POOL_W + 4096].rearrange("p (a b) -> p a b", b=P)
                nc.scalar.activation(LT[:, :, :], z3, ACT.Sigmoid).then_inc(S("dn_zs"), 1)
                act.wait_ge(S("sc_s"), 2 * hf + 2)
                nc.scalar.copy(MT[:, :, :], B8).then_inc(S("dn_oc"), 1)
                act.wait_ge(S("dn_oms"), hf + 1)
                nc.scalar.activation(r16[:, 0:8], m16[:, 0:8], ACT.Sqrt).then_inc(S("dn_ort"), 1)
                act.wait_ge(S("dn_yt"), hf + 1)
                nc.scalar.copy(hhi[:, 8:16, hf * P:hf * P + P], A8).then_inc(S("dn_hi"), 1)

            phase(PH["mix_out"], {})
            act.wait_ge(S("mem_in"), 16)
            norm("mem", memt, [(S("mem_in"), 16)])
            phase(PH["xkv"], store(PH["xkv"], kv))
            turn_in_act(act, "kx", kTx)
            norm("xa", x, [(S("evac0"), 1 + PH["mix_out"].ev1), (S("evac1"), 1 + PH["mix_out"].ev1)])
            phase(PH["xq"], store(PH["xq"], kv))
            turn_in_act(act, "qx", qTx)
            attention_act(act, "xatt", cross_units())
            phase(PH["xo"], {})
            norm("ffn", x, [(S("evac0"), 1 + PH["xo"].ev1), (S("evac1"), 1 + PH["xo"].ev1)])

            def ffn1(q, fb0):
                def evac(e):
                    def f(it):
                        act.wait_ge(S("mm_done"), block_end(q, it, e) + NRING)
                        nc.scalar.copy(tok[e][:, :, :], GP[:, 2 * e:2 * e + 2, :]).then_inc(S(f"evac{e}"), 1)
                    return f

                def gate(it):
                    act.wait_ge(S("f1_tg"), it + fb0 + 1)
                    act.wait_ge(S("f1_lo"), it + fb0 + 1)
                    for f in range(4):
                        c = 16 * (it + fb0) + 4 * f
                        m = nc.scalar.activation(ft[:, f, :], v(TA, T)[:, f, :], ACT.Identity,
                                                 scale=ffn_w[:, bass.ds(c + 2, 1)], bias=ffn_w[:, bass.ds(c + 3, 1)])
                    m.then_inc(S("f1_a"), 1)
                    act.wait_ge(S("f1_conv"), it + fb0 + 2)
                    nc.scalar.activation(fsg[:, :, :], ft[:, :, :], ACT.Sigmoid).then_inc(S("f1_s"), 1)

                def up(it):
                    act.wait_ge(S("f1_f"), it + fb0 + 2)
                    nc.scalar.copy(fhi[:, bass.ds(4 * it, 4), :], ft[:, :, :]).then_inc(S("f1_hi"), 1)
                return {q.units + LEAD: [evac(0)], 2 * q.units: [gate], 2 * q.units + LEAD: [evac(1), up]}

            phase(PH["ffn1a"], ffn1(PH["ffn1a"], 0))
            phase(PH["down1a"], {})
            phase(PH["ffn1b"], ffn1(PH["ffn1b"], 6))
            phase(PH["down1b"], {})

            for e in range(2):
                act.wait_ge(S(f"evac{e}"), 1 + PH["down1b"].ev1)
            for h in range(NH):
                nc.scalar.activation(xn_f[:, h, :], x[:, h, :], ACT.Square, accum_out=ss[:, h:h + 1]).then_inc(N("fin", "ss")[0], 1)
            act.wait_ge(*N("fin", "ms", 1))
            nc.scalar.activation(rt, ms, ACT.Sqrt).then_inc(N("fin", "rt")[0], 1)
            norm("pre2", x, [(S("fin_x"), 2)])
            phase(PH["w_in2"], store(PH["w_in2"], p2, lastcol=IN2_W - 472))
            for e in range(2):
                act.wait_ge(S(f"evac{e}"), 1 + PH["w_in2"].ev1)
            nc.scalar.activation(gates.rearrange("p (a b) -> p a b", b=24), p2[:, :, 2560:2584], ACT.Sigmoid).then_inc(S("gates"), 1)
            for j in range(2):
                act.wait_ge(S("cmp_t"), j + 1)
                if j:
                    act.wait_ge(S("cmp_r"), 1)
                nc.scalar.copy(kTc, v(TA, T)[:, 0:2, :]).then_inc(S("cmp_kt"), 1)
                act.wait_ge(S("cmp_hb"), j + 1)
                nc.scalar.activation(hid[:, 31:61], hid[:, 0:30], ACT.Sigmoid).then_inc(S("cmp_sg"), 1)
                act.wait_ge(S("cmp_o"), j + 1)
                if j == 0:
                    nc.scalar.copy(kcT, TB[:, 0:30].rearrange("p (a b) -> p a b", b=15)).then_inc(S("cmp_oc"), 1)
                else:
                    nc.scalar.copy(vc, TB[0:CMP_N, 0:256].rearrange("p (a b) -> p a b", b=P)).then_inc(S("cmp_oc"), 1)
            turn_in2_act(act, "n2")
            attention_act(act, "natt", nsa_units())
            turn_in2_act(act, "m2")
            attention_act(act, "matt", moba_units())
            phase(PH["w_o"], store(PH["w_o"], o2))

            def post(n, o, first):
                for w in first:
                    act.wait_ge(*w)
                for h in range(NH):
                    nc.scalar.activation(junk[:, :], o[:, h, :], ACT.Square, accum_out=ss[:, h:h + 1]).then_inc(S("po_ss"), 1)
                    act.wait_ge(S("po_ss"), 2 * n + h + 1)
                act.wait_ge(S("po_ms"), n + 1)
                nc.scalar.activation(rt, ms, ACT.Sqrt).then_inc(S("po_rt"), 1)
                for i in range(4):
                    act.wait_ge(S("gate_mm"), 4 * n + i + 1)
                    nc.scalar.copy(gpb[:, 512 * i:512 * i + 512], TA[:, 512 * (i % 2):512 * (i % 2) + 512]).then_inc(S("gpb"), 1)

            post(0, o2, [(S("evac0"), 1 + PH["w_o"].ev1), (S("evac1"), 1 + PH["w_o"].ev1)])
            norm("pf2", x, [(S("y_mix"), 2)])

            def up2(q, s):
                def evac(e):
                    def f(it):
                        act.wait_ge(S("mm_done"), block_end(q, it, e) + NRING)
                        nc.scalar.activation(tok2[e][:, :, :], GP[:, 2 * e:2 * e + 2, :], ACT.Relu).then_inc(S(f"evac{e}"), 1)
                    return f

                def square(e):
                    def f(it):
                        act.wait_ge(S(f"f2_t{e}"), it + 2 * s + 1)
                        act.wait_ge(S("f2_lo"), 2 * it + 4 * s + e + 1)
                        nc.scalar.activation(fq2[e][:, :, :], v((TA, TB)[e], T), ACT.Square).then_inc(S(f"f2_q{e}"), 1)
                        act.wait_ge(S(f"f2_q{e}"), it + 2 * s + 2)
                        nc.scalar.copy(f2hi[:, bass.ds(8 * it + 4 * e, 4), :], fq2[e][:, :, :]).then_inc(S("f2_hi"), 1)
                    return f
                return {q.units + LEAD: [evac(0)], 2 * q.units: [square(0)], 2 * q.units + LEAD: [evac(1), square(1)]}
            for s in range(4):
                phase(PH[f"up2{s}"], up2(PH[f"up2{s}"], s))
                phase(PH[f"down2{s}"], {}, peel=(s == 3))
            post(1, o3, [(S("evac0"), 1 + PH["down23"].ev1), (S("evac1"), 1 + PH["down23"].ev1)])

        @block.vector
        def _(dve):
            link = Chain(dve, S("dve_step"))
            TTo = nc.vector.tensor_tensor

            def split_lo(q, it, j):
                kind, b, u = q.seq[j]
                if kind == "a":
                    dve.wait_ge(S(f"raw_in{j % NSLOT}"), 16 * (it * (len(q.seq) // NSLOT) + q.unit0 // NSLOT + j // NSLOT + 1))
                    for k in range(4):
                        kt = 4 * u + k
                        c = csig[:, kt:kt + 1]
                        if kt == 0:
                            dve.wait_ge(S("ada_sum"), it + q.ada0 + 1)
                            m = nc.vector.tensor_scalar(ada_acc[:, :], raw[j % NSLOT][:, k, :], c, None, ALU.mult)
                        else:
                            m = nc.vector.scalar_tensor_tensor(ada_acc[:, :], raw[j % NSLOT][:, k, :], c, ada_acc[:, :],
                                                               ALU.mult, ALU.add)
                        if k >= 2:
                            m.then_inc(S("unit_used"), 1)
                            dve.wait_ge(S("unit_used"), it * (2 * len(q.seq)) + 2 * (q.unit0 + j) + (k - 1) + CREDIT)
                        else:
                            link(m)
                    return
                g = b * q.units + u
                for s in range(2):
                    r = (2 * g + s) % NRING
                    dve.wait_ge(S("hi_done"), it * q.subs + (q.sub0 + 2 * g + s + 1))
                    TTo(wlo[r][:, :, 0:q.width], raw[j % NSLOT][:, 2 * s:2 * s + 2, 0:q.width],
                        whi[r][:, :, 0:q.width].bitcast(F32), ALU.subtract).then_inc(S("unit_used"), 1)

            def body(q, it, nxt, hooks):
                g = 0
                for j, (kind, b, u) in enumerate(q.seq):
                    if j < LEAD:
                        g += 1
                        continue
                    split_lo(q, it, j)
                    if kind == "g":
                        g += 1
                        for f in hooks.get(g, ()):
                            f(it)
                for j in range(LEAD):
                    if nxt is not None:
                        split_lo(*nxt, j)
                    for f in hooks.get(g + j + 1, ()):
                        f(it)
                if q.ada:
                    dve.wait_ge(S("ada_sum"), it + q.ada0 + 2)
                    nc.vector.tensor_copy(mod[:, bass.ds(4 * (it + q.ada0), 4)], TB[:, 512:516]).then_inc(S("ada_read"), 1)

            def phase(q, hooks, peel=False, links=0):
                i0 = order.index(q)
                nq = order[i0 + 1] if i0 + 1 < len(order) else None
                same = nq is not None and nq.width == q.width and not peel
                per = links + (8 if q.ada else 0)
                m = q.n if same else q.n - 1
                if m:
                    with loop(dve, m) as it:
                        with link.loop(it, m, per):
                            body(q, it, (q, it + 1), hooks)
                if not same:
                    body(q, q.n - 1, (nq, 0) if nq is not None else None, hooks)

            def add_to_x(q):
                def hook(b):
                    def f(it):
                        e = b % 2
                        dve.wait_ge(S("mm_done"), block_end(q, it, b) + NRING)
                        c = bass.ds((q.nb * it + b) * 512, 512)
                        TTo(x[:, :, c], GP[:, 2 * e:2 * e + 2, :], x[:, :, c], ALU.add).then_inc(S(f"evac{e}"), 1)
                    return f
                return {(b + 1) * q.units + LEAD: [hook(b)] for b in range(q.nb)}

            def rsqrt_mean(nm_, n):
                dve.wait_ge(*N(nm_, "ss", NH * n))
                nc.vector.tensor_scalar(ms, ss, 1.0 / D, EPS, ALU.mult, ALU.add).then_inc(N(nm_, "ms")[0], 1)
                dve.wait_ge(*N(nm_, "rt", n))
                link(nc.vector.reciprocal(rstd, rt))

            def norm(nm_, X, gain, shift=None):
                rsqrt_mean(nm_, 1)
                for h in range(NH):
                    nc.vector.tensor_scalar(xn_of[nm_][:, h, :], X[:, h, :], rstd[:, h:h + 1], None, ALU.mult)\
                        .then_inc(N(nm_, "xn")[0], 1)

                def low(g):
                    q, h = divmod(g, NH)
                    a, t = slice(4 * q, 4 * q + 4), slice(h * P, h * P + P)
                    dve.wait_ge(*N(nm_, "hi", g + 1))
                    TTo(hlo[:, a, t], fbx[g % 2].rearrange("p (a b) -> p a b", b=P), hhi[:, a, t].bitcast(F32),
                        ALU.subtract).then_inc(N(nm_, "lo")[0], 1)
                for g in range(8):
                    q, h = divmod(g, NH)
                    dve.wait_ge(*N(nm_, "t", g + 1))
                    bank = (TA[:, 0:512], TA[:, 512:1024], TB[:, 0:512])[g % 3].rearrange("p (a b) -> p a b", b=P)
                    f3 = fbx[g % 2].rearrange("p (a b) -> p a b", b=P)
                    if g >= 2:
                        dve.wait_ge(*N(nm_, "lo", g - 1))
                    m = TTo(f3, bank, cols(gain[:, 4 * q:4 * q + 4], P), ALU.mult)
                    if shift is not None:
                        link(m)
                        m = TTo(f3, f3, cols(shift[:, 4 * q:4 * q + 4], P), ALU.add)
                    m.then_inc(N(nm_, "f")[0], 1)
                    if g:
                        low(g - 1)
                low(7)

            for name, n in (("unit_used", CREDIT), ("mm_done", NRING), ("evac0", 1), ("evac1", 1), ("ada_sum", 1),
                            ("ada_read", 1), ("f1_lo", 1), ("f2_lo", 2), ("f1_conv", 1), ("f1_f", 1), ("f2_q0", 1), ("f2_q1", 1)):
                dve.sem_inc(S(name), n)
            dve.wait_ge(S("cst_in"), 16)
            for j in range(LEAD):
                split_lo(order[0], 0, j)
            dve.wait_ge(S("tab_in"), 16 * 17)
            norm("mix", x, gains[:, 0, :])
            dve.wait_ge(S("csig"), 1)
            link(TTo(csig[:, :], csig[:, :], cvec[:, :], ALU.mult))
            phase(PH["w_in"], {})

            for i in range(4):
                dve.wait_ge(S("pool_y"), i + 1)
                if i:
                    dve.wait_ge(S("pool_lo"), i)
                TTo(fpool[:, :, :], v(TB, T)[:, 0:2, :], cols(pool_s[:, 2 * i:2 * i + 2], T), ALU.mult).then_inc(S("pool_f"), 1)
                dve.wait_ge(S("pool_hi"), i + 1)
                TTo(hlo[:, 2 * i:2 * i + 2, :], fpool[:, :, :], hhi[:, 2 * i:2 * i + 2, :].bitcast(F32),
                    ALU.subtract).then_inc(S("pool_lo"), 1)

            for g in range(6):
                dve.wait_ge(S("cv_a"), g + 1)
                cb = cbuf[g % 2]
                for s in range(1, 4):
                    for f in range(4):
                        m = nc.vector.scalar_tensor_tensor(cb[:, f, s:T], v(TA, T)[:, f, 0:T - s], conv_w[:, 4 * g + f, 3 - s:4 - s],
                                                           cb[:, f, s:T], ALU.mult, ALU.add)
                    if s < 3:
                        link(m)
                m.then_inc(S("cv_c"), 1)
                dve.wait_ge(S("cv_s"), g + 1)
                TTo(cb[:, :, :], cb[:, :, :], csg[:, :, :], ALU.mult).then_inc(S("cv_m"), 1)

            dve.wait_ge(S("gp_b"), 1)
            al = p1[:, :, IN_W - 8:IN_W]
            link(TTo(za.rearrange("p (a b) -> p a b", b=8), al, rows(dtb, 2), ALU.add))
            nc.vector.scalar_tensor_tensor(zb, za, -1.0, za, ALU.mult, ALU.max).then_inc(S("gp_ax"), 1)
            dve.wait_ge(S("gp_e"), 1)
            link(nc.vector.tensor_scalar(zd, zc, 2.0, None, ALU.add))
            link(nc.vector.reciprocal(ze, zd))
            link(TTo(zc, zc, ze, ALU.mult))
            link(TTo(zd, zc, zc, ALU.mult))
            link(nc.vector.tensor_scalar(ze, zd, 1.0 / 19, None, ALU.mult))
            for c in (17, 15, 13, 11, 9, 7, 5, 3):
                link(nc.vector.scalar_tensor_tensor(ze, ze, 1.0 / c, zd, ALU.add, ALU.mult))
            link(nc.vector.scalar_tensor_tensor(ze, ze, 1.0, zc, ALU.add, ALU.mult))
            link(nc.vector.tensor_scalar(za, za, 0.0, None, ALU.max))
            link(nc.vector.scalar_tensor_tensor(ze, ze, 2.0, za, ALU.mult, ALU.add))
            nc.vector.scalar_tensor_tensor(gdec.rearrange("p (a b) -> p a b", b=8), ze.rearrange("p (a b) -> p a b", b=8), -1.0,
                                           rows(ea, 2), ALU.mult, ALU.mult).then_inc(S("gp_g"), 1)
            dve.wait_ge(S("gp_g"), 1)

            A8, B8 = v(TA, P), v(TB, P)
            for hf in range(NH):
                q3 = p1[:, hf, POOL_W:POOL_W + 1024].rearrange("p (a b) -> p a b", b=P)
                k3 = p1[:, hf, POOL_W + 1024:POOL_W + 2048].rearrange("p (a b) -> p a b", b=P)
                v3 = p1[:, hf, POOL_W + 2048:POOL_W + 3072].rearrange("p (a b) -> p a b", b=P)
                z3 = p1[:, hf, POOL_W + 3072:POOL_W + 4096].rearrange("p (a b) -> p a b", b=P)
                gd = gdec[:, hf * 8:hf * 8 + 8]
                bt = beta[:, hf * 8:hf * 8 + 8]
                dve.wait_ge(S("cv_e"), 6)
                if hf == 0:
                    nc.vector.memset(ST, 0.0).then_inc(S("sc_u"), 1)
                TTo(KB[:, :, :], rows(C("upto"), 8), cols(gd, P), ALU.mult).then_inc(S("dn_tg"), 1)
                for i, t3 in enumerate((q3, k3)):
                    link(TTo(SQ, t3, t3, ALU.mult))
                    link(nc.vector.tensor_reduce(s16[:, 8 * i:8 * i + 8], SQ, AX.X, ALU.add))
                nc.vector.tensor_scalar(m16, s16, EPS, None, ALU.add).then_inc(S("dn_ms"), 1)
                dve.wait_ge(S("dn_rt"), hf + 1)
                link(nc.vector.reciprocal(i16, r16))
                link(nc.vector.tensor_scalar(i16[:, 0:8], i16[:, 0:8], P ** -0.5, None, ALU.mult))
                link(TTo(k3, k3, cols(i16[:, 8:16], P), ALU.mult))
                link(TTo(q3, q3, cols(i16[:, 0:8], P), ALU.mult))
                dve.wait_ge(S("dn_diff"), hf + 1)
                TTo(DT[:, :, :], B8, rows(C("chunk_mask"), 8), ALU.add).then_inc(S("dn_dm"), 1)
                TTo(KB[:, :, :], k3, cols(bt, P), ALU.mult).then_inc(S("dn_kb"), 1)
                link(nc.vector.tensor_copy(TT[:, :, :], rows(ident, 8)))
                link(nc.vector.tensor_copy(AA[:, :, :], rows(ident, 8)))
                dve.wait_ge(S("dn_dt"), hf + 1)
                dve.wait_ge(S("dn_lt_mm"), hf + 1)
                link(TTo(LT[:, :, :], B8, DT[:, :, :], ALU.mult))
                TTo(LT[:, :, :], LT[:, :, :], rows(C("strict"), 8), ALU.mult).then_inc(S("dn_lt"), 1)
                dve.wait_ge(S("dn_ex"), hf + 1)
                dve.wait_ge(S("dn_t"), 4 * hf + 3)
                TTo(q3, q3, cols(ex[:, 0:8], P), ALU.mult).then_inc(S("dn_qd"), 1)
                dve.wait_ge(S("dn_at_mm"), hf + 1)
                TTo(DT[:, :, :], A8, DT[:, :, :], ALU.mult).then_inc(S("dn_at"), 1)
                link(TTo(k3, k3, cols(ex[:, 8:16], P), ALU.mult))
                link(TTo(v3, v3, cols(bt, P), ALU.mult))
                dve.wait_ge(S("dn_kb"), hf + 1)
                TTo(KB[:, :, :], KB[:, :, :], cols(ex[:, 0:8], P), ALU.mult).then_inc(S("dn_mul"), 1)
                dve.wait_ge(S("dn_lt"), hf + 1)
                with loop(dve, 6) as lv:
                    c = lv + 6 * hf
                    TTo(MT[:, :, :], LT[:, :, :], rows(cst[:, bass.ds(CAT["levels"][0] + lv * P, P)], 8), ALU.mult).then_inc(S("lv_m"), 1)
                    dve.wait_ge(S("lv_z"), c + 1)
                    TTo(TT[:, :, :], TT[:, :, :], B8, ALU.subtract)
                    TTo(AA[:, :, :], AA[:, :, :], A8, ALU.subtract).then_inc(S("lv_u"), 1)
                    dve.wait_ge(S("lv_u"), c + 1)
                for c in range(2):
                    r = slice(64 * c, 64 * c + 64)
                    n = 2 * hf + c
                    dve.wait_ge(S("sc_w"), n + 1)
                    TTo(YY[r, :, :], TT[r, :, :], A8[r, :, :], ALU.subtract).then_inc(S("sc_v"), 1)
                    dve.wait_ge(S("sc_s"), n + 1)
                    link(TTo(ST, ST, cols(ex[:, 16 + 8 * c:24 + 8 * c], P), ALU.mult))
                    TTo(ST, ST, A8, ALU.add).then_inc(S("sc_u"), 1)
                dve.wait_ge(S("dn_zs"), hf + 1)
                link(TTo(z3, z3, LT[:, :, :], ALU.mult))
                dve.wait_ge(S("dn_oc"), hf + 1)
                link(TTo(SQ, MT[:, :, :], MT[:, :, :], ALU.mult))
                link(nc.vector.tensor_reduce(s16[:, 0:8], SQ, AX.X, ALU.add))
                nc.vector.tensor_scalar(m16[:, 0:8], s16[:, 0:8], 1.0 / P, EPS, ALU.mult, ALU.add).then_inc(S("dn_oms"), 1)
                dve.wait_ge(S("dn_ort"), hf + 1)
                link(nc.vector.reciprocal(i16[:, 0:8], r16[:, 0:8]))
                link(TTo(MT[:, :, :], MT[:, :, :], cols(i16[:, 0:8], P), ALU.mult))
                link(TTo(MT[:, :, :], MT[:, :, :], rows(ngb[:, :], 8), ALU.mult))
                TTo(MT[:, :, :], MT[:, :, :], z3, ALU.mult).then_inc(S("dn_y"), 1)
                dve.wait_ge(S("dn_hi"), hf + 1)
                t = slice(hf * P, hf * P + P)
                TTo(hlo[:, 8:16, t], A8, hhi[:, 8:16, t].bitcast(F32), ALU.subtract).then_inc(S("dn_lo"), 1)

            phase(PH["mix_out"], add_to_x(PH["mix_out"]))
            dve.wait_ge(S("mem_in"), 16)
            norm("mem", memt, gains[:, 2, :])
            phase(PH["xkv"], {})
            norm("xa", x, gains[:, 1, :])
            phase(PH["xq"], {})
            dve.wait_ge(*N("qx", "c", 4))
            dve.sem_inc(N("xatt", "go")[0], 1)
            attention_dve(dve, link, "xatt", cross_units())
            phase(PH["xo"], add_to_x(PH["xo"]))
            norm("ffn", x, gains[:, 3, :])

            def ffn1(q, fb0):
                def gate(it):
                    dve.wait_ge(S("f1_a"), it + fb0 + 1)
                    for s in (1, 2):
                        for f in range(4):
                            m = nc.vector.scalar_tensor_tensor(ft[:, f, s:T], v(TA, T)[:, f, 0:T - s],
                                                               ffn_w[:, bass.ds(16 * (it + fb0) + 4 * f + 2 - s, 1)],
                                                               ft[:, f, s:T], ALU.mult, ALU.add)
                        if s == 1:
                            link(m)
                    m.then_inc(S("f1_conv"), 1)
                    dve.wait_ge(S("f1_s"), it + fb0 + 1)
                    link(TTo(ft[:, :, :], ft[:, :, :], fsg[:, :, :], ALU.mult))

                def up(it):
                    dve.wait_ge(S("f1_tu"), it + fb0 + 1)
                    TTo(ft[:, :, :], v(TB, T), ft[:, :, :], ALU.mult).then_inc(S("f1_f"), 1)
                    dve.wait_ge(S("f1_hi"), it + fb0 + 1)
                    TTo(flo[:, bass.ds(4 * it, 4), :], ft[:, :, :], fhi[:, bass.ds(4 * it, 4), :].bitcast(F32),
                        ALU.subtract).then_inc(S("f1_lo"), 1)
                return {2 * q.units: [gate], 2 * q.units + LEAD: [up]}

            phase(PH["ffn1a"], ffn1(PH["ffn1a"], 0), links=2)
            phase(PH["down1a"], add_to_x(PH["down1a"]))
            phase(PH["ffn1b"], ffn1(PH["ffn1b"], 6), links=2)
            phase(PH["down1b"], add_to_x(PH["down1b"]))

            dve.wait_ge(S("fgb_in"), 16)
            rsqrt_mean("fin", 1)
            for h in range(NH):
                link(nc.vector.tensor_scalar(x[:, h, :], x[:, h, :], rstd[:, h:h + 1], None, ALU.mult))
                TTo(x[:, h, :], x[:, h, :], fgb[:, :], ALU.mult).then_inc(S("fin_x"), 1)
            def modulation(j, c0, gi):
                link(TTo(shifts[:, j, :], mod[:, c0:c0 + 16], b_ada[:, c0:c0 + 16], ALU.add))
                link(TTo(mod[:, c0 + 16:c0 + 32], mod[:, c0 + 16:c0 + 32], b_ada[:, c0 + 16:c0 + 32], ALU.add))
                link(nc.vector.scalar_tensor_tensor(gains[:, gi, :], mod[:, c0 + 16:c0 + 32], 1.0, gains[:, gi, :], ALU.add, ALU.mult))
            modulation(0, 0, 4)
            norm("pre2", x, gains[:, 4, :], shifts[:, 0, :])
            phase(PH["w_in2"], {})

            for e in range(2):
                dve.wait_ge(S(f"evac{e}"), 1 + PH["w_in2"].ev1)
            ropes = [(0, 8), (KV0, 2), (KV0 + 512, 2), (KV0 + 1024, 2), (QM0, 8), (QM0 + 1024, 8)]

            def rope(c0, n, h):
                xx = p2[:, h, c0:c0 + n * P].rearrange("p (a b) -> p a b", b=P)
                x1, x2 = xx[:, :, 0:64], xx[:, :, 64:P]
                cs, sn = rows(C("cos", 64 * h, 64), n), rows(C("sin", 64 * h, 64), n)
                TTo(rp[0][:, 0:n, :], x1, cs, ALU.mult)
                TTo(rp[1][:, 0:n, :], x2, sn, ALU.mult)
                TTo(rp[2][:, 0:n, :], x1, sn, ALU.mult)
                link(TTo(rp[3][:, 0:n, :], x2, cs, ALU.mult))
                TTo(x1, rp[0][:, 0:n, :], rp[1][:, 0:n, :], ALU.subtract)
                link(TTo(x2, rp[3][:, 0:n, :], rp[2][:, 0:n, :], ALU.add))
            for c0, n in ropes:
                for h in range(NH):
                    rope(c0, n, h)
            dve.sem_inc(S("rope_done"), 1)
            for j in range(2):
                dve.wait_ge(S("cmp_kt"), j + 1)
                dve.wait_ge(S("cmp_in"), 64)
                if j:
                    dve.wait_ge(S("cmp_hid"), 1)
                for g in range(2):
                    for half in range(2):
                        src = kTc[:, g, 16 * half:16 * half + 240].rearrange("p (c l) -> p l c", l=16)
                        nc.vector.tensor_copy(rc1[:, 16 * half:16 * half + 16, 15 * g:15 * g + 15], src)
                nc.vector.tensor_copy(rc1[:, :, 30], posT[:, j, :]).then_inc(S("cmp_r"), 1)
                dve.wait_ge(S("cmp_hid"), j + 1)
                if j:
                    dve.wait_ge(S("cmp_o"), 1)
                link(nc.vector.tensor_copy(hid[:, 30:31], TA[:, 542:543]))
                nc.vector.tensor_scalar(hid[:, 0:30], TA[:, 512:542], hid[:, 30:31], None, ALU.add).then_inc(S("cmp_hb"), 1)
                dve.wait_ge(S("cmp_sg"), j + 1)
                TTo(hid[:, 0:30], hid[:, 0:30], hid[:, 31:61], ALU.mult).then_inc(S("cmp_s"), 1)
            dve.wait_ge(S("gates"), 1)
            dve.wait_ge(S("cmp_oc"), 2)
            dve.wait_ge(*N("n2", "c", 3))
            dve.sem_inc(N("natt", "go")[0], 1)
            attention_dve(dve, link, "natt", nsa_units())
            dve.wait_ge(*N("m2", "c", 4))
            dve.sem_inc(N("matt", "go")[0], 1)
            attention_dve(dve, link, "matt", moba_units())
            dve.sem_inc(S("o_lo"), 1)
            phase(PH["w_o"], {})

            def post(n, o, c0, done):
                dve.wait_ge(S("po_ss"), 2 * n + 2)
                nc.vector.tensor_scalar(ms, ss, 1.0 / D, EPS, ALU.mult, ALU.add).then_inc(S("po_ms"), 1)
                dve.wait_ge(S("po_rt"), n + 1)
                link(nc.vector.reciprocal(rstd, rt))
                link(TTo(mod[:, c0:c0 + 16], mod[:, c0:c0 + 16], b_ada[:, c0:c0 + 16], ALU.add))
                for i in range(4):
                    if i:
                        dve.wait_ge(S("gate_mm"), 4 * n + i)
                    if i >= 2:
                        dve.wait_ge(S("gpb"), 4 * n + i - 1)
                    TTo(dg[:, :, :], rows(ident, 4), cols(mod[:, c0 + 4 * i:c0 + 4 * i + 4], P), ALU.mult).then_inc(S("dg_done"), 1)
                dve.wait_ge(S("gpb"), 4 * n + 4)
                dve.wait_ge(S("pn_in"), 16 * (n + 1))
                link(TTo(gpb[:, :], gpb[:, :], pnb[:, :], ALU.mult))
                for h in range(NH):
                    link(nc.vector.scalar_tensor_tensor(o[:, h, :], o[:, h, :], rstd[:, h:h + 1], gpb[:, :], ALU.mult, ALU.mult))
                    TTo(x[:, h, :], x[:, h, :], o[:, h, :], ALU.add).then_inc(S(done), 1)

            post(0, o2, 32, "y_mix")
            modulation(1, 48, 5)
            dve.wait_ge(S("y_mix"), 2)
            norm("pf2", x, gains[:, 5, :], shifts[:, 1, :])

            def up2(q, s):
                def low(e):
                    def f(it):
                        dve.wait_ge(S("f2_hi"), 2 * it + 4 * s + e + 1)
                        c = bass.ds(8 * it + 4 * e, 4)
                        TTo(f2lo[:, c, :], fq2[e][:, :, :], f2hi[:, c, :].bitcast(F32), ALU.subtract).then_inc(S("f2_lo"), 1)
                    return f
                return {2 * q.units: [low(0)], 2 * q.units + LEAD: [low(1)]}

            def down2(q, s):
                def hook(b):
                    def f(it):
                        dve.wait_ge(S("mm_done"), block_end(q, it, b) + NRING)
                        c = bass.ds((2 * it + b) * 512, 512)
                        if s == 0:
                            m = nc.vector.tensor_copy(o3[:, :, c], GP[:, 2 * b:2 * b + 2, :])
                        else:
                            m = TTo(o3[:, :, c], GP[:, 2 * b:2 * b + 2, :], o3[:, :, c], ALU.add)
                        m.then_inc(S(f"evac{b}"), 1)
                    return f
                return {(b + 1) * q.units + LEAD: [hook(b)] for b in range(2)}
            for s in range(4):
                phase(PH[f"up2{s}"], up2(PH[f"up2{s}"], s))
                phase(PH[f"down2{s}"], down2(PH[f"down2{s}"], s), peel=(s == 3))
            post(1, o3, 80, "y_done")


_INS = {
    "x": None, "mem": None, "w_in": "m", "w_mix_out": "m", "w_xq": "m", "w_xkv": "m", "w_xo": "m",
    "w_gate": "m", "w_up": "m", "w_down": "m", "w_ada_2": "m", "w_in_2": "m", "w_o_2": "m", "w_up_2": "m", "w_down_2": "m",
    "mix_norm_g": "c", "xa_norm_g": "c", "mem_norm_g": "c", "ffn_norm_g": "c", "pre_norm_mix_2": "c", "pre_norm_ffn_2": "c",
    "pool_scale": "c", "b_ada_2": "c", "c_2": "c", "dn_dt_bias": "v", "dn_a_log": "v", "dn_norm_g": "v",
    "final_norm_g": "v", "post_norm_mix_2": "v", "post_norm_ffn_2": "v",
}


def kernel(**inputs):
    import concourse.bacc as bacc
    from concourse.bass_utils import run_bass_kernel_spmd as run

    nc = bacc.Bacc("TRN2", target_bir_lowering=False, num_devices=1)
    arrays, A = {}, {}

    def give(name, a):
        a = np.ascontiguousarray(a)
        arrays["in_" + name] = a
        A[name] = nc.dram_tensor("in_" + name, a.shape, F32, kind="ExternalInput").ap()

    for name, how in _INS.items():
        a = np.asarray(inputs[name])
        if how == "m":
            a = a.reshape(a.shape[-2], a.shape[-1])
        elif how == "c":
            a = a.reshape(-1, P).T
        elif how == "v":
            a = a.reshape(-1)
        give(name, a)
    give("dn_conv_w", np.asarray(inputs["dn_conv_w"]).reshape(4, 24, P).transpose(2, 1, 0))
    give("ffn_conv_w", np.asarray(inputs["ffn_conv_w"]).reshape(3, FF1 // P, P, 1).transpose(2, 0, 1, 3))
    give("ffn_conv_b", np.asarray(inputs["ffn_conv_b"]).reshape(FF1 // P, P, 1).transpose(1, 0, 2))
    give("w_pool", np.asarray(inputs["w_pool"]).reshape(4, 2, P, 256).transpose(2, 0, 1, 3))
    for n in ("cmp_k_", "cmp_v_"):
        give(n + "pos_2", np.asarray(inputs[n + "pos_2"]).reshape(32, P).T)
        give(n + "w1_2", np.asarray(inputs[n + "w1_2"]).reshape(32, P, P).transpose(1, 0, 2))
        give(n + "w2_2", np.asarray(inputs[n + "w2_2"]).reshape(P, P))
    give("const", CONST)
    give("pool_mats", pooling_table())
    out = nc.dram_tensor("out_0", (1, T, D), F32, kind="ExternalOutput").ap()
    program(nc, A, out)
    return run(nc, [arrays], core_ids=[0]).results[0]["out_0"]
```

```python
import numpy as np
from contextlib import ExitStack, contextmanager

import concourse.bass as bass
from concourse import mybir

F32 = mybir.dt.float32
F32R = mybir.dt.float32r
ALU = mybir.AluOpType
ACT = mybir.ActivationFunctionType
AX = mybir.AxisListType

P = 128
T = 256
NH = T // P
D = 2048
KT = D // P
EPS = 1e-6
NEG = -1e30
POOL_W = 1024
DN_W = 1024
DN_H = 8
IN_W = 5136
XA_H = 4
XA_D = 512
FF1 = 5632
FF2 = 8192
NSA_W = 2584
IN2_W = NSA_W + 3 * 1024
W2A = 432
UK = 4
NSLOT = 4
NRING = 4
LEAD = 2
TABS = 18
CREDIT = 8
CMP_N = (T - 32) // 16 + 1


def constant_table():
    parts, at, n = [], {}, 0

    def put(name, a):
        nonlocal n
        a = np.asarray(a, np.float32).reshape(P, -1)
        at[name] = (n, a.shape[1])
        parts.append(a)
        n += a.shape[1]

    i = np.arange(P)
    same = (i[:, None] // 64) == (i[None, :] // 64)
    put("ident", np.eye(P))
    put("ones", np.ones((P, P)))
    put("negones", -np.ones((P, P)))
    put("upto", same & (i[:, None] <= i[None, :]))
    put("after", same & (i[:, None] > i[None, :]))
    put("chunk0", np.repeat((i < 64)[:, None], P, 1))
    put("chunk1", np.repeat((i >= 64)[:, None], P, 1))
    put("chunk_mask", np.where(same & (i[:, None] <= i[None, :]), 0.0, NEG))
    put("strict", same & (i[:, None] < i[None, :]))
    levels = []
    for s in range(6):
        b = 1 << s
        levels.append((i[:, None] // (2 * b) == i[None, :] // (2 * b))
                      & (i[:, None] % (2 * b) < b) & (i[None, :] % (2 * b) >= b))
    put("levels", np.stack(levels, 1))
    put("causal", np.where(i[None, :] <= i[:, None], 0.0, NEG))
    ang = (np.arange(T, dtype=np.float32)[:, None]
           * (np.float32(10000.0) ** (-np.arange(0, P, 2, dtype=np.float32) / P))[None, :])
    put("cos", np.cos(ang).reshape(NH, P, 64).transpose(1, 0, 2))
    put("sin", np.sin(ang).reshape(NH, P, 64).transpose(1, 0, 2))
    t = np.arange(T)
    ok = (np.arange(CMP_N) * 16 + 31)[None, :] <= t[:, None]
    put("cmp_mask", np.where(ok, 0.0, NEG).reshape(NH, P, CMP_N).transpose(1, 0, 2))
    put("cmp_valid", ok.any(1).reshape(NH, P).T)
    return np.concatenate(parts, 1), at


def pooling_table():
    t = np.arange(T)
    m = []
    for w in (2, 4, 8, 16):
        b = ((t[:, None] <= t[None, :]) & (t[:, None] > t[None, :] - w)).astype(np.float32)
        b = b / np.minimum(t + 1, w)[None, :].astype(np.float32) - np.eye(T, dtype=np.float32)
        m.append(b.reshape(NH, P, T).transpose(1, 0, 2))
    return np.ascontiguousarray(np.stack(m, 1).reshape(P, -1))


CONST, CAT = constant_table()


class Phase:

    def __init__(self, name, n, nb, units, width, ada=False):
        self.name, self.n, self.nb, self.units, self.width, self.ada = name, n, nb, units, width, ada
        self.seq = []
        g = [("g", b, u) for b in range(nb) for u in range(units)]
        for i, x in enumerate(g):
            self.seq.append(x)
            if ada and i % 2 == 1:
                self.seq.append(("a", 0, i // 2))
        assert len(self.seq) % NSLOT == 0 and (2 * len(g)) % NRING == 0


def plan():
    ph = [Phase("w_in", 6, 2, 4, 428, True), Phase("mix_out", 2, 2, 4, 512, True),
          Phase("xkv", 4, 2, 4, 512, True), Phase("xq", 2, 2, 4, 512, True),
          Phase("xo", 2, 2, 4, 512, True),
          Phase("ffn1a", 6, 2, 4, 512), Phase("down1a", 2, 2, 6, 512),
          Phase("ffn1b", 5, 2, 4, 512), Phase("down1b", 1, 4, 5, 512),
          Phase("w_in2a", 3, 2, 4, W2A, True), Phase("w_in2b", 2, 2, 4, 512, True), Phase("w_in2c", 1, 2, 4, 512, True),
          Phase("w_oa", 1, 2, 4, 512, True), Phase("w_ob", 1, 2, 4, 512, True)]
    for s in range(4):
        ph += [Phase(f"up2{s}", 2, 2, 4, 512), Phase(f"down2{s}", 2, 2, 4, 512)]
    units = subs = evs = adas = 0
    for q in ph:
        q.unit0, q.sub0, q.ev0, q.ada0 = units, subs, evs, adas
        q.subs = 2 * q.nb * q.units
        units += q.n * len(q.seq)
        subs += q.n * q.subs
        evs += q.n * q.nb // 2
        adas += q.n * q.ada
        q.sub1, q.ev1, q.ada1 = subs, evs, adas
    assert adas == 24
    return {q.name: q for q in ph}


def program(nc, A, out):
    PH = plan()
    order = list(PH.values())
    with ExitStack() as ctx:
        sems = {}

        def S(name):
            if name not in sems:
                sems[name] = ctx.enter_context(nc.semaphore(name))
            return sems[name]

        def fixed(name, shape, dt=F32):
            return ctx.enter_context(nc.sbuf_tensor(name, shape, dt))

        raw = [fixed(f"raw{i}", [P, UK, 512]) for i in range(NSLOT)]
        whi = [fixed(f"whi{i}", [P, 2, 512], F32R) for i in range(NRING)]
        wlo = [fixed(f"wlo{i}", [P, 2, 512], F32R) for i in range(NRING)]
        x = fixed("x", [P, NH, D])
        hhi = fixed("hhi", [P, KT, T], F32R)
        hlo = fixed("hlo", [P, KT, T], F32R)
        cst = fixed("cst", [P, CONST.shape[1]])
        gains = fixed("gains", [P, 6, KT])
        post_gain = fixed("post_gain", [P, 2, KT])
        shifts = fixed("shifts", [P, 2, KT])
        conv_w = fixed("conv_w", [P, 24, 4])
        ffn_w = fixed("ffn_w", [P, FF1 // P * 4])
        pool_s = fixed("pool_s", [P, 8])
        mod = fixed("mod", [P, 96])
        b_ada = fixed("b_ada", [P, 96])
        cvec = fixed("cvec", [P, KT])
        csig = fixed("csig", [P, KT])
        ada_acc = fixed("ada_acc", [P, 512])
        small = fixed("small", [P, 320])
        ngb = fixed("ngb", [P, P])
        flat = fixed("flat", [P, 1024])
        fbx = [flat[:, 512 * i:512 * i + 512] for i in range(2)]
        kTc = flat[:, 0:512].rearrange("p (a b) -> p a b", b=T)
        kcT = flat[:, 512:512 + 2 * CMP_N].rearrange("p (a b) -> p a b", b=CMP_N)
        vc = flat[0:CMP_N, 640:896].rearrange("p (a b) -> p a b", b=P)
        arena0 = ((nc.sbuf_base + 31) // 32) * 32
        arena_end = nc.sbuf_usable_end
        names = iter(range(10 ** 6))

        class Arena:
            def __init__(self):
                self.at = arena0

            def __call__(self, name, shape, dt=F32):
                t = nc.alloc_sbuf_tensor_at(f"{name}_{next(names)}", shape, dt, offset=self.at)
                self.at += (int(np.prod(shape[1:])) * 4 + 31) // 32 * 32
                assert self.at <= arena_end, (name, self.at, arena_end)
                return t

        GP = ctx.enter_context(nc.psum_tensor("GP", [P, 4, 512], F32))
        TA = ctx.enter_context(nc.psum_tensor("TA", [P, 1024], F32))
        TB = ctx.enter_context(nc.psum_tensor("TB", [P, 1024], F32))

        norm_banks = [TA[:, 0:512], TA[:, 512:1024], TB[:, 0:512], GP[:, 2, :], GP[:, 3, :]]

        def C(name, lo=0, n=None):
            a, w = CAT[name]
            return cst[:, a + lo:a + (w if n is None else lo + n)]

        STAGES, grown = {}, dict.fromkeys(("ss", "ms", "rt", "xn", "t", "f", "hi", "lo"), 0)
        for n in ("mix", "mem", "xa", "ffn", "fin", "pre2", "post0", "pf2", "post1"):
            STAGES[n] = ("norm", dict(grown))
            for k, m in (("ss", 2), ("ms", 2), ("rt", 2)) + (n not in ("fin", "post0", "post1")) * (("xn", 2), ("t", 8), ("f", 8), ("hi", 8), ("lo", 8)):
                grown[k] += m
        STAGES |= {n: ("att", {k: (i if k == "go" else g if k in ("o", "hi", "lo") else u)
                               for k in ("go", "qk", "m", "e", "n", "t", "c", "o", "hi", "lo")})
                   for i, (n, u, g) in enumerate((("xatt", 0, 0), ("natt", 2, 8), ("matt", 14, 12)))}
        STAGES |= {n: ("turn", {"t": i, "c": i}) for n, i in (("kx", 0), ("qx", 4), ("n2", 8), ("m2", 11))}

        def N(stage, what, count=0):
            kind, before = STAGES[stage]
            return S(f"{kind}_{what}"), before[what] + count

        ident = C("ident")

        def rows(ap, n):
            return ap.unsqueeze(1).broadcast_to([ap.shape[0], n, ap.shape[1]])

        def cols(ap, n):
            return ap.unsqueeze(2).broadcast_to([ap.shape[0], ap.shape[1], n])

        def v(ps, b):
            return ps[:, :].rearrange("p (a b) -> p a b", b=b)

        _s = [0]

        def sm(n):
            a = _s[0]
            _s[0] += n
            assert _s[0] <= 320
            return small[:, a:a + n]

        ss = sm(2); ms = sm(2); rt = sm(2); rstd = sm(2)
        beta = sm(16); gdec = sm(16); za = sm(16); zb = sm(16); zc = sm(16); zd = sm(16); ze = sm(16)
        dtb = sm(8); ea = sm(8); ex = sm(32); s16 = sm(16); m16 = sm(16); r16 = sm(16); i16 = sm(16)
        gates = sm(48)
        mx = [sm(4), sm(4)]; nm = [sm(4), sm(4)]; sme = [sm(4), sm(4)]; rc = [sm(4), sm(4)]

        ar = Arena()
        p1 = ar("p1", [P, NH, IN_W])
        norm_at = ar.at
        tmp = [ar(f"t{i}", [P, 8, P]) for i in range(9)]
        tmp += [flat[:, :].rearrange("p (a b) -> p a b", b=P)]
        tmp += [p1[:, h, 0:1024].rearrange("p (a b) -> p a b", b=P) for h in range(2)]
        (KB, KBT, KTt, QT, DT, LT, MT, TT, AA, YY) = tmp[:10]
        ST, SQ = tmp[10], tmp[11]
        ar = Arena(); ar.at = norm_at
        pmat = ar("pmat", [P, 4, NH, T]); wpool = ar("wpool", [P, 4, 2, T])
        mixT = ar("mixT", [P, 2, T]); fpool = ar("fpool", [P, 2, T])
        ar = Arena(); ar.at = norm_at
        cbuf = [ar(f"cbuf{i}", [P, 4, T]) for i in range(3)]; csg = ar("csg", [P, 4, T])
        ar = Arena()
        xn = ar("xn", [P, NH, D])
        memt = ar("memt", [P, NH, D])
        ar = Arena()
        kv = ar("kv", [P, NH, 2 * D]); kTx = ar("kTx", [P, KT, T]); qTx = ar("qTx", [P, KT, T])
        xq = kv[:, :, 0:D]
        xpr = [kv[:, 0, 1024 * i:1024 * i + 1024].rearrange("p (a b) -> p a b", b=T) for i in range(2)]
        xpT = [kv[:, 1, 1024 * i:1024 * i + 1024].rearrange("p (a b c) -> p a b c", b=4, c=P) for i in range(2)]
        ar = Arena()
        fhi = ar("fhi", [P, 24, T], F32R); flo = ar("flo", [P, 24, T], F32R)
        tok = [ar(f"tok{i}", [P, NH, 512]) for i in range(2)]
        ft = ar("ft", [P, 4, T]); fsg = ar("fsg", [P, 4, T])
        ar = Arena()
        xn_f = ar("xn_f", [P, NH, D]); fgb = ar("fgb", [P, D])
        ar = Arena()
        p2 = ar("p2", [P, NH, IN2_W])
        qT2 = ar("qT2", [P, 8, T]); kT2 = ar("kT2", [P, 8, T])
        scr2 = ar.at
        pr2 = [p2[:, i, 0:1024].rearrange("p (a b) -> p a b", b=T) for i in range(2)]
        pT2 = [ar(f"pT2{i}", [P, 2, 4, P]) for i in range(3)]
        cmp_at = ar.at
        pr2 += [ar("pr2c", [P, 4, T])]
        ar.at = cmp_at
        posT = ar("posT", [P, 2, 32]); w2c = ar("w2c", [P, 2, P]); hid = ar("hid", [P, 62])
        ar = Arena(); ar.at = scr2
        rc1 = ar("rc1", [P, 32, 31])
        rp = [ar(f"rp{i}", [P, 8, 64]) for i in range(4)]
        assert ar.at <= scr2 + 4 * 3 * 1024
        ar = Arena(); ar.at = scr2 - 16384
        w1c = ar("w1c", [P, 32, P])
        ar = Arena()
        o2 = ar("o2", [P, NH, D]); junk = ar("junk", [P, D]); gpb = [ar("gpb0", [P, D])]; dg = [ar("dg0", [P, 4, P])]
        ar = Arena()
        o3 = ar("o3", [P, NH, D])
        f2hi = ar("f2hi", [P, 16, T], F32R); f2lo = ar("f2lo", [P, 16, T], F32R)
        tok2 = [ar(f"tok2{i}", [P, NH, 512]) for i in range(2)]; fq2 = [ar(f"fq2{i}", [P, 4, T]) for i in range(2)]
        gpb += [ar("gpb1", [P, D])]; dg += [ar("dg1", [P, 4, P])]

        block = ctx.enter_context(nc.Block())

        @contextmanager
        def loop(eng, n):
            if n == 1:
                yield 0
            else:
                with eng.Fori(0, n) as i:
                    yield i

        class Chain:

            def __init__(self, eng, sem):
                self.eng, self.sem, self.n, self.reg, self.per = eng, sem, 0, 0, 0

            def __call__(self, ins):
                self.n += 1
                ins.then_inc(self.sem, 1)
                self.eng.wait_ge(self.sem, self.reg * self.per + self.n if self.per else self.n)

            @contextmanager
            def loop(self, i, n, per):
                start = self.n
                self.reg, self.per = i, per if n > 1 else 0
                yield
                assert self.n - start == per, (self.n - start, per)
                self.n, self.reg, self.per = start + n * per, 0, 0

        def block_end(q, it, b):
            return q.sub0 + it * q.subs + (b + 1) * 2 * q.units

        def cross_units():
            us = []
            for hf in range(NH):
                us.append(dict(hf=hf, L=T, mask=None, scale=XA_D ** -0.5,
                               qk=[[(qTx[:, 4 * h + d, hf * P:hf * P + P], kTx[:, 4 * h + d, :]) for d in range(4)] for h in range(4)],
                               pr=xpr[hf], pT=xpT[hf], coef=None,
                               groups=[dict(kt0=4 * h, hf=hf,
                                            pv=[[(kv[:, m, D + h * XA_D + d * P:D + h * XA_D + d * P + P], xpT[hf][:, m, h, :]) for m in range(2)]
                                                for d in range(4)]) for h in range(4)]))
            return us

        KV0 = 1024

        def nsa_units():
            us = []
            n = 0
            for hf in range(NH):
                for g in range(2):
                    hs = range(4 * g, 4 * g + 4)
                    pts = [pT2[(n + i) % 3] for i in range(3)]
                    nk = hf + 1
                    for br in range(3):
                        q = lambda h: qT2[:, h, hf * P:hf * P + P]
                        if br == 0:
                            us.append(dict(hf=hf, L=CMP_N, mask="cmp", scale=P ** -0.5, qk=[[(q(h), kcT[:, g, :])] for h in hs],
                                           pr=pr2[n % 3], pT=pts[0], coef=(g, 0), groups=[]))
                        else:
                            kk = kT2[:, 2 * (br - 1) + g, 0:nk * P]
                            us.append(dict(hf=hf, L=nk * P, mask="causal", scale=P ** -0.5, qk=[[(q(h), kk)] for h in hs],
                                           pr=pr2[n % 3], pT=pts[br], coef=(g, br), groups=[]))
                        n += 1
                    pv = []
                    for i, h in enumerate(hs):
                        one = [(vc[:, g, :], pts[0][0:CMP_N, 0, i, :])]
                        for br in (1, 2):
                            c = KV0 + 512 * br + 256 + P * g
                            one += [(p2[:, m, c:c + P], pts[br][:, m, i, :]) for m in range(nk)]
                        pv.append(one)
                    us[-1]["groups"] = [dict(kt0=4 * g, hf=hf, pv=pv)]
            return us

        QM0 = NSA_W

        def moba_units():
            us = []
            n = 0
            for hf in range(NH):
                for g in range(2):
                    hs = range(4 * g, 4 * g + 4)
                    nk = hf + 1
                    pt = pT2[n % 3]
                    us.append(dict(hf=hf, L=nk * P, mask="causal", scale=P ** -0.5,
                                   qk=[[(qT2[:, h, hf * P:hf * P + P], kT2[:, h, 0:nk * P])] for h in hs],
                                   pr=pr2[n % 3], pT=pt, coef=None,
                                   groups=[dict(kt0=8 + 4 * g, hf=hf,
                                                pv=[[(p2[:, m, QM0 + 2048 + h * P:QM0 + 2048 + h * P + P], pt[:, m, i, :]) for m in range(nk)]
                                                    for i, h in enumerate(hs)])]))
                    n += 1
            return us

        def group_of(us, i):
            n = 0
            for j, u in enumerate(us):
                n += len(u["groups"])
                if j >= i and u["groups"]:
                    return n
            return n

        def attention_pe(pe, turn, nm_, us):
            pe.wait_ge(*N(nm_, "go", 1))
            ngroup = 0

            def scores(i):
                u = us[i]
                if i >= 2:
                    pe.wait_ge(*N(nm_, "m", i - 1))
                o = GP[:, 2 * (i % 2):2 * (i % 2) + 2, :].rearrange("p a b -> p (a b)")
                for h in range(4):
                    n = len(u["qk"][h])
                    for d, (l, r) in enumerate(u["qk"][h]):
                        m = pe.matmul(o[:, h * T:h * T + u["L"]], l, r, start=(d == 0), stop=(d == n - 1),
                                      skip_group_check=True)
                m.then_inc(N(nm_, "qk")[0], 1)

            def values(i):
                nonlocal ngroup
                for gr in us[i]["groups"]:
                    pe.wait_ge(*N(nm_, "c", i + 1))
                    if ngroup >= 2:
                        pe.wait_ge(*N(nm_, "lo", ngroup - 1))
                    bank = TB[:, 512 * (ngroup % 2):512 * (ngroup % 2) + 512]
                    for j, terms in enumerate(gr["pv"]):
                        for d, (l, r) in enumerate(terms):
                            m = pe.matmul(bank[:, j * P:j * P + P], l, r, start=(d == 0), stop=(d == len(terms) - 1),
                                          skip_group_check=True)
                    m.then_inc(N(nm_, "o")[0], 1)
                    ngroup += 1

            scores(0)
            scores(1)
            for i, u in enumerate(us):
                if i + 2 < len(us):
                    scores(i + 2)
                pe.wait_ge(*N(nm_, "n", i + 1))
                if i:
                    pe.wait_ge(*N(nm_, "c", i))
                for kb in range((u["L"] + P - 1) // P):
                    w = min(P, u["L"])
                    for h in range(4):
                        m = turn(TA[0:w, kb * 512 + h * P:kb * 512 + h * P + P], u["pr"][:, h, kb * P:kb * P + w])
                m.then_inc(N(nm_, "t")[0], 1)
                if i:
                    values(i - 1)
            values(len(us) - 1)

        def attention_act(act, nm_, us):
            ng = 0

            def exps(i):
                u = us[i]
                act.wait_ge(*N(nm_, "m", i + 1))
                for h in range(4):
                    a = u["pr"][:, h, 0:u["L"]]
                    m = nc.scalar.activation(a, a, ACT.Exp, bias=nm[i % 2][:, h:h + 1], scale=u["scale"],
                                             accum_out=sme[i % 2][:, h:h + 1])
                m.then_inc(N(nm_, "e")[0], 1)

            def upper(i):
                nonlocal ng
                for gr in us[i]["groups"]:
                    act.wait_ge(*N(nm_, "o", ng + 1))
                    t = slice(gr["hf"] * P, gr["hf"] * P + P)
                    nc.scalar.copy(hhi[:, gr["kt0"]:gr["kt0"] + 4, t], v(TB, P)[:, 4 * (ng % 2):4 * (ng % 2) + 4, :])\
                        .then_inc(N(nm_, "hi")[0], 1)
                    ng += 1

            exps(0)
            for i, u in enumerate(us):
                if i + 1 < len(us):
                    exps(i + 1)
                act.wait_ge(*N(nm_, "t", i + 1))
                if i >= 3:
                    act.wait_ge(*N(nm_, "o", group_of(us, i - 3)))
                w = min(P, u["L"])
                for kb in range((u["L"] + P - 1) // P):
                    m = nc.scalar.copy(u["pT"][0:w, kb, :, :], v(TA, P)[0:w, 4 * kb:4 * kb + 4, :])
                m.then_inc(N(nm_, "c")[0], 1)
                if i:
                    upper(i - 1)
            upper(len(us) - 1)

        def attention_dve(dve, link, nm_, us):
            ng = 0

            def mask_max(i):
                u = us[i]
                L, hf = u["L"], u["hf"]
                dve.wait_ge(*N(nm_, "qk", i + 1))
                ps = v(GP_flat(i % 2), T)[:, :, 0:L] if L != T else v(GP_flat(i % 2), T)
                pr = u["pr"]
                if i >= 3:
                    dve.wait_ge(*N(nm_, "t", i - 2))
                if u["mask"] is None:
                    link(nc.vector.tensor_copy(pr[:, :, 0:L], ps))
                elif u["mask"] == "cmp":
                    link(nc.vector.tensor_tensor(pr[:, :, 0:L], ps, rows(C("cmp_mask", hf * CMP_N, CMP_N), 4), ALU.add))
                else:
                    if L > P:
                        nc.vector.tensor_copy(pr[:, :, 0:P], ps[:, :, 0:P])
                    link(nc.vector.tensor_tensor(pr[:, :, L - P:L], ps[:, :, L - P:L], rows(C("causal"), 4), ALU.add))
                link(nc.vector.tensor_reduce(mx[i % 2], pr[:, :, 0:L], AX.X, ALU.max))
                nc.vector.tensor_scalar(nm[i % 2], mx[i % 2], -u["scale"], None, ALU.mult).then_inc(N(nm_, "m")[0], 1)

            def normalise(i):
                u = us[i]
                L = u["L"]
                dve.wait_ge(*N(nm_, "e", i + 1))
                r = rc[i % 2]
                link(nc.vector.tensor_scalar(sme[i % 2], sme[i % 2], 1e-30, None, ALU.max))
                link(nc.vector.reciprocal(r, sme[i % 2]))
                if u["coef"] is not None:
                    g, br = u["coef"]
                    gt = gates[:, u["hf"] * 24:u["hf"] * 24 + 24].rearrange("p (h b) -> p h b", b=3)[:, 4 * g:4 * g + 4, br]
                    link(nc.vector.tensor_tensor(r, r, gt, ALU.mult))
                    if br == 0:
                        link(nc.vector.tensor_scalar(r, r, C("cmp_valid", u["hf"], 1), None, ALU.mult))
                nc.vector.tensor_tensor(u["pr"][:, :, 0:L], u["pr"][:, :, 0:L], cols(r, L), ALU.mult).then_inc(N(nm_, "n")[0], 1)

            def lower(i):
                nonlocal ng
                for gr in us[i]["groups"]:
                    dve.wait_ge(*N(nm_, "hi", ng + 1))
                    t = slice(gr["hf"] * P, gr["hf"] * P + P)
                    a = slice(gr["kt0"], gr["kt0"] + 4)
                    nc.vector.tensor_tensor(hlo[:, a, t], v(TB, P)[:, 4 * (ng % 2):4 * (ng % 2) + 4, :],
                                            hhi[:, a, t].bitcast(F32), ALU.subtract).then_inc(N(nm_, "lo")[0], 1)
                    ng += 1

            mask_max(0)
            for i, u in enumerate(us):
                if i + 1 < len(us):
                    mask_max(i + 1)
                normalise(i)
                if i >= 2:
                    lower(i - 2)
            for i in range(len(us) - 2, len(us)):
                lower(i)

        def GP_flat(e):
            class _F:
                def __getitem__(self, k):
                    return GP[:, 2 * e:2 * e + 2, :].rearrange("p a b -> p (a b)")
            return _F()

        def turn_in(pe, turn, nm_, src, c0, _):
            for g in range(4):
                tp = (TA, TB)[g % 2]
                if g >= 2:
                    pe.wait_ge(*N(nm_, "c", g - 1))
                for f in range(4):
                    for h in range(NH):
                        c = c0 + (4 * g + f) * P
                        m = turn(tp[:, f * T + h * P:f * T + h * P + P], src[:, h, c:c + P])
                m.then_inc(N(nm_, "t")[0], 1)

        def turn_in_act(act, nm_, dst):
            for g in range(4):
                act.wait_ge(*N(nm_, "t", g + 1))
                nc.scalar.copy(dst[:, 4 * g:4 * g + 4, :], v((TA, TB)[g % 2], T)).then_inc(N(nm_, "c")[0], 1)

        def columns2(nm_):
            if nm_ == "n2":
                return [(qT2, 0, [0, 128, 256, 384]), (qT2, 4, [512, 640, 768, 896]),
                        (kT2, 0, [KV0 + 512, KV0 + 640, KV0 + 1024, KV0 + 1152])]
            return [(qT2, 0, [QM0 + P * i for i in range(4)]), (qT2, 4, [QM0 + P * i for i in range(4, 8)]),
                    (kT2, 0, [QM0 + 1024 + P * i for i in range(4)]), (kT2, 4, [QM0 + 1024 + P * i for i in range(4, 8)])]

        def turn_in2(pe, turn, nm_):
            for g, (_, _, cs) in enumerate(columns2(nm_)):
                tp = (TA, TB)[g % 2]
                if g >= 2:
                    pe.wait_ge(*N(nm_, "c", g - 1))
                elif nm_ == "m2":
                    pe.wait_ge(*N("natt", "lo", 4))
                    pe.wait_ge(*N("natt", "c", 12))
                for f, c in enumerate(cs):
                    for h in range(NH):
                        m = turn(tp[:, f * T + h * P:f * T + h * P + P], p2[:, h, c:c + P])
                m.then_inc(N(nm_, "t")[0], 1)

        def turn_in2_act(act, nm_):
            for g, (dst, a, _) in enumerate(columns2(nm_)):
                act.wait_ge(*N(nm_, "t", g + 1))
                m = nc.scalar.copy(dst[:, a:a + 4, :], v((TA, TB)[g % 2], T)).then_inc(N(nm_, "c")[0], 1)

        xn_of = {"mix": xn, "mem": xn, "xa": None, "ffn": xn, "pre2": xn_f, "pf2": None}
        ar = Arena(); ar.at = arena0 + 4 * NH * 2 * D
        ar.at += 4 * KT * T
        xn_of["xa"] = ar("xn_xa", [P, NH, D])
        ar = Arena(); ar.at = arena0 + 4 * NH * D
        xn_of["pf2"] = ar("xn_pf2", [P, NH, D])

        def wsrc(w, col, width, k0=0, u=0):
            return w.rearrange("(u k p) n -> p u k n", k=UK, p=P)[:, k0 + u, :, bass.ds(col, width)]

        def unit_source(q, it, b, u):
            n = q.name
            if n == "w_in":
                return wsrc(A["w_in"], (2 * it + b) * 428, 428, 0, u)
            if n == "w_in2a":
                return wsrc(A["w_in_2"], (2 * it + b) * W2A, W2A, 0, u)
            if n in ("w_in2b", "w_in2c"):
                return wsrc(A["w_in_2"], NSA_W + (2 * it + b) * 512 + (2048 if n == "w_in2c" else 0), 512, 0, u)
            if n in ("w_oa", "w_ob"):
                return wsrc(A["w_o_2"], b * 512 + (1024 if n == "w_ob" else 0), 512, 0, u)
            if n in ("mix_out", "xkv", "xq", "xo"):
                w = A[{"mix_out": "w_mix_out", "xkv": "w_xkv", "xq": "w_xq", "xo": "w_xo"}[n]]
                return wsrc(w, (2 * it + b) * 512, 512, 0, u)
            if n in ("ffn1a", "ffn1b"):
                return wsrc(A["w_gate" if b == 0 else "w_up"], (it + (6 if n == "ffn1b" else 0)) * 512, 512, 0, u)
            if n in ("down1a", "down1b"):
                return wsrc(A["w_down"], (q.nb * it + b) * 512, 512, 6 if n == "down1b" else 0, u)
            if n.startswith("up2"):
                return wsrc(A["w_up_2"], (2 * it + b) * 512 + 2048 * int(n[3:]), 512, 0, u)
            return wsrc(A["w_down_2"], (2 * it + b) * 512, 512, 4 * int(n[5:]), u)

        @block.sync
        def _(sp):
            def iteration(q, it, last_cols=False):
                for j, (kind, b, u) in enumerate(q.seq):
                    sp.wait_ge(S("unit_used"), (it * len(q.seq) + (q.unit0 + j - NSLOT + 1)) * 2 + CREDIT)
                    if kind == "a":
                        src = wsrc(A["w_ada_2"], (it + q.ada0) * 512, 512, 0, u)
                        dst = raw[j % NSLOT][:, :, :]
                    elif last_cols and b == 1:
                        src = wsrc(A["w_in_2"], NSA_W - W2A, W2A, 0, u)
                        dst = raw[j % NSLOT][:, :, 0:W2A]
                    else:
                        src = unit_source(q, it, b, u)
                        dst = raw[j % NSLOT][:, :, 0:q.width]
                    sp.dma_start(dst, src).then_inc(S(f"raw_in{j % NSLOT}"), 16)

            for q in order:
                n = q.n - 1 if q.name == "w_in2a" else q.n
                with loop(sp, n) as it:
                    iteration(q, it)
                if q.name == "w_in2a":
                    iteration(q, n, True)

        @block.gpsimd
        def _(g):
            link = Chain(g, S("pool_step"))

            def rope(c0, n, h):
                xx = p2[:, h, c0:c0 + n * P].rearrange("p (a b) -> p a b", b=P)
                x1, x2 = xx[:, :, 0:64], xx[:, :, 64:P]
                cs, sn = rows(C("cos", 64 * h, 64), n), rows(C("sin", 64 * h, 64), n)
                g.tensor_tensor(rp[0][:, 0:n, :], x1, cs, ALU.mult)
                g.tensor_tensor(rp[1][:, 0:n, :], x2, sn, ALU.mult)
                g.tensor_tensor(rp[2][:, 0:n, :], x1, sn, ALU.mult)
                link(g.tensor_tensor(rp[3][:, 0:n, :], x2, cs, ALU.mult))
                g.tensor_tensor(x1, rp[0][:, 0:n, :], rp[1][:, 0:n, :], ALU.subtract)
                link(g.tensor_tensor(x2, rp[3][:, 0:n, :], rp[2][:, 0:n, :], ALU.add))

            for h in range(NH):
                g.dma_start(x[:, h, :], A["x"][0, h * P:(h + 1) * P, :]).then_inc(S(f"x_in{h}"), 16)
            g.dma_start(gains[:, 0, :], A["mix_norm_g"]).then_inc(S("gain_in"), 16)
            g.dma_start(cst[:, :], A["const"]).then_inc(S("cst_in"), 16)
            loads = [(gains[:, 1, :], "xa_norm_g"), (gains[:, 2, :], "mem_norm_g"),
                     (gains[:, 3, :], "ffn_norm_g"), (gains[:, 4, :], "pre_norm_mix_2"), (gains[:, 5, :], "pre_norm_ffn_2"),
                     (conv_w[:, :, :], "dn_conv_w"), (pool_s[:, :], "pool_scale"), (b_ada[:, :], "b_ada_2"),
                     (cvec[:, :], "c_2"), (post_gain[:, 0, :], "post_norm_mix_2"), (post_gain[:, 1, :], "post_norm_ffn_2"),
                     (ffn_w[:, :].rearrange("p (c j) -> p c j", j=4)[:, :, 3:4], "ffn_conv_b")]
            with nc.allow_non_contiguous_dma(reason="per-channel constants"):
                for dst, name in loads:
                    g.dma_start(dst, A[name]).then_inc(S("tab_in"), 16)
                for j in range(3):
                    g.dma_start(ffn_w[:, :].rearrange("p (c j) -> p c j", j=4)[:, :, j:j + 1],
                                A["ffn_conv_w"][:, j, :, :]).then_inc(S("tab_in"), 16)
                g.dma_start(dtb, A["dn_dt_bias"].partition_broadcast(P)).then_inc(S("tab_in"), 16)
                g.dma_start(ea, A["dn_a_log"].partition_broadcast(P)).then_inc(S("tab_in"), 16)
                g.dma_start(ngb[:, :], A["dn_norm_g"].partition_broadcast(P)).then_inc(S("tab_in"), 16)
            g.wait_ge(*N("mix", "lo", 8))
            g.dma_start(pmat[:, :, :, :].rearrange("p a b c -> p (a b c)"), A["pool_mats"]).then_inc(S("pool_in"), 16)
            g.dma_start(wpool[:, :, :, :], A["w_pool"]).then_inc(S("pool_in"), 16)
            for n in range(6):
                g.wait_ge(S("cv_s"), n + 1)
                cb = cbuf[n % 3][:, :, :]
                g.tensor_tensor(cb, cb, csg[:, :, :], ALU.mult).then_inc(S("cv_m"), 1)
            for hf in range(NH):
                k3, v3, z3 = (p1[:, hf, POOL_W + c:POOL_W + c + 1024].rearrange("p (a b) -> p a b", b=P) for c in (1024, 2048, 3072))

                def joined(e, level):
                    a = slice(4 * e, 4 * e + 4)
                    g.tensor_tensor(MT[:, a, :], LT[:, a, :], rows(level, 4), ALU.mult).then_inc(S(f"lv_m{e}"), 1)
                g.wait_ge(S("dn_lt"), hf + 1)
                for e in range(2):
                    joined(e, C("levels", 0, P))
                g.wait_ge(S("dn_at_mm"), hf + 1)
                g.tensor_tensor(k3, k3, cols(ex[:, 8:16], P), ALU.mult)
                g.tensor_tensor(v3, v3, cols(beta[:, hf * 8:hf * 8 + 8], P), ALU.mult)
                g.tensor_tensor(KB[:, :, :], KB[:, :, :], cols(ex[:, 0:8], P), ALU.mult).then_inc(S("dn_mul"), 1)
                for lv in range(1, 6):
                    for e in range(2):
                        g.wait_ge(*((S(f"lv_u{e}"), 6 * hf + 1) if lv == 1 else (S(f"lv_y{e}"), 5 * hf + lv - 1)))
                        joined(e, C("levels", lv * P, P))
                g.wait_ge(S("dn_zs"), hf + 1)
                g.tensor_tensor(z3, z3, LT[:, :, :], ALU.mult).then_inc(S("dn_z1"), 1)
                g.wait_ge(S("dn_z1"), hf + 1)
                g.tensor_tensor(z3, z3, rows(ngb[:, :], 8), ALU.mult).then_inc(S("dn_z"), 1)
            g.wait_ge(S("dn_lo"), 2)
            g.dma_start(memt[:, :, :], A["mem"].rearrange("b (h p) d -> p (b h) d", p=P)).then_inc(S("mem_in"), 16)
            for e in range(2):
                g.wait_ge(S(f"evac{e}"), 1 + PH["down1b"].ev1)
            g.wait_ge(S("f1_lo"), 12)
            g.dma_start(fgb[:, :], A["final_norm_g"].partition_broadcast(P)).then_inc(S("fgb_in"), 16)
            for j, w in enumerate(("cmp_k_w1_2", "cmp_v_w1_2")):
                if j == 0:
                    g.wait_ge(*N("pre2", "lo", 8))
                    for dst, name in ((posT[:, 0, :], "cmp_k_pos_2"), (posT[:, 1, :], "cmp_v_pos_2"),
                                      (w2c[:, 0, :], "cmp_k_w2_2"), (w2c[:, 1, :], "cmp_v_w2_2")):
                        g.dma_start(dst, A[name]).then_inc(S("cmp_in"), 16)
                else:
                    for n, (phase, its, parts) in enumerate((("w_in2a", 3, [(KV0, 2)]),
                                                             ("w_in2a", 3, [(KV0 + 512, 2), (KV0 + 1024, 2), (0, 8)]),
                                                             ("w_in2b", 1, [(QM0, 8)]), ("w_in2b", 2, [(QM0 + 1024, 8)]))):
                        for e in range(2):
                            g.wait_ge(S(f"evac{e}"), 1 + PH[phase].ev0 + its)
                        for c0, heads in parts:
                            for h in range(NH):
                                rope(c0, heads, h)
                        g.sem_inc(S("rope_done"), 1)
                    g.wait_ge(S("cmp_hid"), 1)
                g.dma_start(w1c[:, :, :], A[w]).then_inc(S("w1_in"), 16)
            for h in range(NH):
                g.wait_ge(S("y_done"), h + 1)
                g.dma_start(out[0, h * P:(h + 1) * P, :], x[:, h, :]).then_inc(S("out_done"), 16)
            g.wait_ge(S("out_done"), 32)

        @block.tensor
        def _(pe):
            def turn(dst, src, n=P):
                return pe.transpose(dst, src, ident[0:n, 0:n] if n != P else ident)

            def product(q, ahi, alo, ready, mid=None, end=None, first=None, points={}):
                def iteration(it, late):
                    for b in range(q.nb):
                        pe.wait_ge(S(f"evac{b % 2}"), it * (q.nb // 2) + (q.ev0 + b // 2 + 1))
                        for u in range(q.units):
                            if b == 0:
                                pe.wait_ge(*ready(u))
                            for s in range(2):
                                pos = [i for i, z in enumerate(q.seq) if z == ("g", b, u)][0]
                                pe.wait_ge(S("unit_used"), it * (2 * len(q.seq)) + 2 * (q.unit0 + pos) + s + 1 + CREDIT)
                                r = ((b * q.units + u) * 2 + s) % NRING
                                for k in range(2):
                                    kt = u * UK + 2 * s + k
                                    first, last = kt == 0, kt == q.units * UK - 1
                                    for h in range(NH):
                                        t = slice(h * P, h * P + P)
                                        o = GP[:, 2 * (b % 2) + h, 0:q.width]
                                        pe.matmul(o, ahi[:, kt, t], whi[r][:, k, 0:q.width], start=first, stop=False)
                                        pe.matmul(o, ahi[:, kt, t], wlo[r][:, k, 0:q.width], start=False, stop=False)
                                        m = pe.matmul(o, alo[:, kt, t], whi[r][:, k, 0:q.width], start=False, stop=last)
                                m.then_inc(S("mm_done"), 1)
                            if mid and b % 2 == 1 and u == 1:
                                mid(it)
                            if late and b == 0 and u == 0:
                                late()
                            if (b, u) in points:
                                points[b, u]()
                            if isinstance(it, int) and (it, b, u) in points:
                                points[it, b, u]()
                    if q.ada:
                        pe.wait_ge(S("unit_used"), it * (2 * len(q.seq)) + 2 * (q.unit0 + len(q.seq)) + CREDIT)
                        pe.wait_ge(S("ada_read"), it + (q.ada0 + 1))
                        for j in range(4):
                            m = pe.matmul(TB[:, 512 + j:513 + j], ada_acc[:, j * P:(j + 1) * P], C("ones", 0, 1),
                                          start=True, stop=True)
                        m.then_inc(S("ada_sum"), 1)

                if end or first:
                    iteration(0, first)
                    if q.n > 1:
                        with loop(pe, q.n - 1) as i:
                            iteration(i + 1, (lambda: end(i)) if end else None)
                    return (lambda: end(q.n - 1)) if end else None
                with loop(pe, q.n) as it:
                    iteration(it, None)

            def norm(nm_):
                for q in range(4):
                    for h in range(NH):
                        g = q * NH + h
                        pe.wait_ge(*N(nm_, "xn", h + 1))
                        if g >= 5:
                            pe.wait_ge(*N(nm_, "f", g - 4))
                        bank = norm_banks[g % 5]
                        for k in range(4):
                            m = turn(bank[:, k * P:(k + 1) * P], xn_of[nm_][:, h, (4 * q + k) * P:(4 * q + k + 1) * P])
                        m.then_inc(N(nm_, "t")[0], 1)

            pe.wait_ge(S("cst_in"), 16)
            norm("mix")
            product(PH["w_in"], hhi, hlo, lambda u: N("mix", "lo", 2 * u + 2))

            for e in range(2):
                pe.wait_ge(S(f"evac{e}"), 1 + PH["w_in"].ev1)
            pe.wait_ge(S("pool_in"), 32)
            pe.wait_ge(S("ada_read"), 1 + PH["w_in"].ada1)
            for i in range(4):
                if i:
                    pe.wait_ge(S("pool_mix"), i)
                for f in range(2):
                    for h in range(NH):
                        c = i * 256 + f * P
                        m = pe.matmul(TA[:, f * T:(f + 1) * T], p1[:, h, c:c + P], pmat[:, i, h, :],
                                      start=(h == 0), stop=(h == 1), skip_group_check=True)
                m.then_inc(S("pool_m"), 1)
                pe.wait_ge(S("pool_mix"), i + 1)
                if i:
                    pe.wait_ge(S("pool_f"), i)
                for f in range(2):
                    for k in range(2):
                        m = pe.matmul(TB[:, f * T:(f + 1) * T], wpool[:, i, k, f * P:(f + 1) * P], mixT[:, k, :],
                                      start=(k == 0), stop=(k == 1), skip_group_check=True)
                m.then_inc(S("pool_y"), 1)

            pe.wait_ge(S("pool_f"), 4)
            for g in range(8):
                if g < 6:
                    if g >= 2:
                        pe.wait_ge(S("cv_c"), g - 1)
                    src = v(GP_flat(g % 2), T)
                    for f in range(4):
                        for h in range(NH):
                            c = POOL_W + 512 * g + P * f
                            m = turn(src[:, f, h * P:h * P + P], p1[:, h, c:c + P])
                    m.then_inc(S("cv_t"), 1)
                if g >= 2:
                    pe.wait_ge(S("cv_m"), g - 1)
                    if g >= 3:
                        pe.wait_ge(S("cv_e"), g - 2)
                    for h in range(NH):
                        for f in range(4):
                            m = turn(TB[:, h * 512 + f * P:h * 512 + f * P + P], cbuf[(g - 2) % 3][:, f, h * P:h * P + P])
                    m.then_inc(S("cv_b"), 1)

            A8, B8 = v(TA, P), v(TB, P)
            for hf in range(NH):
                q3 = p1[:, hf, POOL_W:POOL_W + 1024].rearrange("p (a b) -> p a b", b=P)
                k3 = p1[:, hf, POOL_W + 1024:POOL_W + 2048].rearrange("p (a b) -> p a b", b=P)
                v3 = p1[:, hf, POOL_W + 2048:POOL_W + 3072].rearrange("p (a b) -> p a b", b=P)
                gd = gdec[:, hf * 8:hf * 8 + 8]
                pe.wait_ge(S("gp_g"), 1)
                pe.wait_ge(S("cv_e"), 6)
                if hf:
                    pe.wait_ge(S("dn_lo"), 1)
                for j, m_ in enumerate(("upto", "after", "chunk0", "chunk1")):
                    m = pe.matmul(TA[:, 8 * j:8 * j + 8], C(m_), gd, start=True, stop=True)
                m.then_inc(S("dn_sum"), 1)
                pe.wait_ge(S("dn_tg"), hf + 1)
                for b in range(2):
                    pe.matmul(TB[:, 512 * b:512 * b + 512], C("ones"), KB[:, 4 * b:4 * b + 4, :].rearrange("p a b -> p (a b)"),
                              start=True, stop=False, skip_group_check=True)
                    for h in range(4 * b, 4 * b + 4):
                        m = pe.matmul(B8[:, h, :], KB[:, h, :], C("negones"), start=False, stop=(h % 4 == 3),
                                      skip_group_check=True)
                m.then_inc(S("dn_diff"), 1)
                pe.wait_ge(S("dn_ex"), hf + 1)
                pe.wait_ge(S("dn_kb"), hf + 1)
                for h in range(8):
                    m = turn(A8[:, h, :], k3[:, h, :])
                m.then_inc(S("dn_t"), 1)
                pe.wait_ge(S("dn_dm"), hf + 1)
                for h in range(8):
                    m = turn(B8[:, h, :], KB[:, h, :])
                m.then_inc(S("dn_t"), 1)
                pe.wait_ge(S("dn_tc"), 4 * hf + 1)
                for h in range(8):
                    m = turn(A8[:, h, :], q3[:, h, :])
                m.then_inc(S("dn_t"), 1)
                pe.wait_ge(S("dn_tc"), 4 * hf + 2)
                for h in range(8):
                    m = pe.matmul(B8[:, h, :], KTt[:, h, :], KBT[:, h, :], start=True, stop=True)
                m.then_inc(S("dn_lt_mm"), 1)
                pe.wait_ge(S("dn_tc"), 4 * hf + 3)
                for h in range(8):
                    m = pe.matmul(A8[:, h, :], KTt[:, h, :], QT[:, h, :], start=True, stop=True)
                m.then_inc(S("dn_at_mm"), 1)
                pe.wait_ge(S("dn_lt"), hf + 1)
                pe.wait_ge(S("dn_qd"), hf + 1)
                for h in range(8):
                    m = turn(B8[:, h, :], q3[:, h, :])
                m.then_inc(S("dn_t"), 1)
                pe.wait_ge(S("dn_at"), hf + 1)
                pe.wait_ge(S("dn_tc"), 4 * hf + 4)
                for e in range(2):
                    pe.wait_ge(S(f"lv_m{e}"), 6 * hf + 1)
                    for h in range(4 * e, 4 * e + 4):
                        m = turn(B8[:, h, :], MT[:, h, :])
                    m.then_inc(S(f"lv_z{e}"), 1)

                def level(lv, both):
                    for e in range(2):
                        pe.wait_ge(S(f"lv_m{e}"), lv + (6 * hf + 2))
                        pe.wait_ge(S(f"lv_u{e}"), lv + (6 * hf + 1))
                        for h in range(4 * e, 4 * e + 4):
                            m = pe.matmul(A8[:, h, :], MT[:, h, :], TT[:, h, :], start=True, stop=True)
                        m.then_inc(S(f"lv_y{e}"), 1)
                    for e in range(2):
                        pe.wait_ge(S(f"lv_yc{e}"), lv + (5 * hf + 1))
                        if both:
                            for h in range(4 * e, 4 * e + 4):
                                pe.matmul(B8[:, h, :], AA[:, h, :], YY[:, h, :], start=True, stop=True)
                        for h in range(4 * e, 4 * e + 4):
                            m = pe.matmul(A8[:, h, :], YY[:, h, :], AA[:, h, :], start=True, stop=True)
                        m.then_inc(S(f"lv_z{e}"), 1)

                with loop(pe, 4) as lv:
                    level(lv, True)
                level(4, False)
                for e in range(2):
                    pe.wait_ge(S(f"lv_u{e}"), 6 * hf + 6)
                pe.wait_ge(S("dn_mul"), hf + 1)
                for h in range(8):
                    pe.matmul(A8[:, h, :], AA[:, h, :], v3[:, h, :], start=True, stop=True)
                for h in range(8):
                    m = pe.matmul(B8[:, h, :], KB[:, h, :], AA[:, h, :], start=True, stop=True)
                m.then_inc(S("dn_uw"), 1)
                pe.wait_ge(S("dn_uwc"), hf + 1)
                for c in range(2):
                    r = slice(64 * c, 64 * c + 64)
                    n = 2 * hf + c
                    pe.wait_ge(S("sc_u"), n + 1)
                    for h in range(8):
                        m = pe.matmul(A8[r, h, :], KBT[:, h, r], ST[:, h, :], start=True, stop=True)
                    m.then_inc(S("sc_w"), 1)
                    pe.wait_ge(S("sc_v"), n + 1)
                    for h in range(8):
                        pe.matmul(B8[r, h, :], QT[:, h, r], ST[:, h, :], start=True, stop=False, skip_group_check=True)
                        m = pe.matmul(B8[r, h, :], DT[r, h, r], YY[r, h, :], start=False, stop=True, skip_group_check=True)
                    if n < 3:
                        for h in range(8):
                            m = pe.matmul(A8[:, h, :], k3[r, h, :], YY[r, h, :], start=True, stop=True)
                    m.then_inc(S("sc_s"), 1)
                if hf == 0:
                    pe.wait_ge(S("sc_u"), 3)
                pe.wait_ge(S("dn_y"), hf + 1)
                for h in range(8):
                    m = turn(A8[:, h, :], MT[:, h, :])
                m.then_inc(S("dn_yt"), 1)

            pe.wait_ge(S("pool_lo"), 4)
            product(PH["mix_out"], hhi, hlo, lambda u: (S("dn_lo"), 2))
            pe.wait_ge(S("evac1"), 1 + PH["mix_out"].ev1)
            norm("mem")
            product(PH["xkv"], hhi, hlo, lambda u: N("mem", "lo", 2 * u + 2))
            for e in range(2):
                pe.wait_ge(S(f"evac{e}"), 1 + PH["xkv"].ev1)
            pe.wait_ge(S("ada_read"), 1 + PH["xkv"].ada1)
            turn_in(pe, turn, "kx", kv, 0, 0)
            norm("xa")
            product(PH["xq"], hhi, hlo, lambda u: N("xa", "lo", 2 * u + 2))
            for e in range(2):
                pe.wait_ge(S(f"evac{e}"), 1 + PH["xq"].ev1)
            pe.wait_ge(S("ada_read"), 1 + PH["xq"].ada1)
            turn_in(pe, turn, "qx", kv, 0, 0)
            attention_pe(pe, turn, "xatt", cross_units())
            product(PH["xo"], hhi, hlo, lambda u: N("xatt", "lo", 8))
            norm("ffn")

            def ffn1_mid(base):
                def f(it):
                    pe.wait_ge(S("evac0"), it + base[0] + 2)
                    pe.wait_ge(S("f1_conv"), it + base[1] + 1)
                    for f_ in range(4):
                        for h in range(NH):
                            m = turn(TA[:, f_ * T + h * P:f_ * T + h * P + P], tok[0][:, h, f_ * P:f_ * P + P])
                    m.then_inc(S("f1_tg"), 1)
                return f

            def ffn1_end(base):
                def f(it):
                    pe.wait_ge(S("evac1"), it + base[0] + 2)
                    pe.wait_ge(S("f1_f"), it + base[1] + 1)
                    for f_ in range(4):
                        for h in range(NH):
                            m = turn(TB[:, f_ * T + h * P:f_ * T + h * P + P], tok[1][:, h, f_ * P:f_ * P + P])
                    m.then_inc(S("f1_tu"), 1)
                return f

            ba, bb = (PH["ffn1a"].ev0, 0), (PH["ffn1b"].ev0, 6)
            rest = product(PH["ffn1a"], hhi, hlo, lambda u: N("ffn", "lo", 2 * u + 2), ffn1_mid(ba), ffn1_end(ba))
            product(PH["down1a"], fhi, flo, lambda u: (S("f1_lo"), u + 2), first=rest)
            rest = product(PH["ffn1b"], hhi, hlo, lambda u: N("ffn", "lo", 8), ffn1_mid(bb), ffn1_end(bb))
            product(PH["down1b"], fhi, flo, lambda u: (S("f1_lo"), 6 + u + 2), first=rest)
            norm("pre2")
            product(PH["w_in2a"], hhi, hlo, lambda u: N("pre2", "lo", 2 * u + 2))
            product(PH["w_in2b"], hhi, hlo, lambda u: N("pre2", "lo", 8))

            def cmp_turn(j):
                if j == 0:
                    pe.wait_ge(S("rope_done"), 1)
                else:
                    pe.wait_ge(S("cmp_kt"), 1)
                for g in range(2):
                    for h in range(NH):
                        c = 1024 + 256 * j + P * g
                        m = turn(TA[:, g * T + h * P:g * T + h * P + P], p2[:, h, c:c + P])
                m.then_inc(S("cmp_t"), 1)

            def cmp_first(j):
                pe.wait_ge(S("cmp_r"), j + 1)
                pe.wait_ge(S("w1_in"), 16 * (j + 1))
                pe.wait_ge(S("cmp_in"), 64)
                for l in range(32):
                    m = pe.matmul(TA[:, 512:543], w1c[:, l, :], rc1[:, l, :], start=(l == 0), stop=(l == 31))
                m.then_inc(S("cmp_hid"), 1)

            def cmp_second(j):
                pe.wait_ge(S("cmp_s"), j + 1)
                if j:
                    pe.wait_ge(S("cmp_oc"), 1)
                if j == 0:
                    m = pe.matmul(TB[:, 0:30], w2c[:, 0, :], hid[:, 0:30], start=True, stop=True)
                else:
                    for g in range(2):
                        m = pe.matmul(TB[0:CMP_N, g * P:g * P + P], hid[:, 15 * g:15 * g + 15], w2c[:, 1, :],
                                      start=True, stop=True)
                m.then_inc(S("cmp_o"), 1)

            product(PH["w_in2c"], hhi, hlo, lambda u: N("pre2", "lo", 8),
                    points={(0, 0): lambda: cmp_turn(0), (0, 1): lambda: cmp_first(0),
                            (0, 2): lambda: (cmp_second(0), cmp_turn(1)),
                            (1, 1): lambda: cmp_first(1), (1, 2): lambda: cmp_second(1)})
            for e in range(2):
                pe.wait_ge(S(f"evac{e}"), 1 + PH["w_in2c"].ev1)
            pe.wait_ge(S("ada_read"), 1 + PH["w_in2c"].ada1)
            pe.wait_ge(S("cmp_oc"), 2)
            pe.wait_ge(S("rope_done"), 4)
            turn_in2(pe, turn, "n2")
            attention_pe(pe, turn, "natt", nsa_units())
            turn_in2(pe, turn, "m2")
            attention_pe(pe, turn, "matt", moba_units())
            pe.wait_ge(*N("natt", "lo", 4))
            product(PH["w_oa"], hhi, hlo, lambda u: N("matt", "lo", 4))

            def gate_row(n, i):
                pe.wait_ge(S("dg_done"), 4 * n + i + 1)
                bank = (TA[:, 0:512], TA[:, 512:1024])[i % 2]
                pe.matmul(bank, C("ones"), dg[n][:, :, :].rearrange("p a b -> p (a b)"), start=True, stop=True)\
                    .then_inc(S("gate_mm"), 1)
            product(PH["w_ob"], hhi, hlo, lambda u: N("matt", "lo", 4),
                    points={divmod(i + 1, 4): lambda i=i: gate_row(0, i) for i in range(4)})
            norm("pf2")

            def up2_turn(s, e):
                q = PH[f"up2{s}"]

                def f(it):
                    pe.wait_ge(S(f"evac{e}"), it + q.ev0 + 2)
                    pe.wait_ge(S(f"f2_q{e}"), it + 2 * s + 1)
                    tp = (TA, TB)[e]
                    for f_ in range(4):
                        for h in range(NH):
                            m = turn(tp[:, f_ * T + h * P:f_ * T + h * P + P], tok2[e][:, h, f_ * P:f_ * P + P])
                    m.then_inc(S(f"f2_t{e}"), 1)
                return f
            for s in range(4):
                rest = product(PH[f"up2{s}"], hhi, hlo, lambda u: N("pf2", "lo", 2 * u + 2), up2_turn(s, 0), up2_turn(s, 1))
                product(PH[f"down2{s}"], f2hi, f2lo, lambda u: (S("f2_lo"), 4 * s + u + 3), first=rest,
                        points={(1, *divmod(i + 1, 4)): lambda i=i: gate_row(1, i) for i in range(4)} if s == 3 else {})

        @block.scalar
        def _(act):
            def split_hi(q, it, j):
                kind, b, u = q.seq[j]
                if kind == "a":
                    return
                act.wait_ge(S(f"raw_in{j % NSLOT}"), 16 * (it * (len(q.seq) // NSLOT) + q.unit0 // NSLOT + j // NSLOT + 1))
                g = b * q.units + u
                for s in range(2):
                    act.wait_ge(S("mm_done"), it * q.subs + (q.sub0 + 2 * g + s - NRING + 1) + NRING)
                    nc.scalar.copy(whi[(2 * g + s) % NRING][:, :, 0:q.width], raw[j % NSLOT][:, 2 * s:2 * s + 2, 0:q.width])\
                        .then_inc(S("hi_done"), 1)

            def body(q, it, nxt, hooks):
                g = 0
                for j, (kind, b, u) in enumerate(q.seq):
                    if j < LEAD:
                        g += 1
                        continue
                    split_hi(q, it, j)
                    if kind == "g":
                        g += 1
                        for f in hooks.get(g, ()):
                            f(it)
                for j in range(LEAD):
                    if nxt is not None:
                        split_hi(*nxt, j)
                    for f in hooks.get(g + j + 1, ()):
                        f(it)

            def phase(q, hooks, peel=False, last={}):
                i0 = order.index(q)
                nq = order[i0 + 1] if i0 + 1 < len(order) else None
                same = nq is not None and nq.width == q.width and not peel and len(nq.seq) // NSLOT >= 1
                m = q.n if same else q.n - 1
                if m:
                    with loop(act, m) as it:
                        body(q, it, (q, it + 1), hooks)
                if not same:
                    both = {at: hooks.get(at, []) + last.get(at, []) for at in hooks.keys() | last.keys()}
                    body(q, q.n - 1, (nq, 0) if nq is not None else None, both)

            def store(q, dst, base=0, lastcol=None):
                def hook(b):
                    def f(it):
                        e = b % 2
                        act.wait_ge(S("mm_done"), block_end(q, it, b) + NRING)
                        col = (q.nb * it + b) * q.width + base
                        if lastcol is not None and isinstance(it, int) and it == q.n - 1 and b == q.nb - 1:
                            col = lastcol
                        nc.scalar.copy(dst[:, :, bass.ds(col, q.width)], GP[:, 2 * e:2 * e + 2, 0:q.width])\
                            .then_inc(S(f"evac{e}"), 1)
                    return f
                return {(b + 1) * q.units + LEAD: [hook(b)] for b in range(q.nb)}

            def root_mean(nm_, X, ready, dst):
                for h in range(NH):
                    for w in ready[h]:
                        act.wait_ge(*w)
                    nc.scalar.activation(dst(h), X[:, h, :], ACT.Square, accum_out=ss[:, h:h + 1]).then_inc(N(nm_, "ss")[0], 1)
                    act.wait_ge(*N(nm_, "ms", h + 1))
                    nc.scalar.activation(rt[:, h:h + 1], ms[:, h:h + 1], ACT.Sqrt).then_inc(N(nm_, "rt")[0], 1)

            def evacuated(name):
                return [[(S("evac0"), 1 + PH[name].ev1), (S("evac1"), 1 + PH[name].ev1)], []]

            def norm(nm_, X, ready, between=None):
                root_mean(nm_, X, ready, lambda h: xn_of[nm_][:, h, :])
                if between:
                    between()
                for g in range(8):
                    q, h = divmod(g, NH)
                    act.wait_ge(*N(nm_, "f", g + 1))
                    nc.scalar.copy(hhi[:, 4 * q:4 * q + 4, h * P:h * P + P], fbx[g % 2].rearrange("p (a b) -> p a b", b=P))\
                        .then_inc(N(nm_, "hi")[0], 1)

            norm("mix", x, [[(S("x_in0"), 16)], [(S("x_in1"), 16)]], lambda: [split_hi(order[0], 0, j) for j in range(LEAD)])
            act.wait_ge(S("tab_in"), 16 * TABS)
            nc.scalar.activation(csig[:, :], cvec[:, :], ACT.Sigmoid).then_inc(S("csig"), 1)
            phase(PH["w_in"], store(PH["w_in"], p1))

            for e in range(2):
                act.wait_ge(S(f"evac{e}"), 1 + PH["w_in"].ev1)
            bl = p1[:, :, IN_W - 16:IN_W - 8]
            nc.scalar.activation(beta.rearrange("p (a b) -> p a b", b=8), bl, ACT.Sigmoid).then_inc(S("gp_b"), 1)
            act.wait_ge(S("gp_ax"), 1)
            nc.scalar.activation(zc, zb, ACT.Exp, scale=-1.0)
            nc.scalar.activation(ea, ea, ACT.Exp).then_inc(S("gp_e"), 1)

            for i in range(4):
                act.wait_ge(S("pool_m"), i + 1)
                if i:
                    act.wait_ge(S("pool_y"), i)
                nc.scalar.copy(mixT[:, :, :], v(TA, T)[:, 0:2, :]).then_inc(S("pool_mix"), 1)
                act.wait_ge(S("pool_f"), i + 1)
                nc.scalar.copy(hhi[:, 2 * i:2 * i + 2, :], fpool[:, :, :]).then_inc(S("pool_hi"), 1)

            def tap(g):
                act.wait_ge(S("cv_t"), g + 1)
                if g >= 3:
                    act.wait_ge(S("cv_b"), g - 2)
                for f in range(4):
                    m = nc.scalar.activation(cbuf[g % 3][:, f, :], v(GP_flat(g % 2), T)[:, f, :], ACT.Copy, scale=conv_w[:, 4 * g + f, 3:4])
                m.then_inc(S("cv_a"), 1)
            act.wait_ge(S("pool_lo"), 4)
            tap(0)
            tap(1)
            for g in range(6):
                act.wait_ge(S("cv_c"), g + 1)
                if g:
                    act.wait_ge(S("cv_m"), g)
                nc.scalar.activation(csg[:, :, :], cbuf[g % 3][:, :, :], ACT.Sigmoid).then_inc(S("cv_s"), 1)
                if g < 4:
                    tap(g + 2)
                for n in ([g - 1] if g else []) + ([g] if g == 5 else []):
                    act.wait_ge(S("cv_b"), n + 1)
                    c = POOL_W + 512 * n
                    nc.scalar.copy(p1[:, :, c:c + 512], v(TB, 512)).then_inc(S("cv_e"), 1)

            A8, B8 = v(TA, P), v(TB, P)
            for hf in range(NH):
                if hf == 0:
                    act.wait_ge(S("dn_ms"), 1)
                    nc.scalar.activation(r16, m16, ACT.Sqrt).then_inc(S("dn_rt"), 1)
                act.wait_ge(S("dn_sum"), hf + 1)
                nc.scalar.activation(ex, TA[:, 0:32], ACT.Exp).then_inc(S("dn_ex"), 1)
                act.wait_ge(S("dn_dm"), hf + 1)
                nc.scalar.activation(DT[:, :, :], DT[:, :, :], ACT.Exp).then_inc(S("dn_dt"), 1)
                for j, (dst, src) in enumerate(((KTt, A8), (KBT, B8), (QT, A8), (QT, B8))):
                    act.wait_ge(S("dn_t"), 4 * hf + j + 1)
                    if j == 3:
                        act.wait_ge(S("dn_at_mm"), hf + 1)
                    nc.scalar.copy(dst[:, :, :], src).then_inc(S("dn_tc"), 1)
                with loop(act, 5) as lv:
                    for e in range(2):
                        act.wait_ge(S(f"lv_y{e}"), lv + (5 * hf + 1))
                        nc.scalar.copy(YY[:, 4 * e:4 * e + 4, :], A8[:, 4 * e:4 * e + 4, :]).then_inc(S(f"lv_yc{e}"), 1)
                act.wait_ge(S("dn_uw"), hf + 1)
                nc.scalar.copy(TT[:, :, :], A8)
                nc.scalar.copy(KBT[:, :, :], B8).then_inc(S("dn_uwc"), 1)
                if hf == 0:
                    act.wait_ge(S("dn_ms"), 2)
                    nc.scalar.activation(r16, m16, ACT.Sqrt).then_inc(S("dn_rt"), 1)
                z3 = p1[:, hf, POOL_W + 3072:POOL_W + 4096].rearrange("p (a b) -> p a b", b=P)
                nc.scalar.activation(LT[:, :, :], z3, ACT.Sigmoid).then_inc(S("dn_zs"), 1)
                act.wait_ge(S("sc_s"), 2 * hf + 2)
                nc.scalar.copy(MT[:, :, :], B8).then_inc(S("dn_oc"), 1)
                act.wait_ge(S("dn_oms"), hf + 1)
                nc.scalar.activation(r16[:, 0:8], m16[:, 0:8], ACT.Sqrt).then_inc(S("dn_ort"), 1)
                act.wait_ge(S("dn_yt"), hf + 1)
                nc.scalar.copy(hhi[:, 8:16, hf * P:hf * P + P], A8).then_inc(S("dn_hi"), 1)

            phase(PH["mix_out"], {})
            act.wait_ge(S("mem_in"), 16)
            norm("mem", memt, [[(S("mem_in"), 16)], []])
            phase(PH["xkv"], store(PH["xkv"], kv))
            turn_in_act(act, "kx", kTx)
            norm("xa", x, evacuated("mix_out"))
            phase(PH["xq"], store(PH["xq"], kv))
            turn_in_act(act, "qx", qTx)
            attention_act(act, "xatt", cross_units())
            phase(PH["xo"], {})
            norm("ffn", x, evacuated("xo"))

            def ffn1(q, fb0):
                def evac(e):
                    def f(it):
                        act.wait_ge(S("mm_done"), block_end(q, it, e) + NRING)
                        nc.scalar.copy(tok[e][:, :, :], GP[:, 2 * e:2 * e + 2, :]).then_inc(S(f"evac{e}"), 1)
                    return f

                def gate(it):
                    act.wait_ge(S("f1_tg"), it + fb0 + 1)
                    act.wait_ge(S("f1_lo"), it + fb0 + 1)
                    for f in range(4):
                        c = 16 * (it + fb0) + 4 * f
                        m = nc.scalar.activation(ft[:, f, :], v(TA, T)[:, f, :], ACT.Identity,
                                                 scale=ffn_w[:, bass.ds(c + 2, 1)], bias=ffn_w[:, bass.ds(c + 3, 1)])
                    m.then_inc(S("f1_a"), 1)
                    act.wait_ge(S("f1_conv"), it + fb0 + 2)
                    nc.scalar.activation(fsg[:, :, :], ft[:, :, :], ACT.Sigmoid).then_inc(S("f1_s"), 1)

                def up(it):
                    act.wait_ge(S("f1_f"), it + fb0 + 2)
                    nc.scalar.copy(fhi[:, bass.ds(4 * it, 4), :], ft[:, :, :]).then_inc(S("f1_hi"), 1)
                return {q.units + LEAD: [evac(0)], 2 * q.units: [gate], 2 * q.units + LEAD: [evac(1), up]}

            phase(PH["ffn1a"], ffn1(PH["ffn1a"], 0))
            phase(PH["down1a"], {})
            phase(PH["ffn1b"], ffn1(PH["ffn1b"], 6))
            phase(PH["down1b"], {})

            root_mean("fin", x, evacuated("down1b"), lambda h: xn_f[:, h, :])
            norm("pre2", x, [[(S("fin_x"), h + 1)] for h in range(NH)])
            phase(PH["w_in2a"], store(PH["w_in2a"], p2, lastcol=NSA_W - W2A))
            phase(PH["w_in2b"], store(PH["w_in2b"], p2, base=NSA_W))

            def nsa_gates():
                for e in range(2):
                    act.wait_ge(S(f"evac{e}"), 1 + PH["w_in2a"].ev1)
                nc.scalar.activation(gates.rearrange("p (a b) -> p a b", b=24), p2[:, :, NSA_W - 24:NSA_W], ACT.Sigmoid)\
                    .then_inc(S("gates"), 1)

            def cmp_copy(j):
                act.wait_ge(S("cmp_t"), j + 1)
                if j:
                    act.wait_ge(S("cmp_r"), 1)
                nc.scalar.copy(kTc, v(TA, T)[:, 0:2, :]).then_inc(S("cmp_kt"), 1)

            def cmp_sigmoid(j):
                act.wait_ge(S("cmp_hb"), j + 1)
                nc.scalar.activation(hid[:, 31:61], hid[:, 0:30], ACT.Sigmoid).then_inc(S("cmp_sg"), 1)

            def cmp_out(j):
                act.wait_ge(S("cmp_o"), j + 1)
                if j == 0:
                    nc.scalar.copy(kcT, TB[:, 0:30].rearrange("p (a b) -> p a b", b=15)).then_inc(S("cmp_oc"), 1)
                else:
                    nc.scalar.copy(vc, TB[0:CMP_N, 0:256].rearrange("p (a b) -> p a b", b=P)).then_inc(S("cmp_oc"), 1)
            hooks = {3: [lambda it: (nsa_gates(), cmp_copy(0))], 4: [lambda it: cmp_sigmoid(0)],
                     5: [lambda it: (cmp_out(0), cmp_copy(1))], 8: [lambda it: cmp_sigmoid(1)], 9: [lambda it: cmp_out(1)]}
            for at, what in store(PH["w_in2c"], p2, base=NSA_W + 2048).items():
                hooks[at] = what + hooks.get(at, [])
            phase(PH["w_in2c"], hooks)
            turn_in2_act(act, "n2")
            attention_act(act, "natt", nsa_units())
            turn_in2_act(act, "m2")
            attention_act(act, "matt", moba_units())
            def gate_copy(n, i):
                act.wait_ge(S("gate_mm"), 4 * n + i + 1)
                nc.scalar.copy(gpb[n][:, 512 * i:512 * i + 512], TA[:, 512 * (i % 2):512 * (i % 2) + 512]).then_inc(S("gpb"), 1)

            phase(PH["w_oa"], store(PH["w_oa"], o2))
            hooks = {3 + i: [lambda it, i=i: gate_copy(0, i)] for i in range(4)}
            for at, what in store(PH["w_ob"], o2, base=1024).items():
                hooks[at] = what + hooks.get(at, [])
            phase(PH["w_ob"], hooks)

            def post(n, o, first):
                for w in first:
                    act.wait_ge(*w)
                root_mean(f"post{n}", o, [[], []], lambda h: junk[:, :])

            post(0, o2, evacuated("w_ob")[0])
            norm("pf2", x, [[(S("y_mix"), h + 1)] for h in range(NH)])

            def up2(q, s):
                def evac(e):
                    def f(it):
                        act.wait_ge(S("mm_done"), block_end(q, it, e) + NRING)
                        nc.scalar.activation(tok2[e][:, :, :], GP[:, 2 * e:2 * e + 2, :], ACT.Relu).then_inc(S(f"evac{e}"), 1)
                    return f

                def square(e):
                    def f(it):
                        act.wait_ge(S(f"f2_t{e}"), it + 2 * s + 1)
                        act.wait_ge(S("f2_lo"), 2 * it + 4 * s + e + 1)
                        nc.scalar.activation(fq2[e][:, :, :], v((TA, TB)[e], T), ACT.Square).then_inc(S(f"f2_q{e}"), 1)
                        act.wait_ge(S(f"f2_q{e}"), it + 2 * s + 2)
                        nc.scalar.copy(f2hi[:, bass.ds(8 * it + 4 * e, 4), :], fq2[e][:, :, :]).then_inc(S("f2_hi"), 1)
                    return f
                return {q.units + LEAD: [evac(0)], 2 * q.units: [square(0)], 2 * q.units + LEAD: [evac(1), square(1)]}
            for s in range(4):
                phase(PH[f"up2{s}"], up2(PH[f"up2{s}"], s))
                phase(PH[f"down2{s}"], {}, peel=(s == 3),
                      last={3 + i: [lambda it, i=i: gate_copy(1, i)] for i in range(4)} if s == 3 else {})
            post(1, o3, evacuated("down23")[0])

        @block.vector
        def _(dve):
            link = Chain(dve, S("dve_step"))
            TTo = nc.vector.tensor_tensor

            def split_lo(q, it, j):
                kind, b, u = q.seq[j]
                if kind == "a":
                    dve.wait_ge(S(f"raw_in{j % NSLOT}"), 16 * (it * (len(q.seq) // NSLOT) + q.unit0 // NSLOT + j // NSLOT + 1))
                    for k in range(4):
                        kt = 4 * u + k
                        c = csig[:, kt:kt + 1]
                        if kt == 0:
                            dve.wait_ge(S("ada_sum"), it + q.ada0 + 1)
                            m = nc.vector.tensor_scalar(ada_acc[:, :], raw[j % NSLOT][:, k, :], c, None, ALU.mult)
                        else:
                            m = nc.vector.scalar_tensor_tensor(ada_acc[:, :], raw[j % NSLOT][:, k, :], c, ada_acc[:, :],
                                                               ALU.mult, ALU.add)
                        if k >= 2:
                            m.then_inc(S("unit_used"), 1)
                            dve.wait_ge(S("unit_used"), it * (2 * len(q.seq)) + 2 * (q.unit0 + j) + (k - 1) + CREDIT)
                        else:
                            link(m)
                    return
                g = b * q.units + u
                for s in range(2):
                    r = (2 * g + s) % NRING
                    dve.wait_ge(S("hi_done"), it * q.subs + (q.sub0 + 2 * g + s + 1))
                    TTo(wlo[r][:, :, 0:q.width], raw[j % NSLOT][:, 2 * s:2 * s + 2, 0:q.width],
                        whi[r][:, :, 0:q.width].bitcast(F32), ALU.subtract).then_inc(S("unit_used"), 1)

            def body(q, it, nxt, hooks):
                g = 0
                for j, (kind, b, u) in enumerate(q.seq):
                    if j < LEAD:
                        g += 1
                        continue
                    split_lo(q, it, j)
                    if kind == "g":
                        g += 1
                        for f in hooks.get(g, ()):
                            f(it)
                for j in range(LEAD):
                    if nxt is not None:
                        split_lo(*nxt, j)
                    for f in hooks.get(g + j + 1, ()):
                        f(it)
                if q.ada:
                    dve.wait_ge(S("ada_sum"), it + q.ada0 + 2)
                    nc.vector.tensor_copy(mod[:, bass.ds(4 * (it + q.ada0), 4)], TB[:, 512:516]).then_inc(S("ada_read"), 1)

            def phase(q, hooks, peel=False, links=0, last={}):
                i0 = order.index(q)
                nq = order[i0 + 1] if i0 + 1 < len(order) else None
                same = nq is not None and nq.width == q.width and not peel
                per = links + (8 if q.ada else 0)
                m = q.n if same else q.n - 1
                if m:
                    with loop(dve, m) as it:
                        with link.loop(it, m, per):
                            body(q, it, (q, it + 1), hooks)
                if not same:
                    both = {at: hooks.get(at, []) + last.get(at, []) for at in hooks.keys() | last.keys()}
                    body(q, q.n - 1, (nq, 0) if nq is not None else None, both)

            def add_to_x(q):
                def hook(b):
                    def f(it):
                        e = b % 2
                        dve.wait_ge(S("mm_done"), block_end(q, it, b) + NRING)
                        c = bass.ds((q.nb * it + b) * 512, 512)
                        TTo(x[:, :, c], GP[:, 2 * e:2 * e + 2, :], x[:, :, c], ALU.add).then_inc(S(f"evac{e}"), 1)
                    return f
                return {(b + 1) * q.units + LEAD: [hook(b)] for b in range(q.nb)}

            def rsqrt_mean(nm_, h):
                r = slice(h, h + 1)
                dve.wait_ge(*N(nm_, "ss", h + 1))
                nc.vector.tensor_scalar(ms[:, r], ss[:, r], 1.0 / D, EPS, ALU.mult, ALU.add).then_inc(N(nm_, "ms")[0], 1)
                dve.wait_ge(*N(nm_, "rt", h + 1))
                link(nc.vector.reciprocal(rstd[:, r], rt[:, r]))

            def norm(nm_, X, gain, shift=None, between=None):
                for h in range(NH):
                    rsqrt_mean(nm_, h)
                    nc.vector.tensor_scalar(xn_of[nm_][:, h, :], X[:, h, :], rstd[:, h:h + 1], None, ALU.mult)\
                        .then_inc(N(nm_, "xn")[0], 1)
                if between:
                    between()

                def low(g):
                    q, h = divmod(g, NH)
                    a, t = slice(4 * q, 4 * q + 4), slice(h * P, h * P + P)
                    dve.wait_ge(*N(nm_, "hi", g + 1))
                    TTo(hlo[:, a, t], fbx[g % 2].rearrange("p (a b) -> p a b", b=P), hhi[:, a, t].bitcast(F32),
                        ALU.subtract).then_inc(N(nm_, "lo")[0], 1)
                for g in range(8):
                    q, h = divmod(g, NH)
                    dve.wait_ge(*N(nm_, "t", g + 1))
                    bank = norm_banks[g % 5].rearrange("p (a b) -> p a b", b=P)
                    f3 = fbx[g % 2].rearrange("p (a b) -> p a b", b=P)
                    if g >= 2:
                        dve.wait_ge(*N(nm_, "lo", g - 1))
                    m = TTo(f3, bank, cols(gain[:, 4 * q:4 * q + 4], P), ALU.mult)
                    if shift is not None:
                        link(m)
                        m = TTo(f3, f3, cols(shift[:, 4 * q:4 * q + 4], P), ALU.add)
                    m.then_inc(N(nm_, "f")[0], 1)
                    if g:
                        low(g - 1)
                low(7)

            for name, n in (("unit_used", CREDIT), ("mm_done", NRING), ("evac0", 1), ("evac1", 1), ("ada_sum", 1),
                            ("ada_read", 1), ("f1_lo", 1), ("f2_lo", 2), ("f1_conv", 1), ("f1_f", 1), ("f2_q0", 1), ("f2_q1", 1)):
                dve.sem_inc(S(name), n)
            norm("mix", x, gains[:, 0, :], between=lambda: (dve.wait_ge(S("cst_in"), 16), dve.wait_ge(S("gain_in"), 16),
                                                            [split_lo(order[0], 0, j) for j in range(LEAD)]))
            dve.wait_ge(S("tab_in"), 16 * TABS)
            dve.wait_ge(S("csig"), 1)
            link(TTo(csig[:, :], csig[:, :], cvec[:, :], ALU.mult))
            phase(PH["w_in"], {})

            dve.wait_ge(S("gp_b"), 1)
            al = p1[:, :, IN_W - 8:IN_W]
            link(TTo(za.rearrange("p (a b) -> p a b", b=8), al, rows(dtb, 2), ALU.add))
            nc.vector.scalar_tensor_tensor(zb, za, -1.0, za, ALU.mult, ALU.max).then_inc(S("gp_ax"), 1)
            dve.wait_ge(S("gp_e"), 1)
            link(nc.vector.tensor_scalar(zd, zc, 2.0, None, ALU.add))
            link(nc.vector.reciprocal(ze, zd))
            link(TTo(zc, zc, ze, ALU.mult))
            link(TTo(zd, zc, zc, ALU.mult))
            link(nc.vector.tensor_scalar(ze, zd, 1.0 / 19, None, ALU.mult))
            for c in (17, 15, 13, 11, 9, 7, 5, 3):
                link(nc.vector.scalar_tensor_tensor(ze, ze, 1.0 / c, zd, ALU.add, ALU.mult))
            link(nc.vector.scalar_tensor_tensor(ze, ze, 1.0, zc, ALU.add, ALU.mult))
            link(nc.vector.tensor_scalar(za, za, 0.0, None, ALU.max))
            link(nc.vector.scalar_tensor_tensor(ze, ze, 2.0, za, ALU.mult, ALU.add))
            nc.vector.scalar_tensor_tensor(gdec.rearrange("p (a b) -> p a b", b=8), ze.rearrange("p (a b) -> p a b", b=8), -1.0,
                                           rows(ea, 2), ALU.mult, ALU.mult).then_inc(S("gp_g"), 1)
            dve.wait_ge(S("gp_g"), 1)

            for i in range(4):
                dve.wait_ge(S("pool_y"), i + 1)
                if i:
                    dve.wait_ge(S("pool_lo"), i)
                TTo(fpool[:, :, :], v(TB, T)[:, 0:2, :], cols(pool_s[:, 2 * i:2 * i + 2], T), ALU.mult).then_inc(S("pool_f"), 1)
                dve.wait_ge(S("pool_hi"), i + 1)
                TTo(hlo[:, 2 * i:2 * i + 2, :], fpool[:, :, :], hhi[:, 2 * i:2 * i + 2, :].bitcast(F32),
                    ALU.subtract).then_inc(S("pool_lo"), 1)

            for g in range(6):
                dve.wait_ge(S("cv_a"), g + 1)
                cb = cbuf[g % 3]
                for s in range(1, 4):
                    for f in range(4):
                        m = nc.vector.scalar_tensor_tensor(cb[:, f, s:T], v(GP_flat(g % 2), T)[:, f, 0:T - s], conv_w[:, 4 * g + f, 3 - s:4 - s],
                                                           cb[:, f, s:T], ALU.mult, ALU.add)
                    if s < 3:
                        link(m)
                m.then_inc(S("cv_c"), 1)

            A8, B8 = v(TA, P), v(TB, P)

            def unit_length(hf):
                q3 = p1[:, hf, POOL_W:POOL_W + 1024].rearrange("p (a b) -> p a b", b=P)
                k3 = p1[:, hf, POOL_W + 1024:POOL_W + 2048].rearrange("p (a b) -> p a b", b=P)
                for i, t3 in enumerate((q3, k3)):
                    link(TTo(SQ, t3, t3, ALU.mult))
                    link(nc.vector.tensor_reduce(s16[:, 8 * i:8 * i + 8], SQ, AX.X, ALU.add))
                nc.vector.tensor_scalar(m16, s16, EPS, None, ALU.add).then_inc(S("dn_ms"), 1)
                dve.wait_ge(S("dn_rt"), hf + 1)
                link(nc.vector.reciprocal(i16, r16))
                link(nc.vector.tensor_scalar(i16[:, 0:8], i16[:, 0:8], P ** -0.5, None, ALU.mult))
                link(TTo(k3, k3, cols(i16[:, 8:16], P), ALU.mult))
                link(TTo(q3, q3, cols(i16[:, 0:8], P), ALU.mult))

            for hf in range(NH):
                q3 = p1[:, hf, POOL_W:POOL_W + 1024].rearrange("p (a b) -> p a b", b=P)
                k3 = p1[:, hf, POOL_W + 1024:POOL_W + 2048].rearrange("p (a b) -> p a b", b=P)
                v3 = p1[:, hf, POOL_W + 2048:POOL_W + 3072].rearrange("p (a b) -> p a b", b=P)
                z3 = p1[:, hf, POOL_W + 3072:POOL_W + 4096].rearrange("p (a b) -> p a b", b=P)
                gd = gdec[:, hf * 8:hf * 8 + 8]
                bt = beta[:, hf * 8:hf * 8 + 8]
                if hf == 0:
                    nc.vector.memset(ST, 0.0).then_inc(S("sc_u"), 1)
                    dve.wait_ge(S("cv_e"), 6)
                TTo(KB[:, :, :], rows(C("upto"), 8), cols(gd, P), ALU.mult).then_inc(S("dn_tg"), 1)
                if hf == 0:
                    unit_length(0)
                dve.wait_ge(S("dn_diff"), hf + 1)
                TTo(DT[:, :, :], B8, rows(C("chunk_mask"), 8), ALU.add).then_inc(S("dn_dm"), 1)
                TTo(KB[:, :, :], k3, cols(bt, P), ALU.mult).then_inc(S("dn_kb"), 1)
                dve.wait_ge(S("dn_dt"), hf + 1)
                dve.wait_ge(S("dn_lt_mm"), hf + 1)
                link(TTo(LT[:, :, :], B8, DT[:, :, :], ALU.mult))
                TTo(LT[:, :, :], LT[:, :, :], rows(C("strict"), 8), ALU.mult).then_inc(S("dn_lt"), 1)
                dve.wait_ge(S("dn_ex"), hf + 1)
                dve.wait_ge(S("dn_t"), 4 * hf + 3)
                TTo(q3, q3, cols(ex[:, 0:8], P), ALU.mult).then_inc(S("dn_qd"), 1)
                dve.wait_ge(S("dn_at_mm"), hf + 1)
                TTo(DT[:, :, :], A8, DT[:, :, :], ALU.mult).then_inc(S("dn_at"), 1)
                for e in range(2):
                    a = slice(4 * e, 4 * e + 4)
                    dve.wait_ge(S(f"lv_z{e}"), 6 * hf + 1)
                    TTo(TT[:, a, :], rows(ident, 4), B8[:, a, :], ALU.subtract)
                    TTo(AA[:, a, :], rows(ident, 4), MT[:, a, :], ALU.subtract).then_inc(S(f"lv_u{e}"), 1)

                def level(lv, both):
                    for e in range(2):
                        a = slice(4 * e, 4 * e + 4)
                        dve.wait_ge(S(f"lv_z{e}"), lv + (6 * hf + 2))
                        if both:
                            TTo(TT[:, a, :], TT[:, a, :], B8[:, a, :], ALU.subtract)
                        TTo(AA[:, a, :], AA[:, a, :], A8[:, a, :], ALU.subtract).then_inc(S(f"lv_u{e}"), 1)

                with loop(dve, 4) as lv:
                    level(lv, True)
                level(4, False)
                dve.wait_ge(S("lv_u1"), 6 * hf + 6)
                if hf == 0:
                    unit_length(1)
                for c in range(2):
                    r = slice(64 * c, 64 * c + 64)
                    n = 2 * hf + c
                    dve.wait_ge(S("sc_w"), n + 1)
                    TTo(YY[r, :, :], TT[r, :, :], A8[r, :, :], ALU.subtract).then_inc(S("sc_v"), 1)
                    if n == 3:
                        continue
                    dve.wait_ge(S("sc_s"), n + 1)
                    link(TTo(ST, ST, cols(ex[:, 16 + 8 * c:24 + 8 * c], P), ALU.mult))
                    TTo(ST, ST, A8, ALU.add).then_inc(S("sc_u"), 1)
                dve.wait_ge(S("dn_oc"), hf + 1)
                link(TTo(SQ, MT[:, :, :], MT[:, :, :], ALU.mult))
                link(nc.vector.tensor_reduce(s16[:, 0:8], SQ, AX.X, ALU.add))
                nc.vector.tensor_scalar(m16[:, 0:8], s16[:, 0:8], 1.0 / P, EPS, ALU.mult, ALU.add).then_inc(S("dn_oms"), 1)
                dve.wait_ge(S("dn_ort"), hf + 1)
                link(nc.vector.reciprocal(i16[:, 0:8], r16[:, 0:8]))
                link(TTo(MT[:, :, :], MT[:, :, :], cols(i16[:, 0:8], P), ALU.mult))
                dve.wait_ge(S("dn_z"), hf + 1)
                TTo(MT[:, :, :], MT[:, :, :], z3, ALU.mult).then_inc(S("dn_y"), 1)
                dve.wait_ge(S("dn_hi"), hf + 1)
                t = slice(hf * P, hf * P + P)
                TTo(hlo[:, 8:16, t], A8, hhi[:, 8:16, t].bitcast(F32), ALU.subtract).then_inc(S("dn_lo"), 1)

            phase(PH["mix_out"], add_to_x(PH["mix_out"]))
            dve.wait_ge(S("mem_in"), 16)
            norm("mem", memt, gains[:, 2, :])
            phase(PH["xkv"], {})
            norm("xa", x, gains[:, 1, :])
            phase(PH["xq"], {})
            dve.wait_ge(*N("qx", "c", 4))
            dve.sem_inc(N("xatt", "go")[0], 1)
            attention_dve(dve, link, "xatt", cross_units())
            phase(PH["xo"], add_to_x(PH["xo"]))
            norm("ffn", x, gains[:, 3, :])

            def ffn1(q, fb0):
                def gate(it):
                    dve.wait_ge(S("f1_a"), it + fb0 + 1)
                    for s in (1, 2):
                        for f in range(4):
                            m = nc.vector.scalar_tensor_tensor(ft[:, f, s:T], v(TA, T)[:, f, 0:T - s],
                                                               ffn_w[:, bass.ds(16 * (it + fb0) + 4 * f + 2 - s, 1)],
                                                               ft[:, f, s:T], ALU.mult, ALU.add)
                        if s == 1:
                            link(m)
                    m.then_inc(S("f1_conv"), 1)
                    dve.wait_ge(S("f1_s"), it + fb0 + 1)
                    link(TTo(ft[:, :, :], ft[:, :, :], fsg[:, :, :], ALU.mult))

                def up(it):
                    dve.wait_ge(S("f1_tu"), it + fb0 + 1)
                    TTo(ft[:, :, :], v(TB, T), ft[:, :, :], ALU.mult).then_inc(S("f1_f"), 1)
                    dve.wait_ge(S("f1_hi"), it + fb0 + 1)
                    TTo(flo[:, bass.ds(4 * it, 4), :], ft[:, :, :], fhi[:, bass.ds(4 * it, 4), :].bitcast(F32),
                        ALU.subtract).then_inc(S("f1_lo"), 1)
                return {2 * q.units: [gate], 2 * q.units + LEAD: [up]}

            phase(PH["ffn1a"], ffn1(PH["ffn1a"], 0), links=2)
            phase(PH["down1a"], add_to_x(PH["down1a"]))
            phase(PH["ffn1b"], ffn1(PH["ffn1b"], 6), links=2)
            phase(PH["down1b"], add_to_x(PH["down1b"]))

            dve.wait_ge(S("fgb_in"), 16)
            for h in range(NH):
                rsqrt_mean("fin", h)
                nc.vector.scalar_tensor_tensor(x[:, h, :], x[:, h, :], rstd[:, h:h + 1], fgb[:, :], ALU.mult, ALU.mult)\
                    .then_inc(S("fin_x"), 1)
            def modulation(j, c0, gi):
                link(TTo(shifts[:, j, :], mod[:, c0:c0 + 16], b_ada[:, c0:c0 + 16], ALU.add))
                link(TTo(mod[:, c0 + 16:c0 + 32], mod[:, c0 + 16:c0 + 32], b_ada[:, c0 + 16:c0 + 32], ALU.add))
                link(nc.vector.scalar_tensor_tensor(gains[:, gi, :], mod[:, c0 + 16:c0 + 32], 1.0, gains[:, gi, :], ALU.add, ALU.mult))
            modulation(0, 0, 4)
            norm("pre2", x, gains[:, 4, :], shifts[:, 0, :])
            phase(PH["w_in2a"], {})
            phase(PH["w_in2b"], {})

            def cmp_blocks(j):
                dve.wait_ge(S("cmp_kt"), j + 1)
                dve.wait_ge(S("cmp_in"), 64)
                if j:
                    dve.wait_ge(S("cmp_hid"), 1)
                for g in range(2):
                    for half in range(2):
                        src = kTc[:, g, 16 * half:16 * half + 240].rearrange("p (c l) -> p l c", l=16)
                        nc.vector.tensor_copy(rc1[:, 16 * half:16 * half + 16, 15 * g:15 * g + 15], src)
                nc.vector.tensor_copy(rc1[:, :, 30], posT[:, j, :]).then_inc(S("cmp_r"), 1)

            def cmp_silu(j):
                dve.wait_ge(S("cmp_hid"), j + 1)
                if j:
                    dve.wait_ge(S("cmp_o"), 1)
                link(nc.vector.tensor_copy(hid[:, 30:31], TA[:, 542:543]))
                nc.vector.tensor_scalar(hid[:, 0:30], TA[:, 512:542], hid[:, 30:31], None, ALU.add).then_inc(S("cmp_hb"), 1)
                dve.wait_ge(S("cmp_sg"), j + 1)
                TTo(hid[:, 0:30], hid[:, 0:30], hid[:, 31:61], ALU.mult).then_inc(S("cmp_s"), 1)
            phase(PH["w_in2c"], {3: [lambda it: cmp_blocks(0)], 4: [lambda it: cmp_silu(0)], 5: [lambda it: cmp_blocks(1)],
                                 8: [lambda it: cmp_silu(1)]}, links=2)
            dve.wait_ge(S("gates"), 1)
            dve.wait_ge(S("cmp_oc"), 2)
            dve.wait_ge(*N("n2", "c", 3))
            dve.sem_inc(N("natt", "go")[0], 1)
            attention_dve(dve, link, "natt", nsa_units())
            dve.wait_ge(*N("m2", "c", 4))
            dve.sem_inc(N("matt", "go")[0], 1)
            attention_dve(dve, link, "matt", moba_units())
            def gate_column(n, c0, i):
                if i == 0:
                    c = mod[:, c0:c0 + 16]
                    link(TTo(c, c, b_ada[:, c0:c0 + 16], ALU.add))
                    link(TTo(c, c, post_gain[:, n, :], ALU.mult))
                else:
                    dve.wait_ge(S("gate_mm"), 4 * n + i)
                if i >= 2:
                    dve.wait_ge(S("gpb"), 4 * n + i - 1)
                TTo(dg[n][:, :, :], rows(ident, 4), cols(mod[:, c0 + 4 * i:c0 + 4 * i + 4], P), ALU.mult).then_inc(S("dg_done"), 1)

            phase(PH["w_oa"], {})
            phase(PH["w_ob"], {3 + i: [lambda it, i=i: gate_column(0, 32, i)] for i in range(4)}, links=2)

            def post(n, o, done):
                for h in range(NH):
                    rsqrt_mean(f"post{n}", h)
                    if h == 0:
                        dve.wait_ge(S("gpb"), 4 * n + 4)
                    link(nc.vector.scalar_tensor_tensor(o[:, h, :], o[:, h, :], rstd[:, h:h + 1], gpb[n][:, :], ALU.mult, ALU.mult))
                    TTo(x[:, h, :], x[:, h, :], o[:, h, :], ALU.add).then_inc(S(done), 1)

            post(0, o2, "y_mix")
            modulation(1, 48, 5)
            norm("pf2", x, gains[:, 5, :], shifts[:, 1, :])

            def up2(q, s):
                def low(e):
                    def f(it):
                        dve.wait_ge(S("f2_hi"), 2 * it + 4 * s + e + 1)
                        c = bass.ds(8 * it + 4 * e, 4)
                        TTo(f2lo[:, c, :], fq2[e][:, :, :], f2hi[:, c, :].bitcast(F32), ALU.subtract).then_inc(S("f2_lo"), 1)
                    return f
                return {2 * q.units: [low(0)], 2 * q.units + LEAD: [low(1)]}

            def down2(q, s):
                def hook(b):
                    def f(it):
                        dve.wait_ge(S("mm_done"), block_end(q, it, b) + NRING)
                        c = bass.ds((2 * it + b) * 512, 512)
                        if s == 0:
                            m = nc.vector.tensor_copy(o3[:, :, c], GP[:, 2 * b:2 * b + 2, :])
                        else:
                            m = TTo(o3[:, :, c], GP[:, 2 * b:2 * b + 2, :], o3[:, :, c], ALU.add)
                        m.then_inc(S(f"evac{b}"), 1)
                    return f
                return {(b + 1) * q.units + LEAD: [hook(b)] for b in range(2)}
            for s in range(4):
                phase(PH[f"up2{s}"], up2(PH[f"up2{s}"], s))
                phase(PH[f"down2{s}"], down2(PH[f"down2{s}"], s), peel=(s == 3),
                      last={3 + i: [lambda it, i=i: gate_column(1, 80, i)] for i in range(4)} if s == 3 else {})
            post(1, o3, "y_done")


_INS = {
    "x": None, "mem": None, "w_in": "m", "w_mix_out": "m", "w_xq": "m", "w_xkv": "m", "w_xo": "m",
    "w_gate": "m", "w_up": "m", "w_down": "m", "w_ada_2": "m", "w_in_2": "m", "w_o_2": "m", "w_up_2": "m", "w_down_2": "m",
    "mix_norm_g": "c", "xa_norm_g": "c", "mem_norm_g": "c", "ffn_norm_g": "c", "pre_norm_mix_2": "c", "pre_norm_ffn_2": "c",
    "pool_scale": "c", "b_ada_2": "c", "c_2": "c", "dn_dt_bias": "v", "dn_a_log": "v", "dn_norm_g": "v",
    "final_norm_g": "v", "post_norm_mix_2": "c", "post_norm_ffn_2": "c",
}


def kernel(**inputs):
    import concourse.bacc as bacc
    from concourse.bass_utils import run_bass_kernel_spmd as run

    nc = bacc.Bacc("TRN2", target_bir_lowering=False, num_devices=1)
    arrays, A = {}, {}

    def give(name, a):
        a = np.ascontiguousarray(a)
        arrays["in_" + name] = a
        A[name] = nc.dram_tensor("in_" + name, a.shape, F32, kind="ExternalInput").ap()

    for name, how in _INS.items():
        a = np.asarray(inputs[name])
        if how == "m":
            a = a.reshape(a.shape[-2], a.shape[-1])
        elif how == "c":
            a = a.reshape(-1, P).T
        elif how == "v":
            a = a.reshape(-1)
        give(name, a)
    give("dn_conv_w", np.asarray(inputs["dn_conv_w"]).reshape(4, 24, P).transpose(2, 1, 0))
    give("ffn_conv_w", np.asarray(inputs["ffn_conv_w"]).reshape(3, FF1 // P, P, 1).transpose(2, 0, 1, 3))
    give("ffn_conv_b", np.asarray(inputs["ffn_conv_b"]).reshape(FF1 // P, P, 1).transpose(1, 0, 2))
    give("w_pool", np.asarray(inputs["w_pool"]).reshape(4, 2, P, 256).transpose(2, 0, 1, 3))
    for n in ("cmp_k_", "cmp_v_"):
        give(n + "pos_2", np.asarray(inputs[n + "pos_2"]).reshape(32, P).T)
        give(n + "w1_2", np.asarray(inputs[n + "w1_2"]).reshape(32, P, P).transpose(1, 0, 2))
        give(n + "w2_2", np.asarray(inputs[n + "w2_2"]).reshape(P, P))
    give("const", CONST)
    give("pool_mats", pooling_table())
    out = nc.dram_tensor("out_0", (1, T, D), F32, kind="ExternalOutput").ap()
    program(nc, A, out)
    return run(nc, [arrays], core_ids=[0]).results[0]["out_0"]
```
